# Optimizing a Trainium2 kernel written in Bass

```python
import jax
import jax.numpy as jnp
from jax import lax
import numpy as np

D_MODEL = 1024
BATCH = 1
SEQ = 256
DEPTH = 1
DEC_BATCH = 8
DEC_SEQ = 4
PAST_LEN = 1024
PAGE_SIZE = 128

CONV_CH = D_MODEL // 2
CONV_K = 3
N_HEADS = 8
N_KV_HEADS = 2
GROUP = N_HEADS // N_KV_HEADS
HEAD_DIM = 64
CMP_STRIDE = 16
CMP_LEN = 2 * CMP_STRIDE
CMP_HIDDEN = 2 * HEAD_DIM
SEL_BLOCK = 64
SEL_TOPN = 16
WINDOW = 512
BAND_BLOCK = 128
Q_BLOCK = 128
ROPE_THETA = 10000.0
PEER_HEADS = 8
PEER_NKEYS = 128
PEER_EXPERTS = PEER_NKEYS * PEER_NKEYS
PEER_QDIM = 256
PEER_HALF = PEER_QDIM // 2
PEER_TOPK = 16
PEER_BLOCK = 128

RMS_EPS = 1e-6
NEG = -1e30
FORCE_BONUS = 1e4
Q_W = N_HEADS * HEAD_DIM
KV_W = N_KV_HEADS * HEAD_DIM
IN_SIZES = (CONV_CH, CONV_CH, CONV_CH, Q_W, KV_W, KV_W, KV_W, KV_W, KV_W, KV_W, 3 * N_HEADS, 2 * D_MODEL)
IN_WIDTH = sum(IN_SIZES)

kernel_name = 'hybrid_shortconv_nsa_peer_step'

def rmsnorm(x, g):
    xf = x.astype(jnp.float32)
    r = lax.rsqrt(jnp.mean(xf * xf, axis=-1, keepdims=True) + RMS_EPS)
    return (xf * r * g.astype(jnp.float32)).astype(x.dtype)

def rope(x, pos):
    half = HEAD_DIM // 2
    inv = jnp.power(ROPE_THETA, -jnp.arange(half, dtype=jnp.float32) * 2.0 / HEAD_DIM)
    ang = pos.astype(jnp.float32)[:, None] * inv[None, :]
    shape = (1, pos.shape[0]) + (1,) * (x.ndim - 3) + (half,)
    cos = jnp.cos(ang).reshape(shape)
    sin = jnp.sin(ang).reshape(shape)
    xf = x.astype(jnp.float32)
    x1, x2 = xf[..., :half], xf[..., half:]
    return jnp.concatenate([x1 * cos - x2 * sin, x2 * cos + x1 * sin], axis=-1).astype(x.dtype)

def attend(q, k, v, mask):
    s = jnp.einsum('...qgrd,...kgd->...qgrk', q, k).astype(jnp.float32) * (HEAD_DIM ** -0.5)
    p = jax.nn.softmax(jnp.where(mask, s, NEG), axis=-1)
    return jnp.einsum('...qgrk,...kgd->...qgrd', p.astype(v.dtype), v)

def gather_pages(pool, page_table):
    g = pool[page_table]
    return g.reshape((g.shape[0], g.shape[1] * g.shape[2]) + pool.shape[2:])

def compress(raw, pos_emb, w1, b1, w2):
    b, L = raw.shape[:2]
    n_ch = L // CMP_STRIDE
    ch = raw[:, :n_ch * CMP_STRIDE].reshape(b, n_ch, CMP_STRIDE, N_KV_HEADS, HEAD_DIM)
    first = jnp.einsum('bcsgd,sdf->bcgf', ch, w1[:CMP_STRIDE])
    second = jnp.einsum('bcsgd,sdf->bcgf', ch, w1[CMP_STRIDE:])
    bias = jnp.einsum('sd,sdf->f', pos_emb, w1) + b1
    hid = jax.nn.gelu(first[:, :-1] + second[:, 1:] + bias, approximate=False)
    return jnp.einsum('bngf,fd->bngd', hid, w2)

def to_blocks(k):
    b, L = k.shape[:2]
    n_sel = -(-L // SEL_BLOCK)
    k = jnp.pad(k, ((0, 0), (0, n_sel * SEL_BLOCK - L), (0, 0), (0, 0)))
    return k.reshape(b, n_sel, SEL_BLOCK, N_KV_HEADS, HEAD_DIM).transpose(0, 3, 1, 2, 4)

def cmp_to_sel_weights(n_cmp, n_sel):
    c0 = jnp.arange(n_cmp) * CMP_STRIDE
    c1 = c0 + CMP_LEN
    s0 = jnp.arange(n_sel) * SEL_BLOCK
    s1 = s0 + SEL_BLOCK
    ov = jnp.clip(jnp.minimum(c1[:, None], s1[None, :]) - jnp.maximum(c0[:, None], s0[None, :]), 0)
    return ov.astype(jnp.float32) / CMP_STRIDE

def sparse_branches(qn, qr, start, k_cmp, v_cmp, ks_blk, vs_blk):
    b, T = qn.shape[:2]
    qb = min(Q_BLOCK, T)
    nqb = -(-T // qb)
    pad = nqb * qb - T
    padw = ((0, 0), (0, pad), (0, 0), (0, 0), (0, 0))
    qn_b = jnp.pad(qn, padw).reshape(b, nqb, qb, N_KV_HEADS, GROUP, HEAD_DIM).swapaxes(0, 1)
    qr_b = jnp.pad(qr, padw).reshape(b, nqb, qb, N_KV_HEADS, GROUP, HEAD_DIM).swapaxes(0, 1)
    t_b = (start + jnp.arange(nqb * qb, dtype=jnp.int32)).reshape(nqb, qb)
    n_cmp = k_cmp.shape[1]
    n_sel = ks_blk.shape[2]
    k_sel = min(SEL_TOPN, n_sel)
    ov = cmp_to_sel_weights(n_cmp, n_sel)
    cmp_end = jnp.arange(n_cmp, dtype=jnp.int32) * CMP_STRIDE + CMP_LEN - 1
    jsel = jnp.arange(n_sel, dtype=jnp.int32)
    bi = jnp.arange(b)[:, None, None, None]
    gi = jnp.arange(N_KV_HEADS)[None, None, :, None]
    scale = HEAD_DIM ** -0.5

    def one(args):
        q_n, q_r, t = args
        s_c = jnp.einsum('bqgrd,bngd->bqgrn', q_n, k_cmp).astype(jnp.float32) * scale
        vm = (cmp_end[None, :] <= t[:, None])[None, :, None, None, :]
        p_c = jnp.where(vm, jax.nn.softmax(jnp.where(vm, s_c, NEG), axis=-1), 0.0)
        o_c = jnp.einsum('bqgrn,bngd->bqgrd', p_c.astype(v_cmp.dtype), v_cmp)
        p_blk = jnp.einsum('bqgrn,nj->bqgj', p_c, ov)
        cur = t // SEL_BLOCK
        forced = (jsel[None, :] == 0) | (jsel[None, :] == cur[:, None]) | (jsel[None, :] == cur[:, None] - 1)
        future = jsel[None, :] * SEL_BLOCK > t[:, None]
        score = jnp.where(future[None, :, None, :], NEG, p_blk + FORCE_BONUS * forced[None, :, None, :].astype(jnp.float32))
        _, idx = lax.top_k(score, k_sel)
        k_g = ks_blk[bi, gi, idx]
        v_g = vs_blk[bi, gi, idx]
        s_s = jnp.einsum('bqgrd,bqgkld->bqgrkl', q_r, k_g).astype(jnp.float32) * scale
        kpos = idx[..., None] * SEL_BLOCK + jnp.arange(SEL_BLOCK, dtype=jnp.int32)
        valid = (kpos <= t[None, :, None, None, None])[:, :, :, None]
        s_s = jnp.where(valid, s_s, NEG)
        sh = s_s.shape
        p_s = jax.nn.softmax(s_s.reshape(sh[:4] + (sh[4] * sh[5],)), axis=-1).reshape(sh)
        o_s = jnp.einsum('bqgrkl,bqgkld->bqgrd', p_s.astype(v_g.dtype), v_g)
        return o_c.astype(q_n.dtype), o_s.astype(q_n.dtype)

    o_c, o_s = lax.map(one, (qn_b, qr_b, t_b))
    shp = (b, nqb * qb, N_KV_HEADS, GROUP, HEAD_DIM)
    return o_c.swapaxes(0, 1).reshape(shp)[:, :T], o_s.swapaxes(0, 1).reshape(shp)[:, :T]

def window_banded(qr, kw, vw):
    b, T = qr.shape[:2]
    nb = T // BAND_BLOCK
    n_prev = WINDOW // BAND_BLOCK
    padw = ((0, 0), (n_prev * BAND_BLOCK, 0), (0, 0), (0, 0))
    kp = jnp.pad(kw, padw).reshape(b, nb + n_prev, BAND_BLOCK, N_KV_HEADS, HEAD_DIM)
    vp = jnp.pad(vw, padw).reshape(b, nb + n_prev, BAND_BLOCK, N_KV_HEADS, HEAD_DIM)
    kband = jnp.concatenate([kp[:, j:j + nb] for j in range(n_prev + 1)], axis=2)
    vband = jnp.concatenate([vp[:, j:j + nb] for j in range(n_prev + 1)], axis=2)
    qbk = qr.reshape(b, nb, BAND_BLOCK, N_KV_HEADS, GROUP, HEAD_DIM)
    tq = jnp.arange(T, dtype=jnp.int32).reshape(nb, BAND_BLOCK)
    tk = (jnp.arange(nb, dtype=jnp.int32)[:, None] - n_prev) * BAND_BLOCK + jnp.arange((n_prev + 1) * BAND_BLOCK, dtype=jnp.int32)[None, :]
    mask = (tk[:, None, :] <= tq[:, :, None]) & (tk[:, None, :] > tq[:, :, None] - WINDOW) & (tk[:, None, :] >= 0)
    o = attend(qbk, kband, vband, mask[None, :, :, None, None, :])
    return o.reshape(b, T, N_KV_HEADS, GROUP, HEAD_DIM)

def window_cached(qr, kw, vw, kw_prev, vw_prev, start):
    T = qr.shape[1]
    k_all = jnp.concatenate([kw_prev, kw], axis=1)
    v_all = jnp.concatenate([vw_prev, vw], axis=1)
    tk = start - kw_prev.shape[1] + jnp.arange(k_all.shape[1], dtype=jnp.int32)
    tq = start + jnp.arange(T, dtype=jnp.int32)
    mask = (tk[None, :] <= tq[:, None]) & (tk[None, :] > tq[:, None] - WINDOW)
    o = attend(qr, k_all, v_all, mask[None, :, None, None, :])
    keep = min(WINDOW, start + T)
    return o, k_all[:, -keep:], v_all[:, -keep:]

def peer(h, wq, sub_keys, u_tab, v_tab):
    b, T, D = h.shape
    n = b * T
    pb = min(PEER_BLOCK, n)
    nblk = -(-n // pb)
    hf = jnp.pad(h.reshape(n, D), ((0, nblk * pb - n), (0, 0))).reshape(nblk, pb, D)

    def one(hx):
        qq = (hx @ wq).reshape(pb, PEER_HEADS, 2, PEER_HALF)
        s = jnp.einsum('nhcd,hckd->nhck', qq, sub_keys).astype(jnp.float32)
        s1, i1 = lax.top_k(s[:, :, 0], PEER_TOPK)
        s2, i2 = lax.top_k(s[:, :, 1], PEER_TOPK)
        cand = (s1[..., :, None] + s2[..., None, :]).reshape(pb, PEER_HEADS, PEER_TOPK * PEER_TOPK)
        cidx = (i1[..., :, None] * PEER_NKEYS + i2[..., None, :]).reshape(pb, PEER_HEADS, PEER_TOPK * PEER_TOPK)
        top, sel = lax.top_k(cand, PEER_TOPK)
        eidx = jnp.take_along_axis(cidx, sel, axis=-1)
        g = jax.nn.softmax(top, axis=-1)
        a = jax.nn.gelu(jnp.einsum('nd,nhkd->nhk', hx, u_tab[eidx]).astype(jnp.float32), approximate=False)
        w = (g * a).astype(hx.dtype)
        return jnp.einsum('nhk,nhkd->nd', w, v_tab[eidx])

    out = lax.map(one, hf).reshape(nblk * pb, D)[:n]
    return out.reshape(b, T, D)

def block(x, start, past, P):
    b, T, _ = x.shape
    pos = start + jnp.arange(T, dtype=jnp.int32)
    h = rmsnorm(x, P['norm_mix'])
    proj = h @ P['w_in']
    split_pts = np.cumsum(IN_SIZES)[:-1].tolist()
    cb, cc, chh, q, kc, vc, ks, vs, kw, vw, ng, mg = jnp.split(proj, split_pts, axis=-1)

    if past is None:
        conv_prev = jnp.zeros((b, CONV_K - 1, CONV_CH), x.dtype)
    else:
        conv_prev = past['conv']
    conv_in = jnp.concatenate([conv_prev, cc * chh], axis=1)
    cw = P['conv_w']
    conv_out = conv_in[:, 0:T] * cw[0]
    for k in range(1, CONV_K):
        conv_out = conv_out + conv_in[:, k:k + T] * cw[k]
    y_conv = (cb * conv_out) @ P['w_out_conv']
    new_conv = conv_in[:, -(CONV_K - 1):]

    kv_shape = (b, T, N_KV_HEADS, HEAD_DIM)
    qn = rmsnorm(q.reshape(b, T, N_KV_HEADS, GROUP, HEAD_DIM), P['q_norm'])
    qr = rope(qn, pos)
    kc = kc.reshape(kv_shape)
    vc = vc.reshape(kv_shape)
    ks = rope(rmsnorm(ks.reshape(kv_shape), P['k_norm_slc']), pos)
    vs = vs.reshape(kv_shape)
    kw = rope(rmsnorm(kw.reshape(kv_shape), P['k_norm_win']), pos)
    vw = vw.reshape(kv_shape)
    if past is None:
        kc_all, vc_all, ks_all, vs_all = kc, vc, ks, vs
    else:
        kc_all = jnp.concatenate([past['kc'], kc], axis=1)
        vc_all = jnp.concatenate([past['vc'], vc], axis=1)
        ks_all = jnp.concatenate([past['ks'], ks], axis=1)
        vs_all = jnp.concatenate([past['vs'], vs], axis=1)
    k_cmp = rmsnorm(compress(kc_all, P['cmp_pos_k'], P['cmp_w1_k'], P['cmp_b1_k'], P['cmp_w2_k']), P['k_norm_cmp'])
    v_cmp = compress(vc_all, P['cmp_pos_v'], P['cmp_w1_v'], P['cmp_b1_v'], P['cmp_w2_v'])
    o_cmp, o_slc = sparse_branches(qn, qr, start, k_cmp, v_cmp, to_blocks(ks_all), to_blocks(vs_all))
    if past is None:
        o_win = window_banded(qr, kw, vw)
        keep = min(WINDOW, T)
        kw_buf, vw_buf = kw[:, -keep:], vw[:, -keep:]
    else:
        o_win, kw_buf, vw_buf = window_cached(qr, kw, vw, past['kw'], past['vw'], start)
    g = jax.nn.sigmoid(ng.astype(jnp.float32)).reshape(b, T, N_KV_HEADS, GROUP, 3).astype(x.dtype)
    o = g[..., 0:1] * o_cmp + g[..., 1:2] * o_slc + g[..., 2:3] * o_win
    y_nsa = o.reshape(b, T, Q_W) @ P['w_out_nsa']

    ga, gb = jnp.split(jax.nn.sigmoid(mg.astype(jnp.float32)).astype(x.dtype), 2, axis=-1)
    x = x + (ga * y_conv + gb * y_nsa) @ P['w_o']
    x = x + peer(rmsnorm(x, P['norm_ffn']), P['peer_wq'], P['peer_sub_keys'], P['peer_u'], P['peer_v'])
    return x, (kc, vc, ks, vs, kw_buf, vw_buf, new_conv)

def setup_inputs(seed: int = 0) -> dict:
    key = jax.random.key(seed)
    keys = iter(jax.random.split(key, 48))

    def nrm(shape, scale):
        return jax.random.normal(next(keys), shape, jnp.float32) * scale

    def gain(n):
        return 1.0 + nrm((DEPTH, n), 0.1)

    n_pages = PAST_LEN // PAGE_SIZE
    n_pool = (5 * DEC_BATCH * n_pages + 3) // 4
    win_buf = min(WINDOW, PAST_LEN)
    pool_shape = (DEPTH, n_pool, PAGE_SIZE, N_KV_HEADS, HEAD_DIM)
    page_table = jax.random.permutation(next(keys), n_pool)[:DEC_BATCH * n_pages].reshape(DEC_BATCH, n_pages).astype(jnp.int32)
    return {
        'x_prompt': nrm((BATCH, SEQ, D_MODEL), 1.0),
        'x_sample': nrm((DEC_BATCH, DEC_SEQ, D_MODEL), 1.0),
        'cache_cmp_k': nrm(pool_shape, 1.0),
        'cache_cmp_v': nrm(pool_shape, 1.0),
        'cache_slc_k': nrm(pool_shape, 1.0),
        'cache_slc_v': nrm(pool_shape, 1.0),
        'cache_win_k': nrm((DEPTH, DEC_BATCH, win_buf, N_KV_HEADS, HEAD_DIM), 1.0),
        'cache_win_v': nrm((DEPTH, DEC_BATCH, win_buf, N_KV_HEADS, HEAD_DIM), 1.0),
        'state_conv': nrm((DEPTH, DEC_BATCH, CONV_K - 1, CONV_CH), 1.0),
        'page_table': page_table,
        'norm_mix': gain(D_MODEL),
        'w_in': nrm((DEPTH, D_MODEL, IN_WIDTH), D_MODEL ** -0.5),
        'conv_w': nrm((DEPTH, CONV_K, CONV_CH), 0.5),
        'cmp_pos_k': nrm((DEPTH, CMP_LEN, HEAD_DIM), 0.1),
        'cmp_w1_k': nrm((DEPTH, CMP_LEN, HEAD_DIM, CMP_HIDDEN), (CMP_LEN * HEAD_DIM) ** -0.5),
        'cmp_b1_k': nrm((DEPTH, CMP_HIDDEN), 0.01),
        'cmp_w2_k': nrm((DEPTH, CMP_HIDDEN, HEAD_DIM), CMP_HIDDEN ** -0.5),
        'cmp_pos_v': nrm((DEPTH, CMP_LEN, HEAD_DIM), 0.1),
        'cmp_w1_v': nrm((DEPTH, CMP_LEN, HEAD_DIM, CMP_HIDDEN), (CMP_LEN * HEAD_DIM) ** -0.5),
        'cmp_b1_v': nrm((DEPTH, CMP_HIDDEN), 0.01),
        'cmp_w2_v': nrm((DEPTH, CMP_HIDDEN, HEAD_DIM), CMP_HIDDEN ** -0.5),
        'q_norm': gain(HEAD_DIM),
        'k_norm_cmp': gain(HEAD_DIM),
        'k_norm_slc': gain(HEAD_DIM),
        'k_norm_win': gain(HEAD_DIM),
        'w_out_conv': nrm((DEPTH, CONV_CH, D_MODEL), CONV_CH ** -0.5),
        'w_out_nsa': nrm((DEPTH, Q_W, D_MODEL), Q_W ** -0.5),
        'w_o': nrm((DEPTH, D_MODEL, D_MODEL), D_MODEL ** -0.5),
        'norm_ffn': gain(D_MODEL),
        'peer_wq': nrm((DEPTH, D_MODEL, PEER_HEADS * PEER_QDIM), D_MODEL ** -0.5),
        'peer_sub_keys': nrm((DEPTH, PEER_HEADS, 2, PEER_NKEYS, PEER_HALF), PEER_HALF ** -0.5),
        'peer_u': nrm((DEPTH, PEER_EXPERTS, D_MODEL), D_MODEL ** -0.5),
        'peer_v': nrm((DEPTH, PEER_EXPERTS, D_MODEL), PEER_HEADS ** -0.5),
    }

def reference(x_prompt, x_sample, cache_cmp_k, cache_cmp_v, cache_slc_k, cache_slc_v, cache_win_k, cache_win_v, state_conv, page_table, norm_mix, w_in, conv_w, cmp_pos_k, cmp_w1_k, cmp_b1_k, cmp_w2_k, cmp_pos_v, cmp_w1_v, cmp_b1_v, cmp_w2_v, q_norm, k_norm_cmp, k_norm_slc, k_norm_win, w_out_conv, w_out_nsa, w_o, norm_ffn, peer_wq, peer_sub_keys, peer_u, peer_v):
    yp, ys = x_prompt, x_sample
    p_states, s_states = [], []
    for layer in range(DEPTH):
        P = {
            'norm_mix': norm_mix[layer], 'w_in': w_in[layer], 'conv_w': conv_w[layer],
            'cmp_pos_k': cmp_pos_k[layer], 'cmp_w1_k': cmp_w1_k[layer], 'cmp_b1_k': cmp_b1_k[layer], 'cmp_w2_k': cmp_w2_k[layer],
            'cmp_pos_v': cmp_pos_v[layer], 'cmp_w1_v': cmp_w1_v[layer], 'cmp_b1_v': cmp_b1_v[layer], 'cmp_w2_v': cmp_w2_v[layer],
            'q_norm': q_norm[layer], 'k_norm_cmp': k_norm_cmp[layer], 'k_norm_slc': k_norm_slc[layer], 'k_norm_win': k_norm_win[layer],
            'w_out_conv': w_out_conv[layer], 'w_out_nsa': w_out_nsa[layer], 'w_o': w_o[layer], 'norm_ffn': norm_ffn[layer],
            'peer_wq': peer_wq[layer], 'peer_sub_keys': peer_sub_keys[layer], 'peer_u': peer_u[layer], 'peer_v': peer_v[layer],
        }
        yp, st_p = block(yp, 0, None, P)
        p_states.append(st_p)
        past = {
            'kc': gather_pages(cache_cmp_k[layer], page_table),
            'vc': gather_pages(cache_cmp_v[layer], page_table),
            'ks': gather_pages(cache_slc_k[layer], page_table),
            'vs': gather_pages(cache_slc_v[layer], page_table),
            'kw': cache_win_k[layer], 'vw': cache_win_v[layer], 'conv': state_conv[layer],
        }
        ys, st_s = block(ys, PAST_LEN, past, P)
        s_states.append(st_s)
    pn = [jnp.stack(f) for f in zip(*p_states)]
    sn = [jnp.stack(f) for f in zip(*s_states)]
    return (yp, ys, pn[0], pn[1], pn[2], pn[3], pn[4], pn[5], pn[6], sn[0], sn[1], sn[2], sn[3], sn[4], sn[5], sn[6])


_drawn_inputs = setup_inputs


def setup_inputs(seed=0):
    import zlib

    import numpy as np

    out = dict(_drawn_inputs(seed))
    spreads = {}
    factors = {'cmp_pos_k': 5.538, 'cmp_b1_k': 8.0, 'cmp_b1_v': 8.0, 'q_norm': 3.694, 'k_norm_cmp': 5.795}
    for name, (base, spread) in spreads.items():
        noise = np.random.default_rng([zlib.crc32(name.encode()), seed]).standard_normal(out[name].shape)
        drawn = base * np.exp(spread * noise) if base else spread * noise
        out[name] = jnp.asarray(drawn.astype(out[name].dtype))
    for name, factor in factors.items():
        out[name] = (out[name] * factor).astype(out[name].dtype)
    return out
```

```python
from contextlib import ExitStack

import numpy as np

import concourse.bass as bass
from concourse import mybir

D = 1024
SEQ = 256
NB = 8
NQ = 4
PAST = 1024
PAGE = 128
NPOOL = 80
NH, NG, R = 8, 2, 4
HD = 64
STRIDE = 16
WINDOW = 512
BLK = 64
NSEL = 17
PH, PK, PTOP = 8, 128, 16
EPS = 1e-6
NEG = -1e30
P = 128
NS = NB * NQ
NT = SEQ + NS
KC = D // P
TILES = [(0, P), (P, P), (2 * P, NS)]
QKV = 12 * HD + 4 * NG * HD + 3 * NH
PIECES = [(0, 512), (512, 512), (1024, QKV - 1024)]
PAGES = PAST // PAGE
SETB = 4
SCALE = HD ** -0.5
RING = 4
HALF = PK // 2
GT = 6
VBANK = (0, 1, 5, 6)
STAGE = 5

F32 = mybir.dt.float32
BF16 = mybir.dt.bfloat16
I32 = mybir.dt.int32
U32 = mybir.dt.uint32
ALU = mybir.AluOpType
ACT = mybir.ActivationFunctionType
AX = mybir.AxisListType

C_KC, C_VC, C_VS, C_NG = 768, 896, 1024, 1280

W_TOK, W_CONV, W_MG, W_YC, W_YN, W_O, W_Q, W_U, W_V, W_END = 0, 12, 24, 40, 44, 48, 56, 72, 200, 328


def columns(parts):
    at, out = 0, {}
    for name, n in parts:
        out[name] = (at, at + n)
        at += n
    return out, at


CONST, NCONST = columns([("ident", P), ("iota", P), ("ones", P), ("cos", 3 * HD), ("sin", 3 * HD), ("causal", 2 * P),
                         ("cmpmask", 32), ("newmask", 2 * NS), ("winmask", NQ), ("ov", NSEL), ("forced", NSEL),
                         ("jp1", NSEL), ("rep", 2 * P), ("gsel", NH), ("iota16", PTOP)])
SMALL, NSMALL = columns([("norm_mix", KC), ("norm_ffn", KC), ("conv_w", 12), ("b1", 2), ("pos", 32),
                         ("state", 4 * NB * 2), ("gain", 12 * HD), ("kcgain", HD), ("w2", 2 * HD)])

ARENA = PK * NT
AR, USED = columns([("a", 10752), ("b", 6984), ("qnT", 1024), ("qrT", 1024), ("qbn", 256), ("qbr", 256), ("ksT", NT),
                    ("kwT", NT), ("z", 4 * NT), ("oT", 4 * NT), ("up", 4 * 258), ("us", 4 * NB * 6), ("vnew", 768),
                    ("kcT", 4 * P + 16), ("vc", 9 * P), ("sec", 256), ("hid", 256), ("kcn", 5 * P),
                    ("vset", 6144), ("kring", 1536), ("xcp", 512)])
assert USED <= ARENA, (USED, ARENA)
UP0 = HALF * NT
RT, USED = columns([("qq", 16 * NT), ("sub", 2048), ("sp", 3 * 2048), ("lv", 256), ("li", 256), ("lf", 256),
                    ("tv", 128), ("ti", 128), ("ab", 256), ("abf", 256), ("gi", 9 * P), ("z8", 16)])
RT["cand"], RT["eq"] = (0, 2048), (2048, 4096)
assert USED <= HALF * NT, USED


def program(nc, A, O, stage):
    with ExitStack() as ctx:
        def sb(name, shape, dt=F32):
            return ctx.enter_context(nc.sbuf_tensor(name, shape, dt))

        def sem(name):
            return ctx.enter_context(nc.semaphore(name))

        ps = ctx.enter_context(nc.psum_tensor("ps", [P, 8, 512], F32))
        cst = sb("cst", [P, NCONST])
        sml = sb("sml", [P, NSMALL])
        ring = sb("ring", [P, RING, 1024])
        xT = sb("xT", [P, KC, NT])
        hT = sb("hT", [P, KC, NT])
        rr = sb("rr", [P, 2, NT])
        ptab = sb("ptab", [1, 64], I32)
        oh = sb("oh", [P, 3, GT, P + HALF])
        zero16 = sb("zero16", [P, NT], BF16)
        arena = sb("arena", [P, ARENA])
        sg = sb("sg", [P, 3, 3 * NH])
        rg = sb("rg", [P, 6])
        bias = sb("bias", [P, 2])
        st = sb("st", [P, 96])

        def C(name, n=P):
            a, b = CONST[name]
            return cst[0:n, a:b]

        def M(name):
            a, b = SMALL[name]
            return sml[:, a:b]

        def ar(name, lo=0, n=None):
            a, b = AR[name]
            return arena[:, a + lo:(b if n is None else a + lo + n)]

        def rt(name):
            a, b = RT[name]
            return arena[:, UP0 + a:UP0 + b]

        def over(x, axis, n):
            y = x.unsqueeze(axis)
            shape = list(y.shape)
            shape[axis] = n
            return y.broadcast_to(shape)

        ident = C("ident")
        ptok = ar("b", 0, 3 * QKV).rearrange("p (t c) -> p t c", t=3)
        qn = ar("b", 3 * QKV, 768)
        qr = ar("b", 3 * QKV + 768, 768)
        tmpq = ar("b", 3 * QKV + 1536, 768)
        xsq = ar("b", 0, KC * NT).rearrange("p (k n) -> p k n", k=KC)
        mg = ar("b", 0, 16 * NT).rearrange("p (k n) -> p k n", k=16)
        mt = ar("b", 16 * NT, NT)
        w1 = ar("a", 0, 4096).rearrange("p (v k f) -> p v k f", v=2, k=16)
        xc = ar("a", 4096, 6144).rearrange("p (i j k g c) -> p i j k g c", i=3, j=16, k=8, g=NG)
        xcp = ar("xcp").rearrange("p (v k g c) -> p v k g c", v=2, k=8, g=NG)
        sc = ar("a", 0, 2048)
        pT = ar("a", 2048, 2560)
        vset = [ar("vset"), ar("a", 4608, 6144)]
        qnT = ar("qnT").rearrange("p (r n) -> p r n", r=R)
        qrT = ar("qrT").rearrange("p (r n) -> p r n", r=R)
        qbn = ar("qbn").rearrange("p (b m) -> p b m", b=NB)
        qbr = ar("qbr").rearrange("p (b m) -> p b m", b=NB)
        ksT, kwT = ar("ksT"), ar("kwT")
        zT = ar("z").rearrange("p (k n) -> p k n", k=4)
        oT = ar("oT").rearrange("p (r n) -> p r n", r=R)
        up = ar("up").rearrange("p (k n) -> p k n", k=4)
        us = ar("us").rearrange("p (k b n) -> p k b n", k=4, b=NB)
        vnew = ar("vnew").rearrange("p (t c) -> p t c", t=3)
        kcT = ar("kcT")
        vc = ar("vc").rearrange("p (b c) -> p b c", c=P)
        sec, hid = ar("sec"), ar("hid")
        kcn = ar("kcn").rearrange("p (t c) -> p t c", c=P)
        kring = ar("kring").rearrange("p (s c) -> p s c", s=3)

        class Sems(dict):
            def __missing__(self, name):
                self[name] = sem(name)
                return self[name]

        S = Sems()
        ring_in = [sem(f"ring_in{i}") for i in range(RING)]

        def link_on(eng, s):
            count = [0]

            def link(ins):
                count[0] += 1
                ins.then_inc(s, 1)
                eng.wait_ge(s, count[0])
            return link

        block = ctx.enter_context(nc.Block())

        def slot_ready(eng, i):
            eng.wait_ge(ring_in[i % RING], 16 * (i // RING + 1))

        @block.sync
        def _(sp):
            sp.dma_start(xT[:, :, :], A["xT"]).then_inc(S["x_in"], 16)
            sp.dma_start(cst[:, :], A["consts"]).then_inc(S["consts_in"], 16)
            sp.dma_start(sml[:, :], A["smalls"]).then_inc(S["smalls_in"], 16)

            def load(i):
                if i >= RING:
                    sp.wait_ge(S["slots_used"], i - RING + 1)
                if i < W_CONV:
                    w = PIECES[i // 4][1]
                    sp.dma_start(ring[:, i % RING, 0:2 * w], A[f"wtok{i // 4}"][i % 4]).then_inc(ring_in[i % RING], 16)
                    return
                src = A["wT"][i - W_CONV] if i < W_YC else A["wout"][i - W_YC]
                sp.dma_start(ring[:, i % RING, :], src).then_inc(ring_in[i % RING], 16)

            for i in range(W_CONV):
                load(i)
                if i == RING - 1:
                    sp.dma_start(ar("a", 0, 4096), A["w1"]).then_inc(S["w1_in"], 16)
            def load_chunks(u):
                t, v = u // 2, u % 2
                if u == 0:
                    sp.wait_ge(S["ptab_in"], 16)
                if u >= 3:
                    sp.wait_ge(S["comp_mm"], u - 2)
                for j in range(16):
                    page = sp.value_load(ptab[0:1, 16 * t + j:16 * t + j + 1], min_val=0, max_val=NPOOL - 1)
                    sp.dma_start(xc[:, u % 3, j, :, :, :].rearrange("p k g c -> p (k g c)"),
                                 A["cache_cmp_" + "kv"[v]][bass.ds(page, 1)].rearrange("o p c -> (o p) c")).then_inc(S[f"xc_in{u % 3}"], 16)

            for i in range(W_CONV, {1: W_MG, 2: W_MG, 3: W_YC, 4: W_Q, 5: W_U}[stage]):
                if stage >= 2 and i in (W_CONV, W_CONV + 2, W_CONV + 4):
                    load_chunks((i - W_CONV) // 2)
                if stage >= 2 and i == W_MG + RING:
                    for u in range(3, 8):
                        load_chunks(u)
                load(i)
                if i == W_Q - 1 and stage >= 5:
                    sp.dma_start(rt("sub"), A["sub"]).then_inc(S["sub_in"], 16)
            if stage >= 5:
                with sp.Fori(0, PK // RING) as it:
                    for s in range(RING):
                        sp.wait_ge(S["slots_used"], it * RING + (W_U - RING + s + 1))
                        sp.dma_start(ring[:, s, :], A["uT"][bass.ds(it * RING + s, 1)].rearrange("o p c -> (o p) c")).then_inc(ring_in[s], 16)
                with sp.Fori(0, PK // RING) as it:
                    for s in range(RING):
                        sp.wait_ge(S["slots_used"], it * RING + (W_V - RING + s + 1))
                        sp.dma_start(ring[:, s, :], A["v"][bass.ds(it * RING + s, 1)].rearrange("o p c -> (o p) c")).then_inc(ring_in[s], 16)
                for q in range(2):
                    sp.wait_ge(S["y_ready"], 3 + q)
                    sp.dma_start(O["yT"][:, 4 * q:4 * q + 4, :], xT[:, 4 * q:4 * q + 4, :]).then_inc(S["y_out"], 16)
                sp.wait_ge(S["y_out"], 32)
            elif stage >= 4:
                sp.wait_ge(S["x1_ready"], KC)
                sp.dma_start(O["yT"][:, :, :], xT[:, :, :]).then_inc(S["y_out"], 16)
                sp.wait_ge(S["y_out"], 16)

        @block.gpsimd
        def _(pool):
            pool.memset(ar("qbn"), 0.0).then_inc(S["u_free"], 2)
            pool.memset(ar("qbr"), 0.0).then_inc(S["oh_used"], 3)
            pool.memset(up[:, :, 0:2], 0.0).then_inc(S["w_free"], 3)
            pool.memset(hid, 0.0)
            pool.memset(zero16[:, :], 0.0).then_inc(S["zeroed"], 1)
            pool.dma_start(ptab[:, :], A["pages"]).then_inc(S["ptab_in"], 16)
            if stage >= 4:
                pool.wait_ge(S["ptab_in"], 16)
                for b in range(NB):
                    s, b4 = b // SETB, b % SETB
                    if b4 == 0 and s == 1:
                        pool.wait_ge(S["comp_mm"], 10)
                        pool.wait_ge(S["kcn_ready"], 2)
                    for h in range(2):
                        if b:
                            pool.wait_ge(S["k_scored"], 3 * (b - 1) + h + 1)
                        for p in range(4):
                            page = pool.value_load(ptab[0:1, b * PAGES + 4 * h + p:b * PAGES + 4 * h + p + 1], min_val=0, max_val=NPOOL - 1)
                            pool.dma_start(kring[:, h, p * P:(p + 1) * P], A["cache_slc_k"][bass.ds(page, 1)].rearrange("o p c -> (o p) c"))\
                                .then_inc(S[f"k_in{h}"], 16)
                            pool.dma_start(vset[s][:, (b4 * 8 + 4 * h + p) * P:(b4 * 8 + 4 * h + p + 1) * P],
                                           A["cache_slc_v"][bass.ds(page, 1)].rearrange("o p c -> (o p) c")).then_inc(S[f"v_in{s}"], 16)
                    if b:
                        pool.wait_ge(S["k_scored"], 3 * (b - 1) + 3)
                    pool.dma_start(kring[:, 2, :], A["cache_win_kT"][b]).then_inc(S["k_in2"], 16)
                    pool.dma_start(vset[s][:, 4096 + b4 * 512:4096 + (b4 + 1) * 512].rearrange("p (t c) -> p t c", t=4),
                                   A["cache_win_v"][b].rearrange("(t p) c -> p t c", p=P)).then_inc(S[f"v_in{s}"], 16)
                for v in range(2):
                    pool.dma_start(O[["wk", "wv"][v]][:, 0:WINDOW - NQ, :], A["cache_win_" + "kv"[v]][:, NQ:WINDOW, :])\
                        .then_inc(S["win_kept"], 16)
                pool.wait_ge(S["win_kept"], 32)

        @block.scalar
        def _(act):
            act.wait_ge(S["x_in"], 16)
            act.activation(xsq, xT[:, :, :], ACT.Square).then_inc(S["x_squared"], 1)
            act.wait_ge(S["x_var"], 1)
            act.activation(rr[:, 1, :], rr[:, 0, :], ACT.Sqrt).then_inc(S["x_std"], 1)
            for p, (c0, w) in enumerate(PIECES):
                act.wait_ge(S["slots_used"], 4 * (p + 1))
                for t, (n0, n) in enumerate(TILES):
                    act.activation(ptok[0:n, t, c0:c0 + w], ps[0:n, 3 * (p % 2) + t, 0:w], ACT.Copy).then_inc(S["tok_copied"], 1)
            def copy_cc(c):
                act.wait_ge(S["slots_used"], W_CONV + 3 * c + 1)
                if c:
                    act.wait_ge(S["u_ready"], c)
                act.activation(rr[:, 1, :], ps[:, 5, 0:NT], ACT.Copy).then_inc(S["cc_copied"], 1)

            for t, (n0, n) in enumerate(TILES):
                act.wait_ge(S["qk_var"], t + 1)
                act.activation(st[0:n, 16:28], st[0:n, 0:12], ACT.Sqrt).then_inc(S["qk_std"], 1)
                act.wait_ge(S["tok_copied"], 9)
                for name, c in (("kc", C_KC), ("vc", C_VC)):
                    act.dma_start(O[name][n0:n0 + n, :], ptok[0:n, t, c:c + P]).then_inc(S["kv_rows_out"], 16)
                act.dma_start(O["vs"][n0:n0 + n, :], ptok[0:n, t, C_VS:C_VS + P]).then_inc(S["rows_out"], 16)
                copy_cc(t)
                act.wait_ge(S["qk_ready"], t + 1)
                act.dma_start(O["ks"][n0:n0 + n, :], qr[0:n, 512:640]).then_inc(S["k_rows_out"], 16)
                for v, src in enumerate([qr[0:n, 640:768], ptok[0:n, t, C_VS + P:C_VS + 2 * P]]):
                    done = S[["k_rows_out", "rows_out"][v]]
                    if t < 2:
                        act.dma_start(O[["kw", "vw"][v]][n0:n0 + n, :], src).then_inc(done, 16)
                    else:
                        act.dma_start(O[["wk", "wv"][v]][:, WINDOW - NQ:WINDOW, :], src).then_inc(done, 16)
                act.wait_ge(S["qk_turned"], t + 1)
                if t < 2:
                    act.activation(qnT[:, :, n0:n0 + n], ps[:, 0, :].rearrange("p (r n) -> p r n", r=R), ACT.Copy)
                    act.activation(qrT[:, :, n0:n0 + n], ps[:, 1, :].rearrange("p (r n) -> p r n", r=R), ACT.Copy)
                    for v in range(2):
                        for g in range(NG):
                            for s2 in range(2):
                                act.activation(xcp[64 * s2:64 * s2 + 64, v, :, g, 8 * t:8 * t + 8],
                                               ps[64 * g:64 * g + 64, 2, 256 + v * P:256 + (v + 1) * P]
                                               .rearrange("p (c k s) -> p s k c", k=8, s=2)[:, s2, :, :], ACT.Copy)
                else:
                    act.wait_ge(S["zeroed"], 1)
                    for i, q in enumerate((qbn, qbr)):
                        for g in range(NG):
                            for r in range(R):
                                act.activation(
                                    q[64 * g:64 * g + 64, :, 16 * g:16 * g + 16].rearrange("p b (q r) -> p b q r", r=R)[:, :, :, r],
                                    ps[64 * g:64 * g + 64, i, r * P:r * P + NS].rearrange("p (b q) -> p b q", b=NB), ACT.Copy)
                act.activation(ksT[:, n0:n0 + n], ps[:, 2, 0:n], ACT.Copy)
                act.activation(kwT[:, n0:n0 + n], ps[:, 2, P:P + n], ACT.Copy).then_inc(S["qT_copied"], 1)
            copy_cc(3)
            for t, (n0, n) in enumerate(TILES):
                act.activation(sg[0:n, t, :], ptok[0:n, t, C_NG:C_NG + 24], ACT.Exp, scale=-1.0).then_inc(S["gate_exp"], 1)
            act.wait_ge(S["u_ready"], 4)
            cstate = O["cstate"].rearrange("p (k n) -> p k n", k=4)
            act.dma_start(cstate[:, :, 0:2], up[:, :, 256:258]).then_inc(S["conv_out"], 16)
            for k in range(4):
                act.dma_start(cstate[:, k, 2:18].rearrange("p (b n) -> p b n", b=NB), us[:, k, :, 4:6]).then_inc(S["conv_out"], 16)
            for name, count in (("kv_rows_out", 6), ("rows_out", 6), ("k_rows_out", 6), ("conv_out", 5)):
                act.wait_ge(S[name], 16 * count)
            act.wait_ge(S["vnew_ready"], 3)

            for u in range(10 if stage >= 2 else 0):
                t, v = u // 2, u % 2
                n = P if t < 4 else 16
                if u:
                    act.wait_ge(S["hid_ready"], u)
                act.wait_ge(S["comp_mm"], u + 1)
                act.activation(sec[:, 0:2 * n], ps[:, 4, 256:256 + 2 * n], ACT.Copy).then_inc(S["sec_copied"], 1)
                act.wait_ge(S["hid_sum"], u + 1)
                if u:
                    act.wait_ge(S["comp_out"], u)
                L = 64 if t < 4 else 16
                view = lambda x: x[:, 0:2 * n].rearrange("p (g c) -> p g c", c=L)[:, :, 0:L - 1]
                act.activation(view(hid), view(sec), ACT.Gelu, bias=bias[:, v:v + 1]).then_inc(S["hid_ready"], 1)
                act.wait_ge(S["comp_out"], u + 1)
                if v == 0:
                    act.activation(kcn[0:n, t, :], ps[0:n, 5, 0:P], ACT.Copy).then_inc(S["cmp_copied"], 1)
                elif t < 4:
                    act.activation(vc[0:64, 2 * t:2 * t + 2, :], ps[0:64, 5, 0:256].rearrange("p (b c) -> p b c", b=2), ACT.Copy)\
                        .then_inc(S["cmp_copied"], 1)
                else:
                    act.activation(vc[0:16, 8, :], ps[0:16, 5, 0:P], ACT.Copy).then_inc(S["cmp_copied"], 1)
            if stage >= 2:
                act.wait_ge(S["kcn_var"], 1)
                act.activation(st[:, 16:26], st[:, 0:10], ACT.Sqrt).then_inc(S["kcn_std"], 1)
                for t in range(5):
                    n = P if t < 4 else 16
                    act.wait_ge(S["kcn_turned"], t + 1)
                    act.activation(kcT[:, t * P:t * P + n], ps[:, 6 + t % 2, 0:n], ACT.Copy).then_inc(S["kcT_copied"], 1)

            for u in range(4 if stage >= 3 else 0):
                qt, g = u // 2, u % 2
                nk = P * (qt + 1)
                for c in range(4):
                    i = 4 * u + c
                    act.wait_ge(S["slots_used"], W_MG + i + 1)
                    act.activation(mg[:, i, :], ps[:, 6 + i % 2, 0:NT], ACT.Exp, scale=-1.0).then_inc(S["mg_exp"], 1)
                    if c == 0:
                        act.wait_ge(S["pc_shift"], u + 1)
                        act.activation(st[:, 32:96], st[:, 32:96], ACT.Exp).then_inc(S["pc_exp"], 1)
                        act.wait_ge(S["ps_max"], u + 1)
                        for i8 in range(8):
                            last = act.activation(sc[:, i8 * nk:(i8 + 1) * nk], sc[:, i8 * nk:(i8 + 1) * nk], ACT.Exp,
                                                  bias=st[:, i8:i8 + 1], accum_out=st[:, 16 + i8:17 + i8])
                        last.then_inc(S["ps_exp"], 1)
                act.wait_ge(S["pp_turned"], u + 1)
                w = 1024 * (qt + 1)
                act.activation(pT[:, 0:w // 2], ps[:, 0:2, :].rearrange("p b c -> p (b c)")[:, 0:w // 2], ACT.Copy)
                act.activation(pT[0:16, 2048:2560], ps[0:16, 4, :], ACT.Copy).then_inc(S["pT_act"], 1)
                act.wait_ge(S["po_mm"], u + 1)
                act.activation(oT[64 * g:64 * g + 64, :, qt * P:(qt + 1) * P],
                               ps[64 * g:64 * g + 64, 5, :].rearrange("p (r n) -> p r n", r=R), ACT.Copy).then_inc(S["po_copied"], 1)

            for s in range(2 if stage >= 4 else 0):
                act.wait_ge(S["sc_max"], s + 1)
                act.activation(sc[:, 1600:1663], sc[:, 1600:1663], ACT.Exp, bias=st[:, 2:3], accum_out=st[:, 10:11]).then_inc(S["sc_exp"], 1)
                act.wait_ge(S["ss_max"], s + 1)
                act.activation(sc[:, 0:1056], sc[:, 0:1056], ACT.Exp, bias=st[:, 0:1], accum_out=st[:, 8:9])
                act.activation(sc[:, 1056:1600], sc[:, 1056:1600], ACT.Exp, bias=st[:, 1:2], accum_out=st[:, 9:10]).then_inc(S["ss_exp"], 1)
                act.wait_ge(S["sp_turned"], s + 1)
                act.activation(pT[:, 0:1024], ps[:, 0:2, :].rearrange("p b c -> p (b c)"), ACT.Copy).then_inc(S["spT_act"], 1)
                act.wait_ge(S["so_mm"], s + 1)
                for g in range(NG):
                    for r in range(R):
                        last = act.activation(
                            oT[64 * g:64 * g + 64, r, SEQ + 16 * s:SEQ + 16 * s + 16].rearrange("p (b q) -> p b q", b=SETB),
                            ps[64 * g:64 * g + 64, 7, 0:P].rearrange("p (b g q r) -> p b g q r", b=SETB, g=NG, q=NQ)[:, :, g, :, r], ACT.Copy)
                last.then_inc(S["so_copied"], 1)

            if stage >= 5:
                act.wait_ge(S["x1_ready"], KC)
                act.activation(xsq, xT[:, :, :], ACT.Square).then_inc(S["x_squared"], 1)
                act.wait_ge(S["x_var"], 2)
                act.activation(rr[:, 1, :], rr[:, 0, :], ACT.Sqrt).then_inc(S["x_std"], 1)
                for i in range(16):
                    act.wait_ge(S["slots_used"], W_Q + i + 1)
                    act.activation(rt("qq")[:, i * NT:(i + 1) * NT], ps[:, i % 2, 0:NT], ACT.Copy).then_inc(S["qq_copied"], 1)
                for t, (n0, n) in enumerate(TILES):
                    act.wait_ge(S["pk_mm"], t + 1)
                    act.activation(rt("sp")[0:n, t * 2048:(t + 1) * 2048], ps[0:n, 4:8, :].rearrange("p b c -> p (b c)"), ACT.Copy)\
                        .then_inc(S["pk_copied"], 1)

                def gelus(it, j0):
                    for s in range(RING):
                        act.wait_ge(S["slots_used"], it * RING + (W_U + j0 + s + 1))
                        act.activation(arena[:, bass.ds((it * RING + (j0 + s)) * NT, NT)], ps[:, s % 2, 0:NT], ACT.Gelu).then_inc(S["u_free"], 1)

                for t, (n0, n) in enumerate(TILES):
                    with act.Fori(0, 4) as it:
                        gelus(it, 16 * t)
                    act.wait_ge(S["top_shift"], t + 1)
                    act.activation(rt("tv")[0:n, :], rt("tv")[0:n, :], ACT.Exp).then_inc(S["top_exp"], 1)
                with act.Fori(0, 4) as it:
                    gelus(it, 48)
                act.wait_ge(S["route_copied"], 1)
                with act.Fori(0, HALF // RING) as it:
                    gelus(it, HALF)

        @block.vector
        def _(dve):
            link = link_on(dve, S["dve_order"])

            def normalize(gain):
                dve.tensor_scalar(rr[:, 0, :], ps[:, 0, 0:NT], 1.0 / D, EPS, ALU.mult, ALU.add).then_inc(S["x_var"], 1)

            def scaled(gain):
                link(dve.reciprocal(rr[:, 0, :], rr[:, 1, :]))
                for k in range(KC):
                    last = dve.scalar_tensor_tensor(out=hT[:, k, :], in0=xT[:, k, :], scalar=gain[:, k:k + 1],
                                                    in1=rr[:, 0, :], op0=ALU.mult, op1=ALU.mult)
                last.then_inc(S["h_ready"], 1)

            dve.wait_ge(S["smalls_in"], 16)
            dve.wait_ge(S["consts_in"], 16)
            dve.wait_ge(S["x_sumsq"], 1)
            normalize(M("norm_mix"))
            dve.wait_ge(S["x_std"], 1)
            scaled(M("norm_mix"))
            dve.wait_ge(S["zeroed"], 1)
            dve.tensor_copy(us[:, :, :, 0:2], M("state").rearrange("p (k b n) -> p k b n", k=4, b=NB))

            heads = lambda x: x.rearrange("p (h d) -> p h d", d=HD)

            def head_rows(t, n):
                dve.wait_ge(S["tok_copied"], 3 + t + 1)
                if t:
                    dve.wait_ge(S["qk_turned"], t)
                    dve.wait_ge(S["k_rows_out"], 32 * t)
                qk = ptok[0:n, t, 0:768]
                link(dve.tensor_tensor(tmpq[0:n, :], qk, qk, ALU.mult))
                link(dve.tensor_reduce(st[0:n, 0:12], heads(tmpq[0:n, :]), AX.X, ALU.add))
                dve.tensor_scalar(st[0:n, 0:12], st[0:n, 0:12], 1.0 / HD, EPS, ALU.mult, ALU.add).then_inc(S["qk_var"], 1)
                dve.wait_ge(S["qk_std"], t + 1)
                link(dve.reciprocal(st[0:n, 0:12], st[0:n, 16:28]))
                link(dve.tensor_tensor(heads(qn[0:n, :]), heads(qk), over(st[0:n, 0:12], 2, HD), ALU.mult))
                link(dve.tensor_tensor(qn[0:n, :], qn[0:n, :], M("gain")[0:n, :], ALU.mult))
                cos, sin = C("cos", n)[:, t * HD:(t + 1) * HD], C("sin", n)[:, t * HD:(t + 1) * HD]
                q3, t3 = heads(qn[0:n, :]), heads(tmpq[0:n, :])
                dve.tensor_tensor(t3[:, :, 0:32], q3[:, :, 32:64], over(sin[:, 0:32], 1, 12), ALU.mult)
                dve.tensor_tensor(t3[:, :, 32:64], q3[:, :, 0:32], over(sin[:, 32:64], 1, 12), ALU.mult)
                link(dve.tensor_tensor(heads(qr[0:n, :]), q3, over(cos, 1, 12), ALU.mult))
                dve.tensor_tensor(qr[0:n, :], qr[0:n, :], tmpq[0:n, :], ALU.add).then_inc(S["qk_ready"], 1)

            cw = M("conv_w").rearrange("p (k c) -> p k c", k=3)

            def conv(c):
                dve.wait_ge(S["cc_copied"], c + 1)
                dve.wait_ge(S["slots_used"], W_CONV + 3 * c + 2)
                dve.tensor_tensor(up[:, c, 2:258], ps[:, 6, 0:SEQ], rr[:, 1, 0:SEQ], ALU.mult)
                dve.tensor_tensor(us[:, c, :, 2:6], ps[:, 6, SEQ:NT].rearrange("p (b n) -> p b n", b=NB),
                                  rr[:, 1, SEQ:NT].rearrange("p (b n) -> p b n", b=NB), ALU.mult).then_inc(S["u_ready"], 1)
                dve.wait_ge(S["u_ready"], c + 1)
                z_p, z_s = zT[:, c, 0:SEQ], zT[:, c, SEQ:NT].rearrange("p (b n) -> p b n", b=NB)
                dve.tensor_scalar(z_p, up[:, c, 0:SEQ], cw[:, 0, c:c + 1], None, ALU.mult)
                link(dve.tensor_scalar(z_s, us[:, c, :, 0:4], cw[:, 0, c:c + 1], None, ALU.mult))
                for k in (1, 2):
                    dve.scalar_tensor_tensor(out=z_p, in0=up[:, c, k:k + SEQ], scalar=cw[:, k, c:c + 1], in1=z_p, op0=ALU.mult, op1=ALU.add)
                    link(dve.scalar_tensor_tensor(out=z_s, in0=us[:, c, :, k:k + 4], scalar=cw[:, k, c:c + 1], in1=z_s, op0=ALU.mult, op1=ALU.add))
                dve.wait_ge(S["slots_used"], W_CONV + 3 * c + 3)
                dve.tensor_tensor(zT[:, c, :], ps[:, 7, 0:NT], zT[:, c, :], ALU.mult).then_inc(S["z_ready"], 1)

            for t, (n0, n) in enumerate(TILES):
                head_rows(t, n)
                conv(t)
            conv(3)
            dve.wait_ge(S["tok_copied"], 9)
            for t, (n0, n) in enumerate(TILES):
                dve.tensor_copy(vnew[0:n, t, :], ptok[0:n, t, C_VS:C_VS + 2 * P]).then_inc(S["vnew_ready"], 1)
            dve.wait_ge(S["gate_exp"], 3)
            for t, (n0, n) in enumerate(TILES):
                link(dve.tensor_scalar(sg[0:n, t, :], sg[0:n, t, :], 1.0, None, ALU.add))
                dve.reciprocal(sg[0:n, t, :], sg[0:n, t, :]).then_inc(S["gate_ready"], 1)

            if stage >= 2:
                dve.wait_ge(S["cbias_mm"], 1)
                dve.tensor_tensor(bias[:, :], ps[:, 7, 0:2], M("b1"), ALU.add)
            for u in range(10 if stage >= 2 else 0):
                t, v = u // 2, u % 2
                n = P if t < 4 else 16
                dve.wait_ge(S["comp_mm"], u + 1)
                dve.wait_ge(S["sec_copied"], u + 1)
                L = 64 if t < 4 else 16
                f = ps[:, 4, 0:2 * n].rearrange("p (g c) -> p g c", c=L)
                s3 = sec[:, 0:2 * n].rearrange("p (g c) -> p g c", c=L)
                dve.tensor_tensor(s3[:, :, 0:L - 1], f[:, :, 0:L - 1], s3[:, :, 1:L], ALU.add).then_inc(S["hid_sum"], 1)
            if stage >= 2:
                dve.wait_ge(S["cmp_copied"], 10)
                k2 = kcn.rearrange("p t (g d) -> p (t g) d", d=HD)
                sq = ar("a", 4096, 5 * P).rearrange("p (g d) -> p g d", d=HD)
                for n, lo, hi in ((P, 0, 8), (16, 8, 10)):
                    link(dve.tensor_tensor(sq[0:n, lo:hi], k2[0:n, lo:hi], k2[0:n, lo:hi], ALU.mult))
                    if lo == 0:
                        link(dve.memset(st[:, 0:10], 1.0))
                    link(dve.tensor_reduce(st[0:n, lo:hi], sq[0:n, lo:hi], AX.X, ALU.add))
                dve.tensor_scalar(st[:, 0:10], st[:, 0:10], 1.0 / HD, EPS, ALU.mult, ALU.add).then_inc(S["kcn_var"], 1)
                dve.wait_ge(S["kcn_std"], 1)
                link(dve.reciprocal(st[:, 0:10], st[:, 16:26]))
                for n, lo, hi in ((P, 0, 8), (16, 8, 10)):
                    link(dve.tensor_tensor(k2[0:n, lo:hi], k2[0:n, lo:hi], over(st[0:n, lo:hi], 2, HD), ALU.mult))
                    dve.tensor_tensor(k2[0:n, lo:hi], k2[0:n, lo:hi], over(M("kcgain")[0:n, :], 1, hi - lo), ALU.mult).then_inc(S["kcn_ready"], 1)

            for u in range(4 if stage >= 3 else 0):
                qt, g = u // 2, u % 2
                nk = P * (qt + 1)
                dve.wait_ge(S["p_scored"], u + 1)
                if u:
                    dve.wait_ge(S["pp_turned"], u)
                cs = st[:, 32:96].rearrange("p (r c) -> p r c", r=R)
                link(dve.scalar_tensor_tensor(out=cs, in0=ps[:, 4, 0:64].rearrange("p (r c) -> p r c", r=R), scalar=SCALE,
                                              in1=over(C("cmpmask")[:, 16 * qt:16 * qt + 16], 1, R), op0=ALU.mult, op1=ALU.add))
                link(dve.tensor_reduce(st[:, 8:12], cs, AX.X, ALU.max))
                link(dve.tensor_scalar(st[:, 8:12], st[:, 8:12], NEG / 10, None, ALU.max))
                dve.tensor_tensor(cs, cs, over(st[:, 8:12], 2, 16), ALU.subtract).then_inc(S["pc_shift"], 1)
                s8 = sc[:, 0:8 * nk].rearrange("p (i c) -> p i c", c=nk)
                scores = ps[:, 0:2 * (qt + 1), :].rearrange("p b c -> p (b c)").rearrange("p (i c) -> p i c", c=nk)
                mask = C("causal")[:, P - P * qt:2 * P]
                link(dve.scalar_tensor_tensor(out=s8, in0=scores, scalar=SCALE, in1=over(mask, 1, 8), op0=ALU.mult, op1=ALU.add))
                dve.tensor_reduce(st[:, 0:8], s8, AX.X, ALU.max, negate=True).then_inc(S["ps_max"], 1)
                dve.wait_ge(S["pc_exp"], u + 1)
                link(dve.tensor_reduce(st[:, 24:28], cs, AX.X, ALU.add))
                link(dve.tensor_scalar(st[:, 24:28], st[:, 24:28], 1e-30, None, ALU.max))
                dve.wait_ge(S["ps_exp"], u + 1)
                link(dve.reciprocal(st[:, 16:28], st[:, 16:28]))
                gates = sg[:, qt, 12 * g:12 * g + 12].rearrange("p (r b) -> p b r", b=3)
                dve.tensor_tensor(st[:, 24:28], st[:, 24:28], gates[:, 0, :], ALU.mult)
                link(dve.tensor_tensor(st[:, 16:24].rearrange("p (b r) -> p b r", b=2), st[:, 16:24].rearrange("p (b r) -> p b r", b=2),
                                       gates[:, 1:3, :], ALU.mult))
                dve.tensor_tensor(cs, cs, over(st[:, 24:28], 2, 16), ALU.mult)
                dve.tensor_tensor(s8, s8, over(st[:, 16:24], 2, nk), ALU.mult).then_inc(S["p_weights"], 1)
                dve.wait_ge(S["pp_turned"], u + 1)
                w = 1024 * (qt + 1)
                if u:
                    dve.wait_ge(S["po_mm"], u)
                dve.tensor_copy(pT[:, w // 2:w], ps[:, 0:4, :].rearrange("p b c -> p (b c)")[:, w // 2:w]).then_inc(S["pT_dve"], 1)
                dve.wait_ge(S["mg_exp"], 4 * u + 4)
                four = mg[:, 4 * u:4 * u + 4, :]
                link(dve.tensor_scalar(four, four, 1.0, None, ALU.add))
                dve.reciprocal(four, four).then_inc(S["mg_ready"], 1)

            if stage >= 4:
                dve.wait_ge(S["rep_mm"], 1)
                for s in range(2):
                    t24 = st[:, 32:56].rearrange("p (e b) -> p e b", b=3)
                    link(dve.tensor_tensor(t24, ps[:, 5, 24 * s:24 * s + 24].rearrange("p (e b) -> p e b", b=3),
                                           over(C("gsel"), 2, 3), ALU.mult))
                    dve.tensor_reduce(rg[:, 3 * s:3 * s + 3], t24.rearrange("p e b -> p b e"), AX.X, ALU.add).then_inc(S["rg_ready"], 1)
                    dve.wait_ge(S["rg_ready"], s + 1)
            for s in range(2 if stage >= 4 else 0):
                dve.wait_ge(S["k_scored"], 12 * (s + 1))
                if s:
                    dve.wait_ge(S["sp_turned"], s)
                    dve.wait_ge(S["so_mm"], s)
                cn, cg = sc[:, 1600:1663], sc[:, 1664:1727]
                link(dve.tensor_scalar(cn, ps[:, 3, 64:127], SCALE, None, ALU.mult))
                dve.tensor_reduce(st[:, 2:3], cn, AX.X, ALU.max, negate=True).then_inc(S["sc_max"], 1)
                nm = C("newmask")[:, NS * s:NS * s + NS]
                dve.scalar_tensor_tensor(out=sc[:, 1024:1056], in0=ps[:, 3, 0:32], scalar=SCALE, in1=nm, op0=ALU.mult, op1=ALU.add)
                dve.scalar_tensor_tensor(out=sc[:, 1568:1600], in0=ps[:, 3, 32:64], scalar=SCALE, in1=nm, op0=ALU.mult, op1=ALU.add)
                link(dve.tensor_scalar(sc[:, 1056:1568], ps[:, 2, :], SCALE, None, ALU.mult))
                link(dve.tensor_tensor(sc[:, 1056:1060], sc[:, 1056:1060], C("winmask"), ALU.add))
                link(dve.tensor_reduce(st[:, 1:2], sc[:, 1056:1600], AX.X, ALU.max, negate=True))
                dve.wait_ge(S["sc_exp"], s + 1)
                link(dve.reciprocal(st[:, 10:11], st[:, 10:11]))
                dve.tensor_scalar(cn, cn, st[:, 10:11], None, ALU.mult).then_inc(S["cn_ready"], 1)
                dve.wait_ge(S["cn_turned"], s + 1)
                g32, p4 = pT[0:63, 2048:2080], pT[0:63, 2080:2208]
                link(dve.tensor_reduce(g32, ps[0:63, 3, 128:256].rearrange("p (a r) -> p a r", r=R), AX.X, ALU.add))
                dve.tensor_copy(p4.rearrange("p (a r) -> p a r", r=R), over(g32, 2, R)).then_inc(S["p4_ready"], 1)
                dve.wait_ge(S["blk_mm"], s + 1)
                blk, eq = st[:, 32:49], st[:, 52:69]
                link(dve.tensor_tensor(blk, ps[:, 3, 256:273], C("forced"), ALU.add))
                link(dve.tensor_reduce(st[:, 12:13], blk, AX.X, ALU.min))
                link(dve.scalar_tensor_tensor(out=eq, in0=blk, scalar=st[:, 12:13], in1=C("jp1"), op0=ALU.is_equal, op1=ALU.mult))
                link(dve.tensor_reduce(st[:, 13:14], eq, AX.X, ALU.max))
                link(dve.tensor_scalar(eq, C("jp1"), st[:, 13:14], NEG, ALU.is_equal, ALU.mult))
                link(dve.scalar_tensor_tensor(out=sc[:, 0:1024].rearrange("p (j c) -> p j c", c=BLK),
                                              in0=ps[:, 0:2, :].rearrange("p b c -> p (b c)").rearrange("p (j c) -> p j c", c=BLK),
                                              scalar=SCALE, in1=over(eq[:, 0:16], 2, BLK), op0=ALU.mult, op1=ALU.add))
                dve.tensor_reduce(st[:, 0:1], sc[:, 0:1056], AX.X, ALU.max, negate=True).then_inc(S["ss_max"], 1)
                if s == 0:
                    for m in range(KC):
                        dve.wait_ge(S["slots_used"], W_YC + m // 2 + 1)
                        dve.tensor_tensor(hT[:, m, :], ps[:, 4 + m % 2, 0:NT], mg[:, m, :], ALU.mult).then_inc(S["yc_used"], 1)
                dve.wait_ge(S["ss_exp"], s + 1)
                link(dve.reciprocal(st[:, 8:10], st[:, 8:10]))
                link(dve.tensor_tensor(st[:, 8:10], st[:, 8:10], rg[:, 3 * s + 1:3 * s + 3], ALU.mult))
                dve.tensor_scalar(cg, cn, rg[:, 3 * s:3 * s + 1], None, ALU.mult)
                dve.tensor_scalar(sc[:, 0:1056], sc[:, 0:1056], st[:, 8:9], None, ALU.mult)
                dve.tensor_scalar(sc[:, 1056:1600], sc[:, 1056:1600], st[:, 9:10], None, ALU.mult).then_inc(S["s_weights"], 1)
                dve.wait_ge(S["sp_turned"], s + 1)
                dve.tensor_copy(pT[:, 1024:1536], ps[:, 2, :])
                dve.tensor_copy(pT[0:32, 1536:1792], ps[0:32, 3, 0:256])
                dve.tensor_copy(pT[0:63, 1792:1920], ps[0:63, 3, 256:384]).then_inc(S["spT_dve"], 1)
            if stage >= 4:
                for m in range(KC):
                    dve.wait_ge(S["slots_used"], W_YN + m // 2 + 1)
                    if m:
                        dve.wait_ge(S["merged"], m)
                    link(dve.tensor_tensor(mt, ps[:, 4 + m % 2, 0:NT], mg[:, 8 + m, :], ALU.mult))
                    dve.tensor_tensor(hT[:, m, :], hT[:, m, :], mt, ALU.add).then_inc(S["merged"], 1)
                for m in range(KC):
                    dve.wait_ge(S["slots_used"], W_O + m + 1)
                    dve.tensor_tensor(xT[:, m, :], xT[:, m, :], ps[:, 2 + m % 2, 0:NT], ALU.add).then_inc(S["x1_ready"], 1)
            if stage >= 5:
                dve.wait_ge(S["x_sumsq"], 2)
                normalize(M("norm_ffn"))
                dve.wait_ge(S["x_std"], 2)
                scaled(M("norm_ffn"))

                for t, (n0, n) in enumerate(TILES):
                    sp, cand, eq = (rt(x)[0:n, :] for x in ("sp", "cand", "eq"))
                    sp = sp[:, t * 2048:(t + 1) * 2048]
                    lv, li, lf, tv, ti, ab, abf, z8 = (rt(x)[0:n, :] for x in ("lv", "li", "lf", "tv", "ti", "ab", "abf", "z8"))
                    gi = rt("gi")[0:n, 3 * P * t:3 * P * (t + 1)]

                    def top16(groups, width, src, val, idx):
                        for half in range(2):
                            for i in range(groups):
                                last = dve.max(out=val[:, 16 * i + 8 * half:16 * i + 8 * half + 8], in_=src[:, i * width:(i + 1) * width])
                            link(last)
                            for i in range(groups):
                                last = dve.max_index(out=idx[:, 16 * i + 8 * half:16 * i + 8 * half + 8],
                                                     in_max=val[:, 16 * i + 8 * half:16 * i + 8 * half + 8], in_values=src[:, i * width:(i + 1) * width])
                            if half == 0:
                                for i in range(groups):
                                    last = dve.match_replace(out=src[:, i * width:(i + 1) * width], in_to_replace=val[:, 16 * i:16 * i + 8],
                                                             in_values=src[:, i * width:(i + 1) * width], imm_value=-3e38)
                            link(last)

                    dve.wait_ge(S["pk_copied"], t + 1)
                    top16(16, PK, sp, lv, li.bitcast(U32))
                    link(dve.tensor_copy(lf, li.bitcast(U32)))
                    l4 = lv.rearrange("p (h c k) -> p h c k", h=PH, c=2)
                    c4 = cand.rearrange("p (h a b) -> p h a b", h=PH, a=PTOP)
                    dve.wait_ge(S["pk_mm"], 3)
                    link(dve.tensor_tensor(c4, over(l4[:, :, 0, :], 3, PTOP), over(l4[:, :, 1, :], 2, PTOP), ALU.add))
                    top16(PH, 256, cand, tv, ti.bitcast(U32))
                    t3 = tv.rearrange("p (h k) -> p h k", h=PH)
                    link(dve.tensor_copy(z8[:, 0:8], t3[:, :, 0]))
                    dve.tensor_tensor(t3, t3, over(z8[:, 0:8], 2, PTOP), ALU.subtract).then_inc(S["top_shift"], 1)
                    u = ti.bitcast(U32)
                    dve.tensor_scalar(ab[:, 0:P].bitcast(U32), u, 4, None, ALU.logical_shift_right)
                    link(dve.tensor_scalar(ab[:, P:2 * P].bitcast(U32), u, 15, None, ALU.bitwise_and))
                    link(dve.tensor_copy(abf, ab.bitcast(U32)))
                    lf4 = lf.rearrange("p (h c k) -> p h c k", h=PH, c=2)
                    e4 = eq.rearrange("p (h k a) -> p h k a", h=PH, k=PTOP)
                    for c in range(2):
                        place = abf[:, c * P:(c + 1) * P].rearrange("p (h k) -> p h k", h=PH)
                        link(dve.tensor_tensor(eq.rearrange("p (k a) -> p k a", a=PTOP), over(abf[:, c * P:(c + 1) * P], 2, PTOP),
                                               over(C("iota16", n), 1, P), ALU.is_equal))
                        link(dve.tensor_tensor(e4, e4, over(lf4[:, :, c, :], 2, PTOP), ALU.mult))
                        link(dve.tensor_reduce(gi[:, (1 + c) * P:(2 + c) * P], eq.rearrange("p (k a) -> p k a", a=PTOP), AX.X, ALU.add))
                    dve.wait_ge(S["top_exp"], t + 1)
                    link(dve.tensor_reduce(z8[:, 0:8], t3, AX.X, ALU.add))
                    link(dve.reciprocal(z8[:, 8:16], z8[:, 0:8]))
                    dve.tensor_tensor(gi[:, 0:P].rearrange("p (h k) -> p h k", h=PH), t3, over(z8[:, 8:16], 2, PTOP), ALU.mult).then_inc(S["routed"], 1)
                dve.wait_ge(S["route_turned"], 1)
                last = dve.tensor_copy(sml[:, 0:3 * NT].rearrange("p (i n) -> p i n", i=3), ps[:, 5:8, 0:NT])
                last.then_inc(S["route_copied"], 1)
                dve.wait_ge(S["route_copied"], 1)
                gT, i1T, i2T = (sml[:, i * NT:(i + 1) * NT] for i in range(3))

                def one_hots(g, tok, half):
                    for x in range(GT):
                        n = tok + x
                        dve.tensor_scalar(oh[:, g, x, 0:P], C("iota"), i1T[:, bass.ds(n, 1)], None, ALU.is_equal)
                        last = dve.tensor_scalar(oh[:, g, x, P:P + HALF], C("iota")[:, HALF * half:HALF * half + HALF],
                                                 i2T[:, bass.ds(n, 1)], gT[:, bass.ds(n, 1)], ALU.is_equal, ALU.mult)
                    last.then_inc(S["oh_ready"], 1)

                def weigh(g, tok, half):
                    w = arena[:, HALF * half * NT:HALF * (half + 1) * NT].rearrange("p (j n) -> p n j", n=NT)[:, bass.ds(tok, GT), :]
                    dve.tensor_tensor(w, ps[:, 2 + g, 0:GT * HALF].rearrange("p (n j) -> p n j", n=GT), w, ALU.mult).then_inc(S["w_free"], 1)

                def route(it, it0, half):
                    for g in range(3):
                        dve.wait_ge(S["oh_used"], it * 3 + (48 * half + 3 * it0 + g + 1))
                        one_hots(g, it * 18 + (18 * it0 + GT * g), half)
                    for g in range(3):
                        dve.wait_ge(S["oh_used"], it * 3 + (48 * half + 3 * it0 + g + 4))
                        weigh(g, it * 18 + (18 * it0 + GT * g), half)

                def add_sums(q):
                    dve.wait_ge(S["slots_used"], W_V + 32 * (q + 1))
                    for m in range(4):
                        x = xT[:, 4 * (q % 2) + m, :]
                        last = dve.tensor_tensor(x, x, ps[:, VBANK[m], 0:NT], ALU.add)
                    last.then_inc(S["y_ready"], 1)

                dve.wait_ge(S["u_free"], 2 + HALF)
                with dve.Fori(0, 16) as it:
                    route(it, 0, 0)
                dve.wait_ge(S["u_free"], 2 + PK)
                for q in range(2):
                    with dve.Fori(0, 8) as it:
                        route(it, 8 * q, 1)
                    add_sums(q)
                for q in range(2, 4):
                    add_sums(q)

        @block.tensor
        def _(pe):
            def project(i, bank, rhs, n=KC, at=0):
                slot_ready(pe, i)
                for k in range(n):
                    last = pe.matmul(ps[:, bank, 0:NT], ring[:, i % RING, at + k * P:at + (k + 1) * P], rhs[:, k, :],
                                     start=(k == 0), stop=(k == n - 1))
                return last

            def sum_squares():
                for k in range(KC):
                    last = pe.matmul(ps[:, 0, 0:NT], C("ones"), xsq[:, k, :], start=(k == 0), stop=(k == KC - 1))
                last.then_inc(S["x_sumsq"], 1)

            pe.wait_ge(S["consts_in"], 16)
            pe.wait_ge(S["x_squared"], 1)
            sum_squares()
            pe.wait_ge(S["h_ready"], 1)
            for p, (c0, w) in enumerate(PIECES):
                if p == 2:
                    pe.wait_ge(S["tok_copied"], 3)
                for i in range(4):
                    slot_ready(pe, 4 * p + i)
                    for kk in range(2):
                        k = 2 * i + kk
                        for t, (n0, n) in enumerate(TILES):
                            last = pe.matmul(ps[0:n, 3 * (p % 2) + t, 0:w], hT[:, k, n0:n0 + n],
                                             ring[:, (4 * p + i) % RING, kk * w:(kk + 1) * w], start=(k == 0), stop=(k == KC - 1))
                    last.then_inc(S["slots_used"], 1)

            def conv_chunks(c):
                if c == 0:
                    pe.wait_ge(S["tok_copied"], 6)
                else:
                    pe.wait_ge(S["cc_copied"], c)
                project(W_CONV + 3 * c, 5, hT).then_inc(S["slots_used"], 1)
                if c:
                    pe.wait_ge(S["u_ready"], c)
                project(W_CONV + 3 * c + 1, 6, hT).then_inc(S["slots_used"], 1)
                if c:
                    pe.wait_ge(S["z_ready"], c)
                project(W_CONV + 3 * c + 2, 7, hT).then_inc(S["slots_used"], 1)

            for t, (n0, n) in enumerate(TILES):
                conv_chunks(t)
                pe.wait_ge(S["qk_ready"], t + 1)
                if t == 0:
                    pe.wait_ge(S["tok_copied"], 9)
                else:
                    pe.wait_ge(S["qT_copied"], t)
                for i, q in enumerate((qn, qr)):
                    for r in range(R):
                        pe.transpose(ps[:, i, r * P:r * P + n], q[0:n, r * P:(r + 1) * P], ident[0:n, 0:n])
                if t < 2:
                    for v, c in enumerate((C_KC, C_VC)):
                        pe.transpose(ps[:, 2, (2 + v) * P:(3 + v) * P], ptok[:, t, c:c + P], ident)
                pe.transpose(ps[:, 2, 0:n], qr[0:n, 512:640], ident[0:n, 0:n])
                pe.transpose(ps[:, 2, P:P + n], qr[0:n, 640:768], ident[0:n, 0:n]).then_inc(S["qk_turned"], 1)
            conv_chunks(3)

            if stage >= 2:
                pe.wait_ge(S["w1_in"], 16)
                pe.wait_ge(S["z_ready"], 4)
                for v in range(2):
                    for k in range(16):
                        last = pe.matmul(ps[:, 7, v:v + 1], w1[:, v, k, :], M("pos")[:, 16 * v + k:16 * v + k + 1], start=(k == 0), stop=(k == 15))
                last.then_inc(S["cbias_mm"], 1)
                pe.wait_ge(S["qT_copied"], 3)

            def comp_out(u):
                t, v = u // 2, u % 2
                n = P if t < 4 else 16
                pe.wait_ge(S["hid_ready"], u + 1)
                if u:
                    pe.wait_ge(S["cmp_copied"], u)
                w2 = M("w2")[:, v * HD:(v + 1) * HD]
                if v == 0 or t == 4:
                    for g in range(NG):
                        last = pe.matmul(ps[0:n, 5, g * HD:(g + 1) * HD], hid[:, g * n:(g + 1) * n], w2, start=True, stop=True)
                else:
                    for b in range(2):
                        for g in range(NG):
                            last = pe.matmul(ps[0:64, 5, b * P + g * HD:b * P + (g + 1) * HD], hid[:, g * P + b * 64:g * P + b * 64 + 64], w2,
                                             start=True, stop=True)
                last.then_inc(S["comp_out"], 1)

            for u in range(10 if stage >= 2 else 0):
                t, v = u // 2, u % 2
                n = P if t < 4 else 16
                if t < 4:
                    pe.wait_ge(S[f"xc_in{u % 3}"], 256 * (u // 3 + 1))
                if u:
                    pe.wait_ge(S["hid_sum"], u)
                for half in range(2):
                    for k in range(8):
                        if t < 4:
                            src = xc[:, u % 3, :, k, :, :].rearrange("p j g c -> p g j c")
                            dst = ps[:, 4, 256 * half:256 * half + 256].rearrange("p (g j c) -> p g j c", g=NG, j=16)
                        else:
                            src, dst = xcp[:, v, k, :, :], ps[:, 4, 256 * half:256 * half + 32].rearrange("p (g c) -> p g c", g=NG)
                        last = pe.matmul(dst, w1[:, v, 8 * half + k, :], src, start=(k == 0), stop=(k == 7))
                last.then_inc(S["comp_mm"], 1)
                if u:
                    comp_out(u - 1)
            if stage >= 2:
                comp_out(9)
                for t in range(5):
                    n = P if t < 4 else 16
                    pe.wait_ge(S["kcn_ready"], 1 if t < 4 else 2)
                    if t >= 2:
                        pe.wait_ge(S["kcT_copied"], t - 1)
                    pe.transpose(ps[:, 6 + t % 2, 0:n], kcn[0:n, t, :], ident[0:n, 0:n]).then_inc(S["kcn_turned"], 1)
                pe.wait_ge(S["kcT_copied"], 5)

            if stage >= 3:
                pe.wait_ge(S["vnew_ready"], 3)
            for u in range(4 if stage >= 3 else 0):
                qt, g = u // 2, u % 2
                nk = P * (qt + 1)
                lane, n0 = slice(64 * g, 64 * g + 64), qt * P
                if u:
                    pe.wait_ge(S["pT_act"], u)
                    pe.wait_ge(S["pT_dve"], u)
                flat = ps[:, 0:4, :].rearrange("p b c -> p (b c)")
                for r in range(R):
                    pe.matmul(ps[:, 4, 16 * r:16 * r + 16], qnT[lane, r, n0:n0 + P], kcT[lane, 4 * P:4 * P + 16], start=True, stop=True)
                    for br, keys in enumerate((ksT, kwT)):
                        i = 4 * br + r
                        last = pe.matmul(flat[:, i * nk:(i + 1) * nk], qrT[lane, r, n0:n0 + P], keys[lane, 0:nk], start=True, stop=True)
                last.then_inc(S["p_scored"], 1)
                for i in range(4 * u, 4 * u + 4):
                    if i >= 2:
                        pe.wait_ge(S["mg_exp"], i - 1)
                    project(W_MG + i, 6 + i % 2, hT).then_inc(S["slots_used"], 1)
                pe.wait_ge(S["p_weights"], u + 1)
                for i in range(8):
                    for kt in range(qt + 1):
                        x = i * (qt + 1) + kt
                        pe.transpose(flat[:, x * P:(x + 1) * P], sc[:, x * P:(x + 1) * P], ident)
                for r in range(R):
                    last = pe.transpose(ps[0:16, 4, r * P:(r + 1) * P], st[:, 32 + 16 * r:48 + 16 * r], ident)
                last.then_inc(S["pp_turned"], 1)
                pe.wait_ge(S["pT_act"], u + 1)
                pe.wait_ge(S["pT_dve"], u + 1)
                if u:
                    pe.wait_ge(S["po_copied"], u)
                for r in range(R):
                    o = ps[:, 5, r * P:(r + 1) * P]
                    pe.matmul(o, vc[0:16, 8, :], pT[0:16, 2048 + r * P:2048 + (r + 1) * P], start=True, stop=False)
                    for br in range(2):
                        for kt in range(qt + 1):
                            x = (4 * br + r) * (qt + 1) + kt
                            last = pe.matmul(o, vnew[:, kt, br * P:(br + 1) * P], pT[:, x * P:(x + 1) * P], start=False,
                                             stop=(br == 1 and kt == qt))
                last.then_inc(S["po_mm"], 1)

            if stage >= 4:
                pe.wait_ge(S["gate_ready"], 3)
                pe.wait_ge(S["po_copied"], 4)
                for s in range(2):
                    last = pe.matmul(ps[:, 5, 24 * s:24 * s + 24], C("rep")[0:NS, s * P:(s + 1) * P], sg[0:NS, 2, :], start=True, stop=True)
                last.then_inc(S["rep_mm"], 1)
            for s in range(2 if stage >= 4 else 0):
                if s:
                    pe.wait_ge(S["spT_act"], s)
                    pe.wait_ge(S["spT_dve"], s)
                    pe.wait_ge(S["so_copied"], s)
                for b4 in range(SETB):
                    b = SETB * s + b4
                    rows = slice(32 * b4, 32 * b4 + 32)
                    pe.matmul(ps[rows, 3, 0:NS], qbr[:, b, :], ksT[:, SEQ:NT], start=True, stop=True)
                    pe.matmul(ps[rows, 3, NS:2 * NS], qbr[:, b, :], kwT[:, SEQ:NT], start=True, stop=True)
                    pe.matmul(ps[rows, 3, 64:128], qbn[:, b, :], kcT[:, 64 * b:64 * b + 64], start=True, stop=True)
                    for h in range(3):
                        pe.wait_ge(S[f"k_in{h}"], (64 if h < 2 else 16) * (b + 1))
                        pe.matmul(ps[rows, h, :], qbr[:, b, :], kring[:, h, :], start=True, stop=True).then_inc(S["k_scored"], 1)
                pe.wait_ge(S["cn_ready"], s + 1)
                pe.transpose(ps[0:63, 3, 128:256], sc[:, 1600:1663], ident).then_inc(S["cn_turned"], 1)
                pe.wait_ge(S["p4_ready"], s + 1)
                pe.matmul(ps[:, 3, 256:256 + NSEL], pT[0:63, 2080:2208], C("ov")[0:63, :], start=True, stop=True).then_inc(S["blk_mm"], 1)
                if s == 0:
                    pe.wait_ge(S["rg_ready"], 2)
                    for m in range(KC):
                        if m >= 2:
                            pe.wait_ge(S["yc_used"], m - 1)
                        last = project(W_YC + m // 2, 4 + m % 2, zT, 4, (m % 2) * 512)
                        if m % 2:
                            last.then_inc(S["slots_used"], 1)
                pe.wait_ge(S["s_weights"], s + 1)
                for i in range(12):
                    c0 = i * P if i < 8 else 1056 + (i - 8) * P
                    pe.transpose(ps[:, i // 4, (i % 4) * P:(i % 4 + 1) * P], sc[:, c0:c0 + P], ident)
                pe.transpose(ps[0:32, 3, 0:P], sc[:, 1024:1056], ident)
                pe.transpose(ps[0:32, 3, P:2 * P], sc[:, 1568:1600], ident)
                pe.transpose(ps[0:63, 3, 2 * P:3 * P], sc[:, 1664:1727], ident).then_inc(S["sp_turned"], 1)
                pe.wait_ge(S["spT_act"], s + 1)
                pe.wait_ge(S["spT_dve"], s + 1)
                pe.wait_ge(S[f"v_in{s}"], 16 * 9 * SETB)
                o = ps[:, 7, 0:P]
                pe.matmul(o, vnew[0:NS, 2, 0:P], pT[0:NS, 1536:1664], start=True, stop=False, skip_group_check=True)
                pe.matmul(o, vnew[0:NS, 2, P:2 * P], pT[0:NS, 1664:1792], start=False, stop=False, skip_group_check=True)
                for b4 in range(SETB):
                    b = SETB * s + b4
                    o = ps[:, 7, 32 * b4:32 * b4 + 32]
                    pe.matmul(o, vc[0:63, b, :], pT[0:63, 1792 + 32 * b4:1824 + 32 * b4], start=False, stop=False, skip_group_check=True)
                    for i in range(12):
                        v0 = (8 * b4 + i) * P if i < 8 else 4096 + (4 * b4 + i - 8) * P
                        last = pe.matmul(o, vset[s][:, v0:v0 + P], pT[:, i * P + 32 * b4:i * P + 32 * b4 + 32], start=False,
                                         stop=(b4 == 3 and i == 11), skip_group_check=True)
                last.then_inc(S["so_mm"], 1)

            if stage >= 4:
                pe.wait_ge(S["so_copied"], 2)
                pe.wait_ge(S["yc_used"], KC)
                for m in range(KC):
                    if m >= 2:
                        pe.wait_ge(S["merged"], m - 1)
                    last = project(W_YN + m // 2, 4 + m % 2, oT, 4, (m % 2) * 512)
                    if m % 2:
                        last.then_inc(S["slots_used"], 1)
                pe.wait_ge(S["merged"], KC)
                for m in range(KC):
                    if m >= 2:
                        pe.wait_ge(S["x1_ready"], m - 1)
                    project(W_O + m, 2 + m % 2, hT).then_inc(S["slots_used"], 1)
            if stage >= 5:
                pe.wait_ge(S["x_squared"], 2)
                sum_squares()
                pe.wait_ge(S["h_ready"], 2)
                for i in range(16):
                    if i >= 2:
                        pe.wait_ge(S["qq_copied"], i - 1)
                    project(W_Q + i, i % 2, hT).then_inc(S["slots_used"], 1)
                pe.wait_ge(S["qq_copied"], 16)
                pe.wait_ge(S["sub_in"], 16)
                for t, (n0, n) in enumerate(TILES):
                    if t:
                        pe.wait_ge(S["pk_copied"], t)
                    for i in range(16):
                        last = pe.matmul(ps[0:n, 4 + i // 4, (i % 4) * P:(i % 4 + 1) * P], rt("qq")[:, i * NT + n0:i * NT + n0 + n],
                                         rt("sub")[:, i * P:(i + 1) * P], start=True, stop=True)
                    last.then_inc(S["pk_mm"], 1)

                def expert_tile(it, j0, s):
                    pe.wait_ge(ring_in[s], it * 16 + 16 * ((W_U + j0) // RING + 1))
                    pe.wait_ge(S["u_free"], it * RING + (j0 + s + 1))
                    for k in range(KC):
                        last = pe.matmul(ps[:, s % 2, 0:NT], ring[:, s, k * P:(k + 1) * P], hT[:, k, :], start=(k == 0), stop=(k == KC - 1))
                    last.then_inc(S["slots_used"], 1)

                def routing(it, it0, half, g):
                    pe.wait_ge(S["oh_ready"], it * 3 + (48 * half + 3 * it0 + g + 1))
                    pe.wait_ge(S["w_free"], it * 3 + (48 * half + 3 * it0 + g + 1))
                    for x in range(GT):
                        last = pe.matmul(ps[:, 2 + g, x * HALF:(x + 1) * HALF], oh[:, g, x, 0:P], oh[:, g, x, P:P + HALF], start=True, stop=True)
                    last.then_inc(S["oh_used"], 1)

                with pe.Fori(0, HALF // RING) as it:
                    for s in range(RING):
                        expert_tile(it, 0, s)
                pe.wait_ge(S["routed"], 3)
                for t, (n0, n) in enumerate(TILES):
                    for i in range(3):
                        last = pe.transpose(ps[:, 5 + i, n0:n0 + n], rt("gi")[0:n, (3 * t + i) * P:(3 * t + i + 1) * P], ident[0:n, 0:n])
                last.then_inc(S["route_turned"], 1)
                with pe.Fori(0, HALF // RING) as it:
                    expert_tile(it, HALF, 0)
                    expert_tile(it, HALF, 1)
                    routing(it, 0, 0, 0)
                    expert_tile(it, HALF, 2)
                    routing(it, 0, 0, 1)
                    expert_tile(it, HALF, 3)
                    routing(it, 0, 0, 2)
                pe.wait_ge(S["u_free"], 2 + PK)
                for q in range(4):
                    half = q // 2
                    if q:
                        pe.wait_ge(S["y_ready"], q)
                    if q % 2 == 0:
                        pe.wait_ge(S["w_free"], 3 + 48 * (half + 1))
                    for m in range(4):
                        pe.matmul(ps[:, VBANK[m], 0:NT], zero16[:, 0:P], zero16[:, :], start=True, stop=False, skip_group_check=True)
                    with pe.Fori(0, 8) as it:
                        for s in range(RING):
                            pe.wait_ge(ring_in[s], it * 16 + 16 * ((W_V + 32 * q) // RING + 1))
                            for jj in range(2):
                                w = arena[:, bass.ds((it * 8 + (HALF * half + 2 * s + jj)) * NT, NT)]
                                for m in range(4):
                                    last = pe.matmul(ps[:, VBANK[m], 0:NT], ring[:, s, (4 * jj + m) * P:(4 * jj + m + 1) * P], w,
                                                     start=False, stop=False, skip_group_check=True)
                            last.then_inc(S["slots_used"], 1)
                            if q < 2 and s >= 1:
                                routing(it, 8 * q, 1, s - 1)


def constants():
    f = np.float32
    c = np.zeros((P, NCONST), f)

    def put(name, x):
        a, b = CONST[name]
        c[:x.shape[0], a:b] = x

    pos = np.concatenate([np.arange(SEQ), np.tile(PAST + np.arange(NQ), NB)]).astype(f)
    inv = np.power(f(10000.0), -np.arange(HD // 2, dtype=f) * f(2.0) / f(HD)).astype(f)
    ang = (pos[:, None] * inv[None, :]).astype(f)
    cos, sin = np.cos(ang).astype(f), np.sin(ang).astype(f)
    cc, ss = np.zeros((P, 3 * HD), f), np.zeros((P, 3 * HD), f)
    for t, (n0, n) in enumerate(TILES):
        cc[:n, t * HD:(t + 1) * HD] = np.concatenate([cos[n0:n0 + n]] * 2, 1)
        ss[:n, t * HD:(t + 1) * HD] = np.concatenate([-sin[n0:n0 + n], sin[n0:n0 + n]], 1)
    put("ident", np.eye(P, dtype=f))
    put("iota", np.tile(np.arange(P, dtype=f), (P, 1)))
    put("ones", np.ones((P, P), f))
    put("cos", cc)
    put("sin", ss)
    row = np.arange(P)
    tri = np.where(row[None, :] <= row[:, None], 0, NEG).astype(f)
    put("causal", np.concatenate([np.zeros((P, P), f), tri], 1))
    end = np.arange(16) * STRIDE + 2 * STRIDE - 1
    ok = (end[None, None, :] <= (row[:, None] + P * np.arange(2)[None, :])[:, :, None]) & (np.arange(16) < 15)
    put("cmpmask", np.where(ok, 0, NEG).astype(f).reshape(P, 32))
    rb, rq = row // 32, row % 16 // R
    nm = np.full((P, 2, NB, NQ), NEG, f)
    for s in range(2):
        for p in range(P):
            nm[p, s, SETB * s + rb[p], :rq[p] + 1] = 0
    put("newmask", nm.reshape(P, 2 * NS))
    put("winmask", np.where(np.arange(NQ)[None, :] > rq[:, None], 0, NEG).astype(f))
    c0, s0 = np.arange(63)[:, None] * STRIDE, np.arange(NSEL)[None, :] * BLK
    put("ov", (np.clip(np.minimum(c0 + 2 * STRIDE, s0 + BLK) - np.maximum(c0, s0), 0, None) / STRIDE).astype(f))
    forced = np.zeros(NSEL, f)
    forced[[0, NSEL - 2, NSEL - 1]] = 1e4
    put("forced", np.tile(forced, (P, 1)))
    put("jp1", np.tile(np.arange(1, NSEL + 1, dtype=f), (P, 1)))
    rep = np.zeros((NS, 2, P), f)
    for s in range(2):
        rep[(SETB * s + rb) * NQ + rq, s, row] = 1
    put("rep", rep.reshape(NS, 2 * P))
    put("gsel", (np.arange(NH)[None, :] == (row % 32 // 16 * R + row % R)[:, None]).astype(f))
    put("iota16", np.tile(np.arange(PTOP, dtype=f), (P, 1)))
    return c


def kernel(x_prompt, x_sample, cache_cmp_k, cache_cmp_v, cache_slc_k, cache_slc_v, cache_win_k, cache_win_v, state_conv,
           page_table, norm_mix, w_in, conv_w, cmp_pos_k, cmp_w1_k, cmp_b1_k, cmp_w2_k, cmp_pos_v, cmp_w1_v, cmp_b1_v,
           cmp_w2_v, q_norm, k_norm_cmp, k_norm_slc, k_norm_win, w_out_conv, w_out_nsa, w_o, norm_ffn, peer_wq,
           peer_sub_keys, peer_u, peer_v):
    import concourse.bacc as _bacc
    from concourse.bass_utils import run_bass_kernel_spmd as _run

    a = np.asarray
    x = np.concatenate([a(x_prompt)[0], a(x_sample).reshape(NS, D)], 0)
    w = a(w_in)[0]
    cut = np.cumsum([0, 512, 512, 512, 512, P, P, P, P, P, P, 24, 2048])
    cb, cc, ch, q, kc, vc, ks, vs, kw, vw, ng, mg = (w[:, cut[i]:cut[i + 1]] for i in range(12))
    q = q.reshape(D, NG, R, HD).transpose(0, 2, 1, 3).reshape(D, 512)
    tok = np.concatenate([q, ks, kw, kc, vc, vs, vw, ng], 1)

    def chunks(m):
        k, n = m.shape
        return m.reshape(k // P, P, n // P, P).transpose(2, 1, 0, 3).reshape(n // P, P, k // P * P)

    feed = {"xT": x.T.reshape(KC, P, NT).transpose(1, 0, 2), "consts": constants()}
    for p, (c0, n) in enumerate(PIECES):
        feed[f"wtok{p}"] = tok[:, c0:c0 + n].reshape(4, 2, P, n).transpose(0, 2, 1, 3).reshape(4, P, 2 * n)
    conv = np.stack([cc.reshape(D, 4, P), ch.reshape(D, 4, P), cb.reshape(D, 4, P)], 2).reshape(D, 12 * P)
    feed["wT"] = np.concatenate([chunks(conv), chunks(mg)], 0)
    pair = lambda m: chunks(m).reshape(4, 2, P, 512).transpose(0, 2, 1, 3).reshape(4, P, 1024)
    nsa = a(w_out_nsa)[0].reshape(NG, R, HD, D).transpose(1, 0, 2, 3).reshape(512, D)
    feed["wout"] = np.concatenate([pair(a(w_out_conv)[0]), pair(nsa), chunks(a(w_o)[0]), chunks(a(peer_wq)[0])], 0)
    w1 = np.stack([a(cmp_w1_k)[0], a(cmp_w1_v)[0]])
    feed["w1"] = w1.reshape(2, 16, 2 * HD, P).transpose(2, 0, 1, 3).reshape(P, 4096)
    pos = np.stack([a(cmp_pos_k)[0], a(cmp_pos_v)[0]])
    state = a(state_conv)[0].reshape(NB, 2, 4, P).transpose(3, 2, 0, 1).reshape(P, 4 * NB * 2)
    gain = np.concatenate([np.tile(a(q_norm)[0], 8), np.tile(a(k_norm_slc)[0], 2), np.tile(a(k_norm_win)[0], 2)])
    feed["smalls"] = np.concatenate([
        a(norm_mix)[0].reshape(KC, P).T, a(norm_ffn)[0].reshape(KC, P).T,
        a(conv_w)[0].reshape(3, 4, P).transpose(2, 0, 1).reshape(P, 12), np.stack([a(cmp_b1_k)[0], a(cmp_b1_v)[0]], 1),
        pos.reshape(2, 16, 2 * HD).transpose(2, 0, 1).reshape(P, 32), state, np.tile(gain, (P, 1)),
        np.tile(a(k_norm_cmp)[0], (P, 1)), a(cmp_w2_k)[0], a(cmp_w2_v)[0]], 1)
    assert feed["smalls"].shape == (P, NSMALL)
    pt = a(page_table)
    feed["pages"] = pt.reshape(1, 64)
    for n, c in (("cmp_k", cache_cmp_k), ("cmp_v", cache_cmp_v)):
        feed["cache_" + n] = a(c).reshape(NPOOL, 8, 8, 2, NG, HD).transpose(0, 3, 5, 2, 4, 1).reshape(NPOOL, P, P)
    feed["cache_slc_k"] = a(cache_slc_k).reshape(NPOOL, PAGE, P).transpose(0, 2, 1)
    feed["cache_slc_v"] = a(cache_slc_v).reshape(NPOOL, PAGE, P)
    feed["cache_win_kT"] = a(cache_win_k).reshape(NB, WINDOW, P).transpose(0, 2, 1)
    for n, c in (("win_k", cache_win_k), ("win_v", cache_win_v)):
        feed["cache_" + n] = a(c).reshape(NB, WINDOW, P)
    feed["sub"] = a(peer_sub_keys)[0].reshape(16, P, P).transpose(2, 0, 1).reshape(P, 2048)
    feed["uT"] = a(peer_u)[0].reshape(PK, PK, KC, P).transpose(1, 3, 2, 0).reshape(PK, P, D)
    feed["v"] = a(peer_v)[0].reshape(PK, 2, 32, 2, 2, 512).transpose(1, 4, 2, 0, 3, 5).reshape(PK, P, 1024)

    nc = _bacc.Bacc("TRN2", target_bir_lowering=False, num_devices=1)
    arrays, A, O = {}, {}, {}
    for name, v in feed.items():
        v = np.ascontiguousarray(v)
        arrays["in_" + name] = v
        A[name] = nc.dram_tensor("in_" + name, v.shape, mybir.dt.from_np(v.dtype), kind="ExternalInput").ap()
    shapes = {"yT": (P, KC, NT), "kc": (NT, P), "vc": (NT, P), "ks": (NT, P), "vs": (NT, P), "kw": (SEQ, P), "vw": (SEQ, P),
              "wk": (NB, WINDOW, P), "wv": (NB, WINDOW, P), "cstate": (P, 4 * 18)}
    for name, shape in shapes.items():
        O[name] = nc.dram_tensor("out_" + name, shape, F32, kind="ExternalOutput").ap()
    program(nc, A, O, STAGE)
    r = _run(nc, [arrays], core_ids=[0]).results[0]
    got = {name: a(r["out_" + name]) for name in shapes}
    y = got["yT"].transpose(1, 0, 2).reshape(D, NT).T
    cs = got["cstate"].reshape(P, 4, 18).transpose(2, 1, 0).reshape(18, 512)
    new = lambda n: got[n][SEQ:].reshape(1, NB, NQ, NG, HD)
    old = lambda n: got[n][:SEQ].reshape(1, 1, SEQ, NG, HD)
    win = lambda n: got[n].reshape(1, NB, WINDOW, NG, HD)
    return tuple(np.ascontiguousarray(v) for v in (
        y[:SEQ].reshape(1, SEQ, D), y[SEQ:].reshape(NB, NQ, D),
        old("kc"), old("vc"), old("ks"), old("vs"), old("kw"), old("vw"), cs[:2].reshape(1, 1, 2, 512),
        new("kc"), new("vc"), new("ks"), new("vs"), win("wk"), win("wv"), cs[2:].reshape(1, NB, 2, 512)))
```

```python
from contextlib import ExitStack

import numpy as np

import concourse.bass as bass
from concourse import mybir

D = 1024
SEQ = 256
NB = 8
NQ = 4
PAST = 1024
PAGE = 128
NPOOL = 80
NH, NG, R = 8, 2, 4
HD = 64
STRIDE = 16
WINDOW = 512
BLK = 64
NSEL = 17
PH, PK, PTOP = 8, 128, 16
EPS = 1e-6
NEG = -1e30
P = 128
NS = NB * NQ
NT = SEQ + NS
KC = D // P
TILES = [(0, P), (P, P), (2 * P, NS)]
QKV = 12 * HD + 4 * NG * HD + 3 * NH
PIECES = [(0, 512), (512, 512), (1024, QKV - 1024)]
PAGES = PAST // PAGE
SETB = 4
SCALE = HD ** -0.5
RING = 4
HALF = PK // 2
GT = 9
VBANK = (4, 5, 6, 7)

F32 = mybir.dt.float32
F32R = mybir.dt.float32r
BF16 = mybir.dt.bfloat16
I32 = mybir.dt.int32
U32 = mybir.dt.uint32
ALU = mybir.AluOpType
ACT = mybir.ActivationFunctionType
AX = mybir.AxisListType

C_KC, C_VC, C_VS, C_NG = 768, 896, 1024, 1280

W_TOK, W_CONV, W_MG, W_YC, W_YN, W_O, W_Q, W_U, W_V, W_END = 0, 12, 24, 40, 44, 48, 56, 72, 200, 328


def columns(parts):
    at, out = 0, {}
    for name, n in parts:
        out[name] = (at, at + n)
        at += n
    return out, at


CONST, NCONST = columns([("iota", P), ("ident", P), ("ones", P), ("cos", 3 * HD), ("sin", 3 * HD), ("causal", 2 * P),
                         ("cmpmask", 32), ("newmask", 2 * NS), ("winmask", NQ), ("ov", NSEL), ("forced", NSEL),
                         ("jp1", NSEL), ("rep", 2 * P), ("gsel", NH), ("iota16", PTOP)])
SMALL, NSMALL = columns([("norm_mix", KC), ("norm_ffn", KC), ("conv_w", 12), ("b1", 2), ("pos", 32),
                         ("state", 4 * NB * 2), ("gain", 12 * HD), ("kcgain", HD), ("w2", 2 * HD)])

ARENA = PK * NT
AR, USED = columns([("a", 10752), ("b", 6984), ("qnT", 1024), ("qrT", 1024), ("qbn", 256), ("qbr", 256), ("ksT", NT),
                    ("kwT", NT), ("z", 4 * NT), ("oT", 4 * NT), ("up", 4 * 258), ("us", 4 * NB * 6), ("vnew", 768),
                    ("kcT", 4 * P + 16), ("vc", 9 * P), ("sec", 256), ("hid", 256), ("kcn", 5 * P),
                    ("vset", 6144), ("kring", 1536), ("xcp", 512), ("rr", 2 * NT)])
assert USED <= ARENA, (USED, ARENA)
UP0 = HALF * NT
RT, USED = columns([("qq", 16 * NT), ("sub", 2048), ("sp", 3 * 2048), ("lv", 256), ("li", 256), ("lf", 256),
                    ("tv", 128), ("ti", 128), ("ab", 256), ("abf", 256), ("gi", 9 * P), ("z8", 16), ("rr", 2 * NT)])
RT["cand"], RT["eq"] = (0, 2048), (2048, 4096)
assert USED <= HALF * NT, USED
STATS = NCONST + NSMALL
LISTS, HOT = P, P + 3 * NT
AUX = max(STATS + 96 + 9 * NH + 8, HOT + GT * (P + HALF))


def staged(i):
    return 2 * (i - W_Q)


def program(nc, A, O):
    with ExitStack() as ctx:
        def sb(name, shape, dt=F32):
            return ctx.enter_context(nc.sbuf_tensor(name, shape, dt))

        def sem(name):
            return ctx.enter_context(nc.semaphore(name))

        ps = ctx.enter_context(nc.psum_tensor("ps", [P, 8, 512], F32))
        aux = sb("aux", [P, AUX])
        cst, sml = aux[:, 0:NCONST], aux[:, NCONST:STATS]
        ring = sb("ring", [P, RING, 1024])
        xT = sb("xT", [P, KC, NT])
        mov_hi, mov_lo = sb("mov_hi", [P, KC, NT], F32R), sb("mov_lo", [P, KC, NT], F32R)
        w_hi, w_lo = sb("w_hi", [P, 2, 512], F32R), sb("w_lo", [P, 2, 512], F32R)
        ptab = sb("ptab", [1, 64], I32)
        oh = aux[:, HOT:HOT + GT * (P + HALF)].rearrange("p (x c) -> p x c", x=GT)
        zero16 = sb("zero16", [P, NT], BF16)
        arena = sb("arena", [P, ARENA])
        st = aux[:, STATS:STATS + 96]
        sg = aux[:, STATS + 96:STATS + 96 + 9 * NH].rearrange("p (t c) -> p t c", t=3)
        rg = aux[:, STATS + 96 + 9 * NH:STATS + 102 + 9 * NH]
        bias = aux[:, STATS + 102 + 9 * NH:STATS + 104 + 9 * NH]

        def C(name, n=P):
            a, b = CONST[name]
            return cst[0:n, a:b]

        def M(name):
            a, b = SMALL[name]
            return sml[:, a:b]

        def ar(name, lo=0, n=None):
            a, b = AR[name]
            return arena[:, a + lo:(b if n is None else a + lo + n)]

        def rt(name):
            a, b = RT[name]
            return arena[:, UP0 + a:UP0 + b]

        def over(x, axis, n):
            y = x.unsqueeze(axis)
            shape = list(y.shape)
            shape[axis] = n
            return y.broadcast_to(shape)

        ident = C("ident")
        rr = ar("rr").rearrange("p (i n) -> p i n", i=2)
        rr2 = rt("rr").rearrange("p (i n) -> p i n", i=2)
        h2 = arena[:, 0:KC * NT].rearrange("p (k n) -> p k n", k=KC)
        ptok = ar("b", 0, 3 * QKV).rearrange("p (t c) -> p t c", t=3)
        qn = ar("b", 3 * QKV, 768)
        qr = ar("b", 3 * QKV + 768, 768)
        tmpq = ar("b", 3 * QKV + 1536, 768)
        xsq = ar("b", 0, KC * NT).rearrange("p (k n) -> p k n", k=KC)
        mg = ar("b", 0, 16 * NT).rearrange("p (k n) -> p k n", k=16)
        mt = ar("b", 16 * NT, NT)
        w1 = ar("a", 0, 4096).rearrange("p (v k f) -> p v k f", v=2, k=16)
        xc = ar("a", 4096, 6144).rearrange("p (i j k g c) -> p i j k g c", i=3, j=16, k=8, g=NG)
        xcp = ar("xcp").rearrange("p (v k g c) -> p v k g c", v=2, k=8, g=NG)
        sc = ar("a", 0, 2048)
        pT = ar("a", 2048, 2560)
        vset = [ar("vset"), ar("a", 4608, 6144)]
        qnT = ar("qnT").rearrange("p (r n) -> p r n", r=R)
        qrT = ar("qrT").rearrange("p (r n) -> p r n", r=R)
        qbn = ar("qbn").rearrange("p (b m) -> p b m", b=NB)
        qbr = ar("qbr").rearrange("p (b m) -> p b m", b=NB)
        ksT, kwT = ar("ksT"), ar("kwT")
        zT = ar("z").rearrange("p (k n) -> p k n", k=4)
        oT = ar("oT").rearrange("p (r n) -> p r n", r=R)
        up = ar("up").rearrange("p (k n) -> p k n", k=4)
        us = ar("us").rearrange("p (k b n) -> p k b n", k=4, b=NB)
        vnew = ar("vnew").rearrange("p (t c) -> p t c", t=3)
        kcT = ar("kcT")
        vc = ar("vc").rearrange("p (b c) -> p b c", c=P)
        sec, hid = ar("sec"), ar("hid")
        kcn = ar("kcn").rearrange("p (t c) -> p t c", c=P)
        kring = ar("kring").rearrange("p (s c) -> p s c", s=3)

        class Sems(dict):
            def __missing__(self, name):
                self[name] = sem(name)
                return self[name]

        S = Sems()
        ring_in = [sem(f"ring_in{i}") for i in range(RING)]

        def link_on(eng, s):
            count = [0]

            def link(ins):
                count[0] += 1
                ins.then_inc(s, 1)
                eng.wait_ge(s, count[0])
            return link

        kbuf = [kring, ar("qnT", 0, 1536).rearrange("p (s c) -> p s c", s=3),
                xT[:, :, :].rearrange("p k n -> p (k n)")[:, 0:1536].rearrange("p (s c) -> p s c", s=3)]

        def load_chunks(eng, u):
            t, v = u // 2, u % 2
            if u >= 3:
                eng.wait_ge(S["comp_mm"], u - 2)
            for j in range(16):
                page = eng.value_load(ptab[0:1, 16 * t + j:16 * t + j + 1], min_val=0, max_val=NPOOL - 1)
                eng.dma_start(xc[:, u % 3, j, :, :, :].rearrange("p k g c -> p (k g c)"),
                              A["cache_cmp_" + "kv"[v]][bass.ds(page, 1)].rearrange("o p c -> (o p) c")).then_inc(S[f"xc_in{u % 6}"], 16)

        def load_keys(eng, b, h):
            if b >= 3:
                eng.wait_ge(S["k_scored"], 3 * (b - 3) + h + 1)
            elif b == 1:
                eng.wait_ge(S["p_scored"], 4)
            elif b == 2:
                eng.wait_ge(S["slots_used"], W_YC)
            if h == 2:
                eng.dma_start(kbuf[b % 3][:, 2, :], A["cache_win_kT"][b]).then_inc(S[f"k_in{b % 3}_2"], 16)
                return
            for p in range(4):
                at = b * PAGES + 4 * h + p
                page = eng.value_load(ptab[0:1, at:at + 1], min_val=0, max_val=NPOOL - 1)
                eng.dma_start(kbuf[b % 3][:, h, p * P:(p + 1) * P], A["cache_slc_k"][bass.ds(page, 1)].rearrange("o p c -> (o p) c"))\
                    .then_inc(S[f"k_in{b % 3}_{h}"], 16)

        block = ctx.enter_context(nc.Block())

        def slot_ready(eng, i):
            eng.wait_ge(ring_in[i % RING], 16 * (i // RING + 1))

        @block.sync
        def _(sp):
            sp.dma_start(xT[:, :, :], A["xT"]).then_inc(S["x_in"], 16)
            sp.dma_start(cst[:, :], A["consts"]).then_inc(S["consts_in"], 16)
            sp.dma_start(sml[:, :], A["smalls"]).then_inc(S["smalls_in"], 16)

            def load(i):
                if i >= W_Q + RING:
                    sp.wait_ge(S["lo_ready"], 2 + staged(i - RING + 1))
                elif i >= RING:
                    sp.wait_ge(S["slots_used"], i - RING + 1)
                if i < W_CONV:
                    w = PIECES[i // 4][1]
                    sp.dma_start(ring[:, i % RING, 0:2 * w], A[f"wtok{i // 4}"][i % 4]).then_inc(ring_in[i % RING], 16)
                    return
                src = A["wT"][i - W_CONV] if i < W_YC else A["wout"][i - W_YC]
                sp.dma_start(ring[:, i % RING, :], src).then_inc(ring_in[i % RING], 16)

            for i in range(W_CONV):
                load(i)
                if i == RING - 1:
                    sp.dma_start(ar("a", 0, 4096), A["w1"]).then_inc(S["w1_in"], 16)
            sp.wait_ge(S["ptab_in"], 16)
            load_keys(sp, 0, 1)
            load_keys(sp, 0, 2)
            for i in range(W_CONV, W_U):
                if i in (W_CONV, W_CONV + 2):
                    load_chunks(sp, i - W_CONV)
                if i == W_MG + RING:
                    load_chunks(sp, 4)
                    load_chunks(sp, 6)
                load(i)
                if i == W_YN - 1:
                    for b in range(1, 7):
                        load_keys(sp, b, 1)
                        load_keys(sp, b, 2)
                if i == W_O - 1:
                    load_keys(sp, 7, 1)
                    load_keys(sp, 7, 2)
                    sp.wait_ge(S["k_scored"], 3 * 5 + 3)
                    sp.dma_start(xT[:, :, :], A["xT"]).then_inc(S["x_in"], 16)
                if i == W_Q - 1:
                    sp.dma_start(rt("sub"), A["sub"]).then_inc(S["sub_in"], 16)
            with sp.Fori(0, PK // RING) as it:
                for s in range(RING):
                    sp.wait_ge(S["lo_ready"], it * (2 * RING) + (2 + staged(W_U - RING + s + 1)))
                    sp.dma_start(ring[:, s, :], A["uT"][bass.ds(it * RING + s, 1)].rearrange("o p c -> (o p) c")).then_inc(ring_in[s], 16)
            with sp.Fori(0, PK // RING) as it:
                for s in range(RING):
                    sp.wait_ge(S["lo_ready"], it * (2 * RING) + (2 + staged(W_V - RING + s + 1)))
                    sp.dma_start(ring[:, s, :], A["v"][bass.ds(it * RING + s, 1)].rearrange("o p c -> (o p) c")).then_inc(ring_in[s], 16)
            for q in range(2):
                sp.wait_ge(S["y_ready"], 3 + q)
                sp.dma_start(O["yT"][:, 4 * q:4 * q + 4, :], xT[:, 4 * q:4 * q + 4, :]).then_inc(S["y_out"], 16)
            sp.wait_ge(S["y_out"], 32)

        @block.gpsimd
        def _(pool):
            pool.memset(ar("qbn"), 0.0).then_inc(S["u_free"], 2)
            pool.memset(ar("qbr"), 0.0).then_inc(S["hi_used"], 2)
            pool.memset(up[:, :, 0:2], 0.0).then_inc(S["w_free"], 1)
            pool.memset(hid[:, 0:128], 0.0).then_inc(S["lo_used"], 2)
            pool.memset(hid[:, 128:256], 0.0).then_inc(S["lo_ready"], 2)
            pool.memset(zero16[:, :], 0.0).then_inc(S["zeroed"], 1)
            pool.dma_start(ptab[:, :], A["pages"]).then_inc(S["ptab_in"], 16)
            pool.wait_ge(S["ptab_in"], 16)

            def load_values(s):
                for b4 in range(SETB):
                    b = SETB * s + b4
                    for p in range(PAGES):
                        page = pool.value_load(ptab[0:1, b * PAGES + p:b * PAGES + p + 1], min_val=0, max_val=NPOOL - 1)
                        pool.dma_start(vset[s][:, (b4 * 8 + p) * P:(b4 * 8 + p + 1) * P],
                                       A["cache_slc_v"][bass.ds(page, 1)].rearrange("o p c -> (o p) c")).then_inc(S[f"v_in{s}"], 16)
                    pool.dma_start(vset[s][:, 4096 + b4 * 512:4096 + (b4 + 1) * 512].rearrange("p (t c) -> p t c", t=4),
                                   A["cache_win_v"][b].rearrange("(t p) c -> p t c", p=P)).then_inc(S[f"v_in{s}"], 16)

            load_chunks(pool, 1)
            load_keys(pool, 0, 0)
            load_values(0)
            for u in (3, 5, 7):
                load_chunks(pool, u)
            pool.wait_ge(S["comp_mm"], 10)
            pool.wait_ge(S["kcn_ready"], 2)
            load_values(1)
            for b in range(1, NB):
                load_keys(pool, b, 0)
            for v in range(2):
                pool.dma_start(O[["wk", "wv"][v]][:, 0:WINDOW - NQ, :], A["cache_win_" + "kv"[v]][:, NQ:WINDOW, :])\
                    .then_inc(S["win_kept"], 16)
            pool.wait_ge(S["win_kept"], 32)

            def split_low(s, n, it=None, step=0):
                at = lambda c: c if it is None else it * step + c
                for h in range(2):
                    pool.wait_ge(S["hi_ready"], at(n + h + 1))
                    pool.wait_ge(S["lo_used"], at(n + h + 1))
                    pool.tensor_tensor(w_lo[:, h, :], ring[:, s, h * 512:(h + 1) * 512], w_hi[:, h, :].bitcast(F32), ALU.subtract)\
                        .then_inc(S["lo_ready"], 1)

            with pool.Fori(0, (W_END - W_Q) // RING) as it:
                for s in range(RING):
                    split_low(s, 2 * s, it, 2 * RING)

        @block.scalar
        def _(act):
            act.wait_ge(S["x_in"], 16)
            act.activation(xsq, xT[:, :, :], ACT.Square).then_inc(S["x_squared"], 1)
            act.wait_ge(S["x_var"], 1)
            act.activation(rr[:, 1, :], rr[:, 0, :], ACT.Sqrt).then_inc(S["x_std"], 1)
            for p, (c0, w) in enumerate(PIECES):
                act.wait_ge(S["slots_used"], 4 * (p + 1))
                for t, (n0, n) in enumerate(TILES):
                    act.activation(ptok[0:n, t, c0:c0 + w], ps[0:n, 3 * (p % 2) + t, 0:w], ACT.Copy).then_inc(S["tok_copied"], 1)
            def copy_cc(c):
                act.wait_ge(S["slots_used"], W_CONV + 3 * c + 1)
                if c:
                    act.wait_ge(S["u_ready"], c)
                act.activation(rr[:, 1, :], ps[:, 5, 0:NT], ACT.Copy).then_inc(S["cc_copied"], 1)

            for t, (n0, n) in enumerate(TILES):
                act.wait_ge(S["qk_var"], t + 1)
                act.activation(st[0:n, 16:28], st[0:n, 0:12], ACT.Sqrt).then_inc(S["qk_std"], 1)
                act.wait_ge(S["tok_copied"], 9)
                for name, c in (("kc", C_KC), ("vc", C_VC)):
                    act.dma_start(O[name][n0:n0 + n, :], ptok[0:n, t, c:c + P]).then_inc(S["kv_rows_out"], 16)
                act.dma_start(O["vs"][n0:n0 + n, :], ptok[0:n, t, C_VS:C_VS + P]).then_inc(S["rows_out"], 16)
                copy_cc(t)
                act.wait_ge(S["qk_ready"], t + 1)
                act.dma_start(O["ks"][n0:n0 + n, :], qr[0:n, 512:640]).then_inc(S["k_rows_out"], 16)
                for v, src in enumerate([qr[0:n, 640:768], ptok[0:n, t, C_VS + P:C_VS + 2 * P]]):
                    done = S[["k_rows_out", "rows_out"][v]]
                    if t < 2:
                        act.dma_start(O[["kw", "vw"][v]][n0:n0 + n, :], src).then_inc(done, 16)
                    else:
                        act.dma_start(O[["wk", "wv"][v]][:, WINDOW - NQ:WINDOW, :], src).then_inc(done, 16)
                act.wait_ge(S["qk_turned"], t + 1)
                if t < 2:
                    act.activation(qnT[:, :, n0:n0 + n], ps[:, 0, :].rearrange("p (r n) -> p r n", r=R), ACT.Copy)
                    act.activation(qrT[:, :, n0:n0 + n], ps[:, 1, :].rearrange("p (r n) -> p r n", r=R), ACT.Copy)
                    for v in range(2):
                        for g in range(NG):
                            for s2 in range(2):
                                act.activation(xcp[64 * s2:64 * s2 + 64, v, :, g, 8 * t:8 * t + 8],
                                               ps[64 * g:64 * g + 64, 2, 256 + v * P:256 + (v + 1) * P]
                                               .rearrange("p (c k s) -> p s k c", k=8, s=2)[:, s2, :, :], ACT.Copy)
                else:
                    act.wait_ge(S["zeroed"], 1)
                    for i, q in enumerate((qbn, qbr)):
                        for g in range(NG):
                            for r in range(R):
                                act.activation(
                                    q[64 * g:64 * g + 64, :, 16 * g:16 * g + 16].rearrange("p b (q r) -> p b q r", r=R)[:, :, :, r],
                                    ps[64 * g:64 * g + 64, i, r * P:r * P + NS].rearrange("p (b q) -> p b q", b=NB), ACT.Copy)
                act.activation(ksT[:, n0:n0 + n], ps[:, 2, 0:n], ACT.Copy)
                act.activation(kwT[:, n0:n0 + n], ps[:, 2, P:P + n], ACT.Copy).then_inc(S["qT_copied"], 1)
            copy_cc(3)
            for t, (n0, n) in enumerate(TILES):
                act.activation(sg[0:n, t, :], ptok[0:n, t, C_NG:C_NG + 24], ACT.Exp, scale=-1.0).then_inc(S["gate_exp"], 1)
            act.wait_ge(S["u_ready"], 4)
            cstate = O["cstate"].rearrange("p (k n) -> p k n", k=4)
            act.dma_start(cstate[:, :, 0:2], up[:, :, 256:258]).then_inc(S["conv_out"], 16)
            for k in range(4):
                act.dma_start(cstate[:, k, 2:18].rearrange("p (b n) -> p b n", b=NB), us[:, k, :, 4:6]).then_inc(S["conv_out"], 16)
            for name, count in (("kv_rows_out", 6), ("rows_out", 6), ("k_rows_out", 6), ("conv_out", 5)):
                act.wait_ge(S[name], 16 * count)
            act.wait_ge(S["vnew_ready"], 3)

            for u in range(10):
                t, v = u // 2, u % 2
                n = P if t < 4 else 16
                if u:
                    act.wait_ge(S["hid_ready"], u)
                act.wait_ge(S["comp_mm"], u + 1)
                act.activation(sec[:, 0:2 * n], ps[:, 4, 256:256 + 2 * n], ACT.Copy).then_inc(S["sec_copied"], 1)
                act.wait_ge(S["hid_sum"], u + 1)
                if u:
                    act.wait_ge(S["comp_out"], u)
                L = 64 if t < 4 else 16
                view = lambda x: x[:, 0:2 * n].rearrange("p (g c) -> p g c", c=L)[:, :, 0:L - 1]
                act.activation(view(hid), view(sec), ACT.Gelu, bias=bias[:, v:v + 1]).then_inc(S["hid_ready"], 1)
                act.wait_ge(S["comp_out"], u + 1)
                if v == 0:
                    act.activation(kcn[0:n, t, :], ps[0:n, 5, 0:P], ACT.Copy).then_inc(S["cmp_copied"], 1)
                elif t < 4:
                    act.activation(vc[0:64, 2 * t:2 * t + 2, :], ps[0:64, 5, 0:256].rearrange("p (b c) -> p b c", b=2), ACT.Copy)\
                        .then_inc(S["cmp_copied"], 1)
                else:
                    act.activation(vc[0:16, 8, :], ps[0:16, 5, 0:P], ACT.Copy).then_inc(S["cmp_copied"], 1)
            act.wait_ge(S["kcn_var"], 1)
            act.activation(st[:, 16:26], st[:, 0:10], ACT.Sqrt).then_inc(S["kcn_std"], 1)
            for t in range(5):
                n = P if t < 4 else 16
                act.wait_ge(S["kcn_turned"], t + 1)
                act.activation(kcT[:, t * P:t * P + n], ps[:, 6 + t % 2, 0:n], ACT.Copy).then_inc(S["kcT_copied"], 1)

            for u in range(4):
                qt, g = u // 2, u % 2
                nk = P * (qt + 1)
                for c in range(4):
                    i = 4 * u + c
                    act.wait_ge(S["slots_used"], W_MG + i + 1)
                    act.activation(mg[:, i, :], ps[:, 6 + i % 2, 0:NT], ACT.Exp, scale=-1.0).then_inc(S["mg_exp"], 1)
                    if c == 0:
                        act.wait_ge(S["pc_shift"], u + 1)
                        act.activation(st[:, 32:96], st[:, 32:96], ACT.Exp).then_inc(S["pc_exp"], 1)
                        act.wait_ge(S["ps_max"], u + 1)
                        for i8 in range(8):
                            last = act.activation(sc[:, i8 * nk:(i8 + 1) * nk], sc[:, i8 * nk:(i8 + 1) * nk], ACT.Exp,
                                                  bias=st[:, i8:i8 + 1], accum_out=st[:, 16 + i8:17 + i8])
                        last.then_inc(S["ps_exp"], 1)
                act.wait_ge(S["pp_turned"], u + 1)
                w = 1024 * (qt + 1)
                act.activation(pT[:, 0:w // 2], ps[:, 0:2, :].rearrange("p b c -> p (b c)")[:, 0:w // 2], ACT.Copy)
                act.activation(pT[0:16, 2048:2560], ps[0:16, 4, :], ACT.Copy).then_inc(S["pT_act"], 1)
                act.wait_ge(S["po_mm"], u + 1)
                act.activation(oT[64 * g:64 * g + 64, :, qt * P:(qt + 1) * P],
                               ps[64 * g:64 * g + 64, 5, :].rearrange("p (r n) -> p r n", r=R), ACT.Copy).then_inc(S["po_copied"], 1)

            for s in range(2):
                act.wait_ge(S["sc_max"], s + 1)
                act.activation(sc[:, 1600:1663], sc[:, 1600:1663], ACT.Exp, bias=st[:, 2:3], accum_out=st[:, 10:11]).then_inc(S["sc_exp"], 1)
                act.wait_ge(S["ss_max"], s + 1)
                act.activation(sc[:, 0:1056], sc[:, 0:1056], ACT.Exp, bias=st[:, 0:1], accum_out=st[:, 8:9])
                act.activation(sc[:, 1056:1600], sc[:, 1056:1600], ACT.Exp, bias=st[:, 1:2], accum_out=st[:, 9:10]).then_inc(S["ss_exp"], 1)
                act.wait_ge(S["sp_turned"], s + 1)
                act.activation(pT[:, 0:1024], ps[:, 0:2, :].rearrange("p b c -> p (b c)"), ACT.Copy).then_inc(S["spT_act"], 1)
                act.wait_ge(S["so_mm"], s + 1)
                for g in range(NG):
                    for r in range(R):
                        last = act.activation(
                            oT[64 * g:64 * g + 64, r, SEQ + 16 * s:SEQ + 16 * s + 16].rearrange("p (b q) -> p b q", b=SETB),
                            ps[64 * g:64 * g + 64, 7, 0:P].rearrange("p (b g q r) -> p b g q r", b=SETB, g=NG, q=NQ)[:, :, g, :, r], ACT.Copy)
                last.then_inc(S["so_copied"], 1)

            act.wait_ge(S["x1_ready"], KC)
            act.activation(xsq, xT[:, :, :], ACT.Square).then_inc(S["x_squared"], 1)
            act.wait_ge(S["x_var"], 2)
            act.activation(rr2[:, 1, :], rr2[:, 0, :], ACT.Sqrt).then_inc(S["x_std"], 1)
            for half in range(2):
                act.wait_ge(S["h2_normed"], half + 1)
                act.activation(mov_hi[:, 4 * half:4 * half + 4, :], h2[:, 4 * half:4 * half + 4, :], ACT.Copy).then_inc(S["h2_high"], 1)

            def split_high(i, it=None):
                n = staged(i)
                at = lambda c, step: c if it is None else it * step + c
                act.wait_ge(ring_in[i % RING], at(16 * (i // RING + 1), 16))
                for h in range(2):
                    act.wait_ge(S["hi_used"], at(n + h + 1, 2 * RING))
                    act.wait_ge(S["lo_ready"], at(n + h + 1, 2 * RING))
                    act.activation(w_hi[:, h, :], ring[:, i % RING, h * 512:(h + 1) * 512], ACT.Copy).then_inc(S["hi_ready"], 1)

            def copy_query(i):
                act.wait_ge(S["lo_used"], 2 + staged(W_Q + i + 1))
                act.activation(rt("qq")[:, i * NT:(i + 1) * NT], ps[:, i % 2, 0:NT], ACT.Copy).then_inc(S["qq_copied"], 1)

            for i in range(16):
                split_high(W_Q + i)
                if i:
                    copy_query(i - 1)
            copy_query(15)
            split_high(W_U)
            for t, (n0, n) in enumerate(TILES):
                act.wait_ge(S["pk_mm"], t + 1)
                act.activation(rt("sp")[0:n, t * 2048:(t + 1) * 2048], ps[0:n, 4:8, :].rearrange("p b c -> p (b c)"), ACT.Copy)\
                    .then_inc(S["pk_copied"], 1)

            def gelus(it, j0, ahead=RING):
                for s in range(RING):
                    if s < ahead:
                        split_high(W_U + j0 + s + 1, it)
                    act.wait_ge(S["lo_used"], it * (2 * RING) + (2 + staged(W_U + j0 + s + 1)))
                    act.activation(arena[:, bass.ds((it * RING + (j0 + s)) * NT, NT)], ps[:, s % 2, 0:NT], ACT.Gelu).then_inc(S["u_free"], 1)

            for t, (n0, n) in enumerate(TILES):
                with act.Fori(0, 4) as it:
                    gelus(it, 16 * t)
                act.wait_ge(S["top_shift"], t + 1)
                act.activation(rt("tv")[0:n, :], rt("tv")[0:n, :], ACT.Exp).then_inc(S["top_exp"], 1)
            with act.Fori(0, 4) as it:
                gelus(it, 48)
            act.wait_ge(S["route_copied"], 1)
            with act.Fori(0, HALF // RING - 1) as it:
                gelus(it, HALF)
            with act.Fori(0, 1) as it:
                gelus(it, PK - RING, RING - 1)

            act.wait_ge(S["w_free"], 1 + 32)
            for q in range(4):
                if q == 2:
                    act.wait_ge(S["w_free"], 1 + 64)
                with act.Fori(0, 8) as it:
                    for s in range(RING):
                        act.wait_ge(S["lo_used"], it * (2 * RING) + (2 + staged(W_V + 32 * q + s - RING + 1)))
                        act.activation(mov_hi[:, 2 * s:2 * s + 2, :].rearrange("p j n -> p (j n)"),
                                       arena[:, bass.ds((it * 8 + (HALF * (q // 2) + 2 * s)) * NT, 2 * NT)], ACT.Copy)\
                            .then_inc(S["mov_high"], 1)
                        split_high(W_V + 32 * q + s, it)

        @block.vector
        def _(dve):
            link = link_on(dve, S["dve_order"])

            def mean_square(rr):
                dve.tensor_scalar(rr[:, 0, :], ps[:, 0, 0:NT], 1.0 / D, EPS, ALU.mult, ALU.add).then_inc(S["x_var"], 1)

            def scaled(out, k, gain, rr):
                return dve.scalar_tensor_tensor(out=out[:, k, :], in0=xT[:, k, :], scalar=gain[:, k:k + 1], in1=rr[:, 0, :],
                                                op0=ALU.mult, op1=ALU.mult)

            dve.wait_ge(S["smalls_in"], 16)
            dve.wait_ge(S["consts_in"], 16)
            dve.wait_ge(S["x_sumsq"], 1)
            mean_square(rr)
            dve.wait_ge(S["x_std"], 1)
            link(dve.reciprocal(rr[:, 0, :], rr[:, 1, :]))
            for k in range(KC):
                last = scaled(xT, k, M("norm_mix"), rr)
            last.then_inc(S["h_ready"], 1)
            dve.wait_ge(S["zeroed"], 1)
            dve.tensor_copy(us[:, :, :, 0:2], M("state").rearrange("p (k b n) -> p k b n", k=4, b=NB))

            heads = lambda x: x.rearrange("p (h d) -> p h d", d=HD)

            def head_rows(t, n):
                dve.wait_ge(S["tok_copied"], 3 + t + 1)
                if t:
                    dve.wait_ge(S["qk_turned"], t)
                    dve.wait_ge(S["k_rows_out"], 32 * t)
                qk = ptok[0:n, t, 0:768]
                link(dve.tensor_tensor(tmpq[0:n, :], qk, qk, ALU.mult))
                link(dve.tensor_reduce(st[0:n, 0:12], heads(tmpq[0:n, :]), AX.X, ALU.add))
                dve.tensor_scalar(st[0:n, 0:12], st[0:n, 0:12], 1.0 / HD, EPS, ALU.mult, ALU.add).then_inc(S["qk_var"], 1)
                dve.wait_ge(S["qk_std"], t + 1)
                link(dve.reciprocal(st[0:n, 0:12], st[0:n, 16:28]))
                link(dve.tensor_tensor(heads(qn[0:n, :]), heads(qk), over(st[0:n, 0:12], 2, HD), ALU.mult))
                link(dve.tensor_tensor(qn[0:n, :], qn[0:n, :], M("gain")[0:n, :], ALU.mult))
                cos, sin = C("cos", n)[:, t * HD:(t + 1) * HD], C("sin", n)[:, t * HD:(t + 1) * HD]
                q3, t3 = heads(qn[0:n, :]), heads(tmpq[0:n, :])
                dve.tensor_tensor(t3[:, :, 0:32], q3[:, :, 32:64], over(sin[:, 0:32], 1, 12), ALU.mult)
                dve.tensor_tensor(t3[:, :, 32:64], q3[:, :, 0:32], over(sin[:, 32:64], 1, 12), ALU.mult)
                link(dve.tensor_tensor(heads(qr[0:n, :]), q3, over(cos, 1, 12), ALU.mult))
                dve.tensor_tensor(qr[0:n, :], qr[0:n, :], tmpq[0:n, :], ALU.add).then_inc(S["qk_ready"], 1)

            cw = M("conv_w").rearrange("p (k c) -> p k c", k=3)

            def conv(c):
                dve.wait_ge(S["cc_copied"], c + 1)
                dve.wait_ge(S["slots_used"], W_CONV + 3 * c + 2)
                dve.tensor_tensor(up[:, c, 2:258], ps[:, 6, 0:SEQ], rr[:, 1, 0:SEQ], ALU.mult)
                dve.tensor_tensor(us[:, c, :, 2:6], ps[:, 6, SEQ:NT].rearrange("p (b n) -> p b n", b=NB),
                                  rr[:, 1, SEQ:NT].rearrange("p (b n) -> p b n", b=NB), ALU.mult).then_inc(S["u_ready"], 1)
                dve.wait_ge(S["u_ready"], c + 1)
                z_p, z_s = zT[:, c, 0:SEQ], zT[:, c, SEQ:NT].rearrange("p (b n) -> p b n", b=NB)
                dve.tensor_scalar(z_p, up[:, c, 0:SEQ], cw[:, 0, c:c + 1], None, ALU.mult)
                link(dve.tensor_scalar(z_s, us[:, c, :, 0:4], cw[:, 0, c:c + 1], None, ALU.mult))
                for k in (1, 2):
                    dve.scalar_tensor_tensor(out=z_p, in0=up[:, c, k:k + SEQ], scalar=cw[:, k, c:c + 1], in1=z_p, op0=ALU.mult, op1=ALU.add)
                    link(dve.scalar_tensor_tensor(out=z_s, in0=us[:, c, :, k:k + 4], scalar=cw[:, k, c:c + 1], in1=z_s, op0=ALU.mult, op1=ALU.add))
                dve.wait_ge(S["slots_used"], W_CONV + 3 * c + 3)
                dve.tensor_tensor(zT[:, c, :], ps[:, 7, 0:NT], zT[:, c, :], ALU.mult).then_inc(S["z_ready"], 1)

            for t, (n0, n) in enumerate(TILES):
                head_rows(t, n)
                conv(t)
            conv(3)
            dve.wait_ge(S["tok_copied"], 9)
            for t, (n0, n) in enumerate(TILES):
                dve.tensor_copy(vnew[0:n, t, :], ptok[0:n, t, C_VS:C_VS + 2 * P]).then_inc(S["vnew_ready"], 1)
            dve.wait_ge(S["gate_exp"], 3)
            for t, (n0, n) in enumerate(TILES):
                link(dve.tensor_scalar(sg[0:n, t, :], sg[0:n, t, :], 1.0, None, ALU.add))
                dve.reciprocal(sg[0:n, t, :], sg[0:n, t, :]).then_inc(S["gate_ready"], 1)

            dve.wait_ge(S["cbias_mm"], 1)
            dve.tensor_tensor(bias[:, :], ps[:, 7, 0:2], M("b1"), ALU.add)
            for u in range(10):
                t, v = u // 2, u % 2
                n = P if t < 4 else 16
                dve.wait_ge(S["comp_mm"], u + 1)
                dve.wait_ge(S["sec_copied"], u + 1)
                L = 64 if t < 4 else 16
                f = ps[:, 4, 0:2 * n].rearrange("p (g c) -> p g c", c=L)
                s3 = sec[:, 0:2 * n].rearrange("p (g c) -> p g c", c=L)
                dve.tensor_tensor(s3[:, :, 0:L - 1], f[:, :, 0:L - 1], s3[:, :, 1:L], ALU.add).then_inc(S["hid_sum"], 1)
            dve.wait_ge(S["cmp_copied"], 10)
            k2 = kcn.rearrange("p t (g d) -> p (t g) d", d=HD)
            sq = ar("a", 4096, 5 * P).rearrange("p (g d) -> p g d", d=HD)
            for n, lo, hi in ((P, 0, 8), (16, 8, 10)):
                link(dve.tensor_tensor(sq[0:n, lo:hi], k2[0:n, lo:hi], k2[0:n, lo:hi], ALU.mult))
                if lo == 0:
                    link(dve.memset(st[:, 0:10], 1.0))
                link(dve.tensor_reduce(st[0:n, lo:hi], sq[0:n, lo:hi], AX.X, ALU.add))
            dve.tensor_scalar(st[:, 0:10], st[:, 0:10], 1.0 / HD, EPS, ALU.mult, ALU.add).then_inc(S["kcn_var"], 1)
            dve.wait_ge(S["kcn_std"], 1)
            link(dve.reciprocal(st[:, 0:10], st[:, 16:26]))
            for n, lo, hi in ((P, 0, 8), (16, 8, 10)):
                link(dve.tensor_tensor(k2[0:n, lo:hi], k2[0:n, lo:hi], over(st[0:n, lo:hi], 2, HD), ALU.mult))
                dve.tensor_tensor(k2[0:n, lo:hi], k2[0:n, lo:hi], over(M("kcgain")[0:n, :], 1, hi - lo), ALU.mult).then_inc(S["kcn_ready"], 1)

            for u in range(4):
                qt, g = u // 2, u % 2
                nk = P * (qt + 1)
                dve.wait_ge(S["p_scored"], u + 1)
                if u:
                    dve.wait_ge(S["pp_turned"], u)
                cs = st[:, 32:96].rearrange("p (r c) -> p r c", r=R)
                link(dve.scalar_tensor_tensor(out=cs, in0=ps[:, 4, 0:64].rearrange("p (r c) -> p r c", r=R), scalar=SCALE,
                                              in1=over(C("cmpmask")[:, 16 * qt:16 * qt + 16], 1, R), op0=ALU.mult, op1=ALU.add))
                link(dve.tensor_reduce(st[:, 8:12], cs, AX.X, ALU.max))
                link(dve.tensor_scalar(st[:, 8:12], st[:, 8:12], NEG / 10, None, ALU.max))
                dve.tensor_tensor(cs, cs, over(st[:, 8:12], 2, 16), ALU.subtract).then_inc(S["pc_shift"], 1)
                s8 = sc[:, 0:8 * nk].rearrange("p (i c) -> p i c", c=nk)
                scores = ps[:, 0:2 * (qt + 1), :].rearrange("p b c -> p (b c)").rearrange("p (i c) -> p i c", c=nk)
                mask = C("causal")[:, P - P * qt:2 * P]
                link(dve.scalar_tensor_tensor(out=s8, in0=scores, scalar=SCALE, in1=over(mask, 1, 8), op0=ALU.mult, op1=ALU.add))
                dve.tensor_reduce(st[:, 0:8], s8, AX.X, ALU.max, negate=True).then_inc(S["ps_max"], 1)
                dve.wait_ge(S["pc_exp"], u + 1)
                link(dve.tensor_reduce(st[:, 24:28], cs, AX.X, ALU.add))
                link(dve.tensor_scalar(st[:, 24:28], st[:, 24:28], 1e-30, None, ALU.max))
                dve.wait_ge(S["ps_exp"], u + 1)
                link(dve.reciprocal(st[:, 16:28], st[:, 16:28]))
                gates = sg[:, qt, 12 * g:12 * g + 12].rearrange("p (r b) -> p b r", b=3)
                dve.tensor_tensor(st[:, 24:28], st[:, 24:28], gates[:, 0, :], ALU.mult)
                link(dve.tensor_tensor(st[:, 16:24].rearrange("p (b r) -> p b r", b=2), st[:, 16:24].rearrange("p (b r) -> p b r", b=2),
                                       gates[:, 1:3, :], ALU.mult))
                dve.tensor_tensor(cs, cs, over(st[:, 24:28], 2, 16), ALU.mult)
                dve.tensor_tensor(s8, s8, over(st[:, 16:24], 2, nk), ALU.mult).then_inc(S["p_weights"], 1)
                dve.wait_ge(S["pp_turned"], u + 1)
                w = 1024 * (qt + 1)
                if u:
                    dve.wait_ge(S["po_mm"], u)
                dve.tensor_copy(pT[:, w // 2:w], ps[:, 0:4, :].rearrange("p b c -> p (b c)")[:, w // 2:w]).then_inc(S["pT_dve"], 1)
                dve.wait_ge(S["mg_exp"], 4 * u + 4)
                four = mg[:, 4 * u:4 * u + 4, :]
                link(dve.tensor_scalar(four, four, 1.0, None, ALU.add))
                dve.reciprocal(four, four).then_inc(S["mg_ready"], 1)

            dve.wait_ge(S["rep_mm"], 1)
            for s in range(2):
                t24 = st[:, 32:56].rearrange("p (e b) -> p e b", b=3)
                link(dve.tensor_tensor(t24, ps[:, 5, 24 * s:24 * s + 24].rearrange("p (e b) -> p e b", b=3),
                                       over(C("gsel"), 2, 3), ALU.mult))
                dve.tensor_reduce(rg[:, 3 * s:3 * s + 3], t24.rearrange("p e b -> p b e"), AX.X, ALU.add).then_inc(S["rg_ready"], 1)
                dve.wait_ge(S["rg_ready"], s + 1)
            for s in range(2):
                dve.wait_ge(S["k_scored"], 12 * (s + 1))
                if s:
                    dve.wait_ge(S["sp_turned"], s)
                    dve.wait_ge(S["so_mm"], s)
                cn, cg = sc[:, 1600:1663], sc[:, 1664:1727]
                link(dve.tensor_scalar(cn, ps[:, 3, 64:127], SCALE, None, ALU.mult))
                dve.tensor_reduce(st[:, 2:3], cn, AX.X, ALU.max, negate=True).then_inc(S["sc_max"], 1)
                nm = C("newmask")[:, NS * s:NS * s + NS]
                dve.scalar_tensor_tensor(out=sc[:, 1024:1056], in0=ps[:, 3, 0:32], scalar=SCALE, in1=nm, op0=ALU.mult, op1=ALU.add)
                dve.scalar_tensor_tensor(out=sc[:, 1568:1600], in0=ps[:, 3, 32:64], scalar=SCALE, in1=nm, op0=ALU.mult, op1=ALU.add)
                link(dve.tensor_scalar(sc[:, 1056:1568], ps[:, 2, :], SCALE, None, ALU.mult))
                link(dve.tensor_tensor(sc[:, 1056:1060], sc[:, 1056:1060], C("winmask"), ALU.add))
                link(dve.tensor_reduce(st[:, 1:2], sc[:, 1056:1600], AX.X, ALU.max, negate=True))
                dve.wait_ge(S["sc_exp"], s + 1)
                link(dve.reciprocal(st[:, 10:11], st[:, 10:11]))
                dve.tensor_scalar(cn, cn, st[:, 10:11], None, ALU.mult).then_inc(S["cn_ready"], 1)
                dve.wait_ge(S["cn_turned"], s + 1)
                g32, p4 = pT[0:63, 2048:2080], pT[0:63, 2080:2208]
                link(dve.tensor_reduce(g32, ps[0:63, 3, 128:256].rearrange("p (a r) -> p a r", r=R), AX.X, ALU.add))
                dve.tensor_copy(p4.rearrange("p (a r) -> p a r", r=R), over(g32, 2, R)).then_inc(S["p4_ready"], 1)
                dve.wait_ge(S["blk_mm"], s + 1)
                blk, eq = st[:, 32:49], st[:, 52:69]
                link(dve.tensor_tensor(blk, ps[:, 3, 256:273], C("forced"), ALU.add))
                link(dve.tensor_reduce(st[:, 12:13], blk, AX.X, ALU.min))
                link(dve.scalar_tensor_tensor(out=eq, in0=blk, scalar=st[:, 12:13], in1=C("jp1"), op0=ALU.is_equal, op1=ALU.mult))
                link(dve.tensor_reduce(st[:, 13:14], eq, AX.X, ALU.max))
                link(dve.tensor_scalar(eq, C("jp1"), st[:, 13:14], NEG, ALU.is_equal, ALU.mult))
                link(dve.scalar_tensor_tensor(out=sc[:, 0:1024].rearrange("p (j c) -> p j c", c=BLK),
                                              in0=ps[:, 0:2, :].rearrange("p b c -> p (b c)").rearrange("p (j c) -> p j c", c=BLK),
                                              scalar=SCALE, in1=over(eq[:, 0:16], 2, BLK), op0=ALU.mult, op1=ALU.add))
                dve.tensor_reduce(st[:, 0:1], sc[:, 0:1056], AX.X, ALU.max, negate=True).then_inc(S["ss_max"], 1)
                if s == 0:
                    for m in range(KC):
                        dve.wait_ge(S["slots_used"], W_YC + m // 2 + 1)
                        dve.tensor_tensor(mg[:, m, :], ps[:, 4 + m % 2, 0:NT], mg[:, m, :], ALU.mult).then_inc(S["yc_used"], 1)
                dve.wait_ge(S["ss_exp"], s + 1)
                link(dve.reciprocal(st[:, 8:10], st[:, 8:10]))
                link(dve.tensor_tensor(st[:, 8:10], st[:, 8:10], rg[:, 3 * s + 1:3 * s + 3], ALU.mult))
                dve.tensor_scalar(cg, cn, rg[:, 3 * s:3 * s + 1], None, ALU.mult)
                dve.tensor_scalar(sc[:, 0:1056], sc[:, 0:1056], st[:, 8:9], None, ALU.mult)
                dve.tensor_scalar(sc[:, 1056:1600], sc[:, 1056:1600], st[:, 9:10], None, ALU.mult).then_inc(S["s_weights"], 1)
                dve.wait_ge(S["sp_turned"], s + 1)
                dve.tensor_copy(pT[:, 1024:1536], ps[:, 2, :])
                dve.tensor_copy(pT[0:32, 1536:1792], ps[0:32, 3, 0:256])
                dve.tensor_copy(pT[0:63, 1792:1920], ps[0:63, 3, 256:384]).then_inc(S["spT_dve"], 1)
            for m in range(KC):
                dve.wait_ge(S["slots_used"], W_YN + m // 2 + 1)
                if m:
                    dve.wait_ge(S["merged"], m)
                link(dve.tensor_tensor(mt, ps[:, 4 + m % 2, 0:NT], mg[:, 8 + m, :], ALU.mult))
                dve.tensor_tensor(mg[:, m, :], mg[:, m, :], mt, ALU.add).then_inc(S["merged"], 1)
            dve.wait_ge(S["x_in"], 32)
            for m in range(KC):
                dve.wait_ge(S["slots_used"], W_O + m + 1)
                dve.tensor_tensor(xT[:, m, :], xT[:, m, :], ps[:, 2 + m % 2, 0:NT], ALU.add).then_inc(S["x1_ready"], 1)
            dve.wait_ge(S["x_sumsq"], 2)
            mean_square(rr2)
            dve.wait_ge(S["x_std"], 2)
            link(dve.reciprocal(rr2[:, 0, :], rr2[:, 1, :]))
            for k in range(KC):
                last = scaled(h2, k, M("norm_ffn"), rr2)
                if k % 4 == 3:
                    last.then_inc(S["h2_normed"], 1)
            for half in range(2):
                four = slice(4 * half, 4 * half + 4)
                dve.wait_ge(S["h2_high"], half + 1)
                dve.tensor_tensor(mov_lo[:, four, :], h2[:, four, :], mov_hi[:, four, :].bitcast(F32), ALU.subtract).then_inc(S["h2_split"], 1)

            for t, (n0, n) in enumerate(TILES):
                sp, cand, eq = (rt(x)[0:n, :] for x in ("sp", "cand", "eq"))
                sp = sp[:, t * 2048:(t + 1) * 2048]
                lv, li, lf, tv, ti, ab, abf, z8 = (rt(x)[0:n, :] for x in ("lv", "li", "lf", "tv", "ti", "ab", "abf", "z8"))
                gi = rt("gi")[0:n, 3 * P * t:3 * P * (t + 1)]

                def top16(groups, width, src, val, idx):
                    for half in range(2):
                        for i in range(groups):
                            last = dve.max(out=val[:, 16 * i + 8 * half:16 * i + 8 * half + 8], in_=src[:, i * width:(i + 1) * width])
                        link(last)
                        for i in range(groups):
                            last = dve.max_index(out=idx[:, 16 * i + 8 * half:16 * i + 8 * half + 8],
                                                 in_max=val[:, 16 * i + 8 * half:16 * i + 8 * half + 8], in_values=src[:, i * width:(i + 1) * width])
                        if half == 0:
                            for i in range(groups):
                                last = dve.match_replace(out=src[:, i * width:(i + 1) * width], in_to_replace=val[:, 16 * i:16 * i + 8],
                                                         in_values=src[:, i * width:(i + 1) * width], imm_value=-3e38)
                        link(last)

                dve.wait_ge(S["pk_copied"], t + 1)
                top16(16, PK, sp, lv, li.bitcast(U32))
                link(dve.tensor_copy(lf, li.bitcast(U32)))
                l4 = lv.rearrange("p (h c k) -> p h c k", h=PH, c=2)
                c4 = cand.rearrange("p (h a b) -> p h a b", h=PH, a=PTOP)
                dve.wait_ge(S["pk_mm"], 3)
                link(dve.tensor_tensor(c4, over(l4[:, :, 0, :], 3, PTOP), over(l4[:, :, 1, :], 2, PTOP), ALU.add))
                top16(PH, 256, cand, tv, ti.bitcast(U32))
                t3 = tv.rearrange("p (h k) -> p h k", h=PH)
                link(dve.tensor_copy(z8[:, 0:8], t3[:, :, 0]))
                dve.tensor_tensor(t3, t3, over(z8[:, 0:8], 2, PTOP), ALU.subtract).then_inc(S["top_shift"], 1)
                u = ti.bitcast(U32)
                dve.tensor_scalar(ab[:, 0:P].bitcast(U32), u, 4, None, ALU.logical_shift_right)
                link(dve.tensor_scalar(ab[:, P:2 * P].bitcast(U32), u, 15, None, ALU.bitwise_and))
                link(dve.tensor_copy(abf, ab.bitcast(U32)))
                lf4 = lf.rearrange("p (h c k) -> p h c k", h=PH, c=2)
                e4 = eq.rearrange("p (h k a) -> p h k a", h=PH, k=PTOP)
                for c in range(2):
                    place = abf[:, c * P:(c + 1) * P].rearrange("p (h k) -> p h k", h=PH)
                    link(dve.tensor_tensor(eq.rearrange("p (k a) -> p k a", a=PTOP), over(abf[:, c * P:(c + 1) * P], 2, PTOP),
                                           over(C("iota16", n), 1, P), ALU.is_equal))
                    link(dve.tensor_tensor(e4, e4, over(lf4[:, :, c, :], 2, PTOP), ALU.mult))
                    link(dve.tensor_reduce(gi[:, (1 + c) * P:(2 + c) * P], eq.rearrange("p (k a) -> p k a", a=PTOP), AX.X, ALU.add))
                dve.wait_ge(S["top_exp"], t + 1)
                link(dve.tensor_reduce(z8[:, 0:8], t3, AX.X, ALU.add))
                link(dve.reciprocal(z8[:, 8:16], z8[:, 0:8]))
                dve.tensor_tensor(gi[:, 0:P].rearrange("p (h k) -> p h k", h=PH), t3, over(z8[:, 8:16], 2, PTOP), ALU.mult).then_inc(S["routed"], 1)
            dve.wait_ge(S["route_turned"], 1)
            last = dve.tensor_copy(aux[:, LISTS:HOT].rearrange("p (i n) -> p i n", i=3), ps[:, 5:8, 0:NT])
            last.then_inc(S["route_copied"], 1)
            dve.wait_ge(S["route_copied"], 1)
            gT, i1T, i2T = (aux[:, LISTS + i * NT:LISTS + (i + 1) * NT] for i in range(3))

            def one_hots(it, g, half, g0):
                for x in range(GT):
                    n = it * (2 * GT) + ((g0 + g) * GT + x)
                    dve.tensor_scalar(oh[:, x, 0:P], C("iota"), i1T[:, bass.ds(n, 1)], None, ALU.is_equal)
                    last = dve.tensor_scalar(oh[:, x, P:P + HALF], C("iota")[:, HALF * half:HALF * half + HALF],
                                             i2T[:, bass.ds(n, 1)], gT[:, bass.ds(n, 1)], ALU.is_equal, ALU.mult)
                last.then_inc(S["oh_ready"], 1)

            def weigh(it, g, half, g0):
                dve.wait_ge(S["route_mm"], it * 2 + (32 * half + g0 + g + 1))
                w = arena[:, HALF * half * NT:HALF * (half + 1) * NT].rearrange("p (j n) -> p n j", n=NT)[:, bass.ds(it * (2 * GT) + (g0 + g) * GT, GT), :]
                dve.tensor_tensor(w, ps[:, 2:4, :].rearrange("p b c -> p (b c)")[:, 0:GT * HALF].rearrange("p (n j) -> p n j", n=GT),
                                  w, ALU.mult).then_inc(S["w_free"], 1)

            def split_moving(it, q, s):
                dve.wait_ge(S["mov_high"], it * RING + (32 * q + s + 1))
                dve.tensor_tensor(mov_lo[:, 2 * s:2 * s + 2, :].rearrange("p j n -> p (j n)"),
                                  arena[:, bass.ds((it * 8 + (HALF * (q // 2) + 2 * s)) * NT, 2 * NT)],
                                  mov_hi[:, 2 * s:2 * s + 2, :].rearrange("p j n -> p (j n)").bitcast(F32), ALU.subtract)\
                    .then_inc(S["mov_ready"], 1)

            dve.wait_ge(S["u_free"], 2 + HALF)
            with dve.Fori(0, 16) as it:
                for g in range(2):
                    one_hots(it, g, 0, 0)
                    weigh(it, g, 0, 0)
            dve.wait_ge(S["u_free"], 2 + PK)
            for q in range(4):
                if q == 0:
                    dve.wait_ge(S["w_free"], 1 + 32)
                if q == 2:
                    dve.wait_ge(S["w_free"], 1 + 64)
                with dve.Fori(0, 8) as it:
                    for s in range(RING):
                        split_moving(it, q, s)
                        if q < 2:
                            (one_hots, weigh)[s % 2](it, s // 2, 1, 16 * q)
                dve.wait_ge(S["lo_used"], 2 + staged(W_V + 32 * (q + 1)))
                for m in range(4):
                    x = xT[:, 4 * (q % 2) + m, :]
                    last = dve.tensor_tensor(x, x, ps[:, VBANK[m], 0:NT], ALU.add)
                last.then_inc(S["y_ready"], 1)

        @block.tensor
        def _(pe):
            def project(i, bank, rhs, n=KC, at=0):
                slot_ready(pe, i)
                for k in range(n):
                    last = pe.matmul(ps[:, bank, 0:NT], ring[:, i % RING, at + k * P:at + (k + 1) * P], rhs[:, k, :],
                                     start=(k == 0), stop=(k == n - 1))
                return last

            def sum_squares():
                for k in range(KC):
                    last = pe.matmul(ps[:, 0, 0:NT], C("ones"), xsq[:, k, :], start=(k == 0), stop=(k == KC - 1))
                last.then_inc(S["x_sumsq"], 1)

            pe.wait_ge(S["consts_in"], 16)
            pe.wait_ge(S["x_squared"], 1)
            sum_squares()
            pe.wait_ge(S["h_ready"], 1)
            for p, (c0, w) in enumerate(PIECES):
                if p == 2:
                    pe.wait_ge(S["tok_copied"], 3)
                for i in range(4):
                    slot_ready(pe, 4 * p + i)
                    for kk in range(2):
                        k = 2 * i + kk
                        for t, (n0, n) in enumerate(TILES):
                            last = pe.matmul(ps[0:n, 3 * (p % 2) + t, 0:w], xT[:, k, n0:n0 + n],
                                             ring[:, (4 * p + i) % RING, kk * w:(kk + 1) * w], start=(k == 0), stop=(k == KC - 1))
                    last.then_inc(S["slots_used"], 1)

            def conv_chunks(c):
                if c == 0:
                    pe.wait_ge(S["tok_copied"], 6)
                else:
                    pe.wait_ge(S["cc_copied"], c)
                project(W_CONV + 3 * c, 5, xT).then_inc(S["slots_used"], 1)
                if c:
                    pe.wait_ge(S["u_ready"], c)
                project(W_CONV + 3 * c + 1, 6, xT).then_inc(S["slots_used"], 1)
                if c:
                    pe.wait_ge(S["z_ready"], c)
                project(W_CONV + 3 * c + 2, 7, xT).then_inc(S["slots_used"], 1)

            for t, (n0, n) in enumerate(TILES):
                conv_chunks(t)
                pe.wait_ge(S["qk_ready"], t + 1)
                if t == 0:
                    pe.wait_ge(S["tok_copied"], 9)
                else:
                    pe.wait_ge(S["qT_copied"], t)
                for i, q in enumerate((qn, qr)):
                    for r in range(R):
                        pe.transpose(ps[:, i, r * P:r * P + n], q[0:n, r * P:(r + 1) * P], ident[0:n, 0:n])
                if t < 2:
                    for v, c in enumerate((C_KC, C_VC)):
                        pe.transpose(ps[:, 2, (2 + v) * P:(3 + v) * P], ptok[:, t, c:c + P], ident)
                pe.transpose(ps[:, 2, 0:n], qr[0:n, 512:640], ident[0:n, 0:n])
                pe.transpose(ps[:, 2, P:P + n], qr[0:n, 640:768], ident[0:n, 0:n]).then_inc(S["qk_turned"], 1)
            conv_chunks(3)

            pe.wait_ge(S["w1_in"], 16)
            pe.wait_ge(S["z_ready"], 4)
            for v in range(2):
                for k in range(16):
                    last = pe.matmul(ps[:, 7, v:v + 1], w1[:, v, k, :], M("pos")[:, 16 * v + k:16 * v + k + 1], start=(k == 0), stop=(k == 15))
            last.then_inc(S["cbias_mm"], 1)
            pe.wait_ge(S["qT_copied"], 3)

            def comp_out(u):
                t, v = u // 2, u % 2
                n = P if t < 4 else 16
                pe.wait_ge(S["hid_ready"], u + 1)
                if u:
                    pe.wait_ge(S["cmp_copied"], u)
                w2 = M("w2")[:, v * HD:(v + 1) * HD]
                if v == 0 or t == 4:
                    for g in range(NG):
                        last = pe.matmul(ps[0:n, 5, g * HD:(g + 1) * HD], hid[:, g * n:(g + 1) * n], w2, start=True, stop=True)
                else:
                    for b in range(2):
                        for g in range(NG):
                            last = pe.matmul(ps[0:64, 5, b * P + g * HD:b * P + (g + 1) * HD], hid[:, g * P + b * 64:g * P + b * 64 + 64], w2,
                                             start=True, stop=True)
                last.then_inc(S["comp_out"], 1)

            for u in range(10):
                t, v = u // 2, u % 2
                n = P if t < 4 else 16
                if t < 4:
                    pe.wait_ge(S[f"xc_in{u % 6}"], 256 * (u // 6 + 1))
                if u:
                    pe.wait_ge(S["hid_sum"], u)
                for half in range(2):
                    for k in range(8):
                        if t < 4:
                            src = xc[:, u % 3, :, k, :, :].rearrange("p j g c -> p g j c")
                            dst = ps[:, 4, 256 * half:256 * half + 256].rearrange("p (g j c) -> p g j c", g=NG, j=16)
                        else:
                            src, dst = xcp[:, v, k, :, :], ps[:, 4, 256 * half:256 * half + 32].rearrange("p (g c) -> p g c", g=NG)
                        last = pe.matmul(dst, w1[:, v, 8 * half + k, :], src, start=(k == 0), stop=(k == 7))
                last.then_inc(S["comp_mm"], 1)
                if u:
                    comp_out(u - 1)
            comp_out(9)
            for t in range(5):
                n = P if t < 4 else 16
                pe.wait_ge(S["kcn_ready"], 1 if t < 4 else 2)
                if t >= 2:
                    pe.wait_ge(S["kcT_copied"], t - 1)
                pe.transpose(ps[:, 6 + t % 2, 0:n], kcn[0:n, t, :], ident[0:n, 0:n]).then_inc(S["kcn_turned"], 1)
            pe.wait_ge(S["kcT_copied"], 5)

            pe.wait_ge(S["vnew_ready"], 3)
            for u in range(4):
                qt, g = u // 2, u % 2
                nk = P * (qt + 1)
                lane, n0 = slice(64 * g, 64 * g + 64), qt * P
                if u:
                    pe.wait_ge(S["pT_act"], u)
                    pe.wait_ge(S["pT_dve"], u)
                flat = ps[:, 0:4, :].rearrange("p b c -> p (b c)")
                for r in range(R):
                    pe.matmul(ps[:, 4, 16 * r:16 * r + 16], qnT[lane, r, n0:n0 + P], kcT[lane, 4 * P:4 * P + 16], start=True, stop=True)
                    for br, keys in enumerate((ksT, kwT)):
                        i = 4 * br + r
                        last = pe.matmul(flat[:, i * nk:(i + 1) * nk], qrT[lane, r, n0:n0 + P], keys[lane, 0:nk], start=True, stop=True)
                last.then_inc(S["p_scored"], 1)
                for i in range(4 * u, 4 * u + 4):
                    if i >= 2:
                        pe.wait_ge(S["mg_exp"], i - 1)
                    project(W_MG + i, 6 + i % 2, xT).then_inc(S["slots_used"], 1)
                pe.wait_ge(S["p_weights"], u + 1)
                for i in range(8):
                    for kt in range(qt + 1):
                        x = i * (qt + 1) + kt
                        pe.transpose(flat[:, x * P:(x + 1) * P], sc[:, x * P:(x + 1) * P], ident)
                for r in range(R):
                    last = pe.transpose(ps[0:16, 4, r * P:(r + 1) * P], st[:, 32 + 16 * r:48 + 16 * r], ident)
                last.then_inc(S["pp_turned"], 1)
                pe.wait_ge(S["pT_act"], u + 1)
                pe.wait_ge(S["pT_dve"], u + 1)
                if u:
                    pe.wait_ge(S["po_copied"], u)
                for r in range(R):
                    o = ps[:, 5, r * P:(r + 1) * P]
                    pe.matmul(o, vc[0:16, 8, :], pT[0:16, 2048 + r * P:2048 + (r + 1) * P], start=True, stop=False)
                    for br in range(2):
                        for kt in range(qt + 1):
                            x = (4 * br + r) * (qt + 1) + kt
                            last = pe.matmul(o, vnew[:, kt, br * P:(br + 1) * P], pT[:, x * P:(x + 1) * P], start=False,
                                             stop=(br == 1 and kt == qt))
                last.then_inc(S["po_mm"], 1)

            pe.wait_ge(S["gate_ready"], 3)
            pe.wait_ge(S["po_copied"], 4)
            for s in range(2):
                last = pe.matmul(ps[:, 5, 24 * s:24 * s + 24], C("rep")[0:NS, s * P:(s + 1) * P], sg[0:NS, 2, :], start=True, stop=True)
            last.then_inc(S["rep_mm"], 1)
            for s in range(2):
                if s:
                    pe.wait_ge(S["spT_act"], s)
                    pe.wait_ge(S["spT_dve"], s)
                    pe.wait_ge(S["so_copied"], s)
                for b4 in range(SETB):
                    b = SETB * s + b4
                    rows = slice(32 * b4, 32 * b4 + 32)
                    pe.matmul(ps[rows, 3, 0:NS], qbr[:, b, :], ksT[:, SEQ:NT], start=True, stop=True)
                    pe.matmul(ps[rows, 3, NS:2 * NS], qbr[:, b, :], kwT[:, SEQ:NT], start=True, stop=True)
                    pe.matmul(ps[rows, 3, 64:128], qbn[:, b, :], kcT[:, 64 * b:64 * b + 64], start=True, stop=True)
                    for h in range(3):
                        pe.wait_ge(S[f"k_in{b % 3}_{h}"], (64 if h < 2 else 16) * (b // 3 + 1))
                        pe.matmul(ps[rows, h, :], qbr[:, b, :], kbuf[b % 3][:, h, :], start=True, stop=True).then_inc(S["k_scored"], 1)
                pe.wait_ge(S["cn_ready"], s + 1)
                pe.transpose(ps[0:63, 3, 128:256], sc[:, 1600:1663], ident).then_inc(S["cn_turned"], 1)
                pe.wait_ge(S["p4_ready"], s + 1)
                pe.matmul(ps[:, 3, 256:256 + NSEL], pT[0:63, 2080:2208], C("ov")[0:63, :], start=True, stop=True).then_inc(S["blk_mm"], 1)
                if s == 0:
                    pe.wait_ge(S["rg_ready"], 2)
                    for m in range(KC):
                        if m >= 2:
                            pe.wait_ge(S["yc_used"], m - 1)
                        last = project(W_YC + m // 2, 4 + m % 2, zT, 4, (m % 2) * 512)
                        if m % 2:
                            last.then_inc(S["slots_used"], 1)
                pe.wait_ge(S["s_weights"], s + 1)
                for i in range(12):
                    c0 = i * P if i < 8 else 1056 + (i - 8) * P
                    pe.transpose(ps[:, i // 4, (i % 4) * P:(i % 4 + 1) * P], sc[:, c0:c0 + P], ident)
                pe.transpose(ps[0:32, 3, 0:P], sc[:, 1024:1056], ident)
                pe.transpose(ps[0:32, 3, P:2 * P], sc[:, 1568:1600], ident)
                pe.transpose(ps[0:63, 3, 2 * P:3 * P], sc[:, 1664:1727], ident).then_inc(S["sp_turned"], 1)
                pe.wait_ge(S["spT_act"], s + 1)
                pe.wait_ge(S["spT_dve"], s + 1)
                pe.wait_ge(S[f"v_in{s}"], 16 * 9 * SETB)
                o = ps[:, 7, 0:P]
                pe.matmul(o, vnew[0:NS, 2, 0:P], pT[0:NS, 1536:1664], start=True, stop=False, skip_group_check=True)
                pe.matmul(o, vnew[0:NS, 2, P:2 * P], pT[0:NS, 1664:1792], start=False, stop=False, skip_group_check=True)
                for b4 in range(SETB):
                    b = SETB * s + b4
                    o = ps[:, 7, 32 * b4:32 * b4 + 32]
                    pe.matmul(o, vc[0:63, b, :], pT[0:63, 1792 + 32 * b4:1824 + 32 * b4], start=False, stop=False, skip_group_check=True)
                    for i in range(12):
                        v0 = (8 * b4 + i) * P if i < 8 else 4096 + (4 * b4 + i - 8) * P
                        last = pe.matmul(o, vset[s][:, v0:v0 + P], pT[:, i * P + 32 * b4:i * P + 32 * b4 + 32], start=False,
                                         stop=(b4 == 3 and i == 11), skip_group_check=True)
                last.then_inc(S["so_mm"], 1)

            pe.wait_ge(S["so_copied"], 2)
            pe.wait_ge(S["yc_used"], KC)
            for m in range(KC):
                if m >= 2:
                    pe.wait_ge(S["merged"], m - 1)
                last = project(W_YN + m // 2, 4 + m % 2, oT, 4, (m % 2) * 512)
                if m % 2:
                    last.then_inc(S["slots_used"], 1)
            pe.wait_ge(S["merged"], KC)
            for m in range(KC):
                if m >= 2:
                    pe.wait_ge(S["x1_ready"], m - 1)
                project(W_O + m, 2 + m % 2, mg).then_inc(S["slots_used"], 1)
            pe.wait_ge(S["x_squared"], 2)
            sum_squares()

            def split_project(n, bank, it=None):
                at = lambda c: c if it is None else it * (2 * RING) + c
                for h in range(2):
                    pe.wait_ge(S["hi_ready"], at(n + h + 1))
                    for mov in (mov_hi, mov_lo):
                        for k in range(4):
                            last = pe.matmul(ps[:, bank, 0:NT], w_hi[:, h, k * P:(k + 1) * P], mov[:, 4 * h + k, :],
                                             start=(h == 0 and k == 0 and mov is mov_hi), stop=False, skip_group_check=True)
                    last.then_inc(S["hi_used"], 1)
                    pe.wait_ge(S["lo_ready"], at(2 + n + h + 1))
                    for k in range(4):
                        last = pe.matmul(ps[:, bank, 0:NT], w_lo[:, h, k * P:(k + 1) * P], mov_hi[:, 4 * h + k, :],
                                         start=False, stop=(h == 1 and k == 3), skip_group_check=True)
                    last.then_inc(S["lo_used"], 1)

            pe.wait_ge(S["h2_split"], 2)
            for i in range(16):
                if i >= 2:
                    pe.wait_ge(S["qq_copied"], i - 1)
                split_project(staged(W_Q + i), i % 2)
            pe.wait_ge(S["qq_copied"], 16)
            pe.wait_ge(S["sub_in"], 16)
            for t, (n0, n) in enumerate(TILES):
                if t:
                    pe.wait_ge(S["pk_copied"], t)
                for i in range(16):
                    last = pe.matmul(ps[0:n, 4 + i // 4, (i % 4) * P:(i % 4 + 1) * P], rt("qq")[:, i * NT + n0:i * NT + n0 + n],
                                     rt("sub")[:, i * P:(i + 1) * P], start=True, stop=True)
                last.then_inc(S["pk_mm"], 1)

            def expert_tile(it, j0, s):
                pe.wait_ge(S["u_free"], it * RING + (j0 + s + 1))
                split_project(staged(W_U + j0 + s), s % 2, it)

            def routing(it, half, g):
                pe.wait_ge(S["oh_ready"], it * 2 + (32 * half + g + 1))
                pe.wait_ge(S["w_free"], it * 2 + (32 * half + g + 1))
                for x in range(GT):
                    at = x * HALF
                    last = pe.matmul(ps[:, 2 + at // 512, at % 512:at % 512 + HALF], oh[:, x, 0:P], oh[:, x, P:P + HALF], start=True, stop=True)
                last.then_inc(S["route_mm"], 1)

            with pe.Fori(0, HALF // RING) as it:
                for s in range(RING):
                    expert_tile(it, 0, s)
            pe.wait_ge(S["routed"], 3)
            for t, (n0, n) in enumerate(TILES):
                for i in range(3):
                    last = pe.transpose(ps[:, 5 + i, n0:n0 + n], rt("gi")[0:n, (3 * t + i) * P:(3 * t + i + 1) * P], ident[0:n, 0:n])
            last.then_inc(S["route_turned"], 1)
            with pe.Fori(0, HALF // RING) as it:
                for s in range(RING):
                    expert_tile(it, HALF, s)
                    if s % 2 == 0:
                        routing(it, 0, s // 2)
            pe.wait_ge(S["u_free"], 2 + PK)
            for q in range(4):
                if q:
                    pe.wait_ge(S["y_ready"], q)
                for m in range(4):
                    pe.matmul(ps[:, VBANK[m], 0:NT], zero16[:, 0:P], zero16[:, :], start=True, stop=False, skip_group_check=True)
                with pe.Fori(0, 8) as it:
                    for s in range(RING):
                        n = staged(W_V + 32 * q + s)
                        pe.wait_ge(S["mov_ready"], it * RING + (32 * q + s + 1))
                        for h in range(2):
                            pe.wait_ge(S["hi_ready"], it * (2 * RING) + (n + h + 1))
                            for m in range(4):
                                for mov in (mov_hi, mov_lo):
                                    last = pe.matmul(ps[:, VBANK[m], 0:NT], w_hi[:, h, m * P:(m + 1) * P], mov[:, 2 * s + h, :],
                                                     start=False, stop=False, skip_group_check=True)
                            last.then_inc(S["hi_used"], 1)
                            pe.wait_ge(S["lo_ready"], it * (2 * RING) + (2 + n + h + 1))
                            for m in range(4):
                                last = pe.matmul(ps[:, VBANK[m], 0:NT], w_lo[:, h, m * P:(m + 1) * P], mov_hi[:, 2 * s + h, :],
                                                 start=False, stop=False, skip_group_check=True)
                            last.then_inc(S["lo_used"], 1)
                        if q < 2 and s % 2 == 0:
                            routing(it, 1, 16 * q + s // 2)


def constants():
    f = np.float32
    c = np.zeros((P, NCONST), f)

    def put(name, x):
        a, b = CONST[name]
        c[:x.shape[0], a:b] = x

    pos = np.concatenate([np.arange(SEQ), np.tile(PAST + np.arange(NQ), NB)]).astype(f)
    inv = np.power(f(10000.0), -np.arange(HD // 2, dtype=f) * f(2.0) / f(HD)).astype(f)
    ang = (pos[:, None] * inv[None, :]).astype(f)
    cos, sin = np.cos(ang).astype(f), np.sin(ang).astype(f)
    cc, ss = np.zeros((P, 3 * HD), f), np.zeros((P, 3 * HD), f)
    for t, (n0, n) in enumerate(TILES):
        cc[:n, t * HD:(t + 1) * HD] = np.concatenate([cos[n0:n0 + n]] * 2, 1)
        ss[:n, t * HD:(t + 1) * HD] = np.concatenate([-sin[n0:n0 + n], sin[n0:n0 + n]], 1)
    put("ident", np.eye(P, dtype=f))
    put("iota", np.tile(np.arange(P, dtype=f), (P, 1)))
    put("ones", np.ones((P, P), f))
    put("cos", cc)
    put("sin", ss)
    row = np.arange(P)
    tri = np.where(row[None, :] <= row[:, None], 0, NEG).astype(f)
    put("causal", np.concatenate([np.zeros((P, P), f), tri], 1))
    end = np.arange(16) * STRIDE + 2 * STRIDE - 1
    ok = (end[None, None, :] <= (row[:, None] + P * np.arange(2)[None, :])[:, :, None]) & (np.arange(16) < 15)
    put("cmpmask", np.where(ok, 0, NEG).astype(f).reshape(P, 32))
    rb, rq = row // 32, row % 16 // R
    nm = np.full((P, 2, NB, NQ), NEG, f)
    for s in range(2):
        for p in range(P):
            nm[p, s, SETB * s + rb[p], :rq[p] + 1] = 0
    put("newmask", nm.reshape(P, 2 * NS))
    put("winmask", np.where(np.arange(NQ)[None, :] > rq[:, None], 0, NEG).astype(f))
    c0, s0 = np.arange(63)[:, None] * STRIDE, np.arange(NSEL)[None, :] * BLK
    put("ov", (np.clip(np.minimum(c0 + 2 * STRIDE, s0 + BLK) - np.maximum(c0, s0), 0, None) / STRIDE).astype(f))
    forced = np.zeros(NSEL, f)
    forced[[0, NSEL - 2, NSEL - 1]] = 1e4
    put("forced", np.tile(forced, (P, 1)))
    put("jp1", np.tile(np.arange(1, NSEL + 1, dtype=f), (P, 1)))
    rep = np.zeros((NS, 2, P), f)
    for s in range(2):
        rep[(SETB * s + rb) * NQ + rq, s, row] = 1
    put("rep", rep.reshape(NS, 2 * P))
    put("gsel", (np.arange(NH)[None, :] == (row % 32 // 16 * R + row % R)[:, None]).astype(f))
    put("iota16", np.tile(np.arange(PTOP, dtype=f), (P, 1)))
    return c


def kernel(x_prompt, x_sample, cache_cmp_k, cache_cmp_v, cache_slc_k, cache_slc_v, cache_win_k, cache_win_v, state_conv,
           page_table, norm_mix, w_in, conv_w, cmp_pos_k, cmp_w1_k, cmp_b1_k, cmp_w2_k, cmp_pos_v, cmp_w1_v, cmp_b1_v,
           cmp_w2_v, q_norm, k_norm_cmp, k_norm_slc, k_norm_win, w_out_conv, w_out_nsa, w_o, norm_ffn, peer_wq,
           peer_sub_keys, peer_u, peer_v):
    import concourse.bacc as _bacc
    from concourse.bass_utils import run_bass_kernel_spmd as _run

    a = np.asarray
    x = np.concatenate([a(x_prompt)[0], a(x_sample).reshape(NS, D)], 0)
    w = a(w_in)[0]
    cut = np.cumsum([0, 512, 512, 512, 512, P, P, P, P, P, P, 24, 2048])
    cb, cc, ch, q, kc, vc, ks, vs, kw, vw, ng, mg = (w[:, cut[i]:cut[i + 1]] for i in range(12))
    q = q.reshape(D, NG, R, HD).transpose(0, 2, 1, 3).reshape(D, 512)
    tok = np.concatenate([q, ks, kw, kc, vc, vs, vw, ng], 1)

    def chunks(m):
        k, n = m.shape
        return m.reshape(k // P, P, n // P, P).transpose(2, 1, 0, 3).reshape(n // P, P, k // P * P)

    feed = {"xT": x.T.reshape(KC, P, NT).transpose(1, 0, 2), "consts": constants()}
    for p, (c0, n) in enumerate(PIECES):
        feed[f"wtok{p}"] = tok[:, c0:c0 + n].reshape(4, 2, P, n).transpose(0, 2, 1, 3).reshape(4, P, 2 * n)
    conv = np.stack([cc.reshape(D, 4, P), ch.reshape(D, 4, P), cb.reshape(D, 4, P)], 2).reshape(D, 12 * P)
    feed["wT"] = np.concatenate([chunks(conv), chunks(mg)], 0)
    pair = lambda m: chunks(m).reshape(4, 2, P, 512).transpose(0, 2, 1, 3).reshape(4, P, 1024)
    nsa = a(w_out_nsa)[0].reshape(NG, R, HD, D).transpose(1, 0, 2, 3).reshape(512, D)
    feed["wout"] = np.concatenate([pair(a(w_out_conv)[0]), pair(nsa), chunks(a(w_o)[0]), chunks(a(peer_wq)[0])], 0)
    w1 = np.stack([a(cmp_w1_k)[0], a(cmp_w1_v)[0]])
    feed["w1"] = w1.reshape(2, 16, 2 * HD, P).transpose(2, 0, 1, 3).reshape(P, 4096)
    pos = np.stack([a(cmp_pos_k)[0], a(cmp_pos_v)[0]])
    state = a(state_conv)[0].reshape(NB, 2, 4, P).transpose(3, 2, 0, 1).reshape(P, 4 * NB * 2)
    gain = np.concatenate([np.tile(a(q_norm)[0], 8), np.tile(a(k_norm_slc)[0], 2), np.tile(a(k_norm_win)[0], 2)])
    feed["smalls"] = np.concatenate([
        a(norm_mix)[0].reshape(KC, P).T, a(norm_ffn)[0].reshape(KC, P).T,
        a(conv_w)[0].reshape(3, 4, P).transpose(2, 0, 1).reshape(P, 12), np.stack([a(cmp_b1_k)[0], a(cmp_b1_v)[0]], 1),
        pos.reshape(2, 16, 2 * HD).transpose(2, 0, 1).reshape(P, 32), state, np.tile(gain, (P, 1)),
        np.tile(a(k_norm_cmp)[0], (P, 1)), a(cmp_w2_k)[0], a(cmp_w2_v)[0]], 1)
    assert feed["smalls"].shape == (P, NSMALL)
    pt = a(page_table)
    feed["pages"] = pt.reshape(1, 64)
    for n, c in (("cmp_k", cache_cmp_k), ("cmp_v", cache_cmp_v)):
        feed["cache_" + n] = a(c).reshape(NPOOL, 8, 8, 2, NG, HD).transpose(0, 3, 5, 2, 4, 1).reshape(NPOOL, P, P)
    feed["cache_slc_k"] = a(cache_slc_k).reshape(NPOOL, PAGE, P).transpose(0, 2, 1)
    feed["cache_slc_v"] = a(cache_slc_v).reshape(NPOOL, PAGE, P)
    feed["cache_win_kT"] = a(cache_win_k).reshape(NB, WINDOW, P).transpose(0, 2, 1)
    for n, c in (("win_k", cache_win_k), ("win_v", cache_win_v)):
        feed["cache_" + n] = a(c).reshape(NB, WINDOW, P)
    feed["sub"] = a(peer_sub_keys)[0].reshape(16, P, P).transpose(2, 0, 1).reshape(P, 2048)
    feed["uT"] = a(peer_u)[0].reshape(PK, PK, KC, P).transpose(1, 3, 2, 0).reshape(PK, P, D)
    feed["v"] = a(peer_v)[0].reshape(PK, 2, 32, 2, 2, 512).transpose(1, 4, 2, 0, 3, 5).reshape(PK, P, 1024)

    nc = _bacc.Bacc("TRN2", target_bir_lowering=False, num_devices=1)
    arrays, A, O = {}, {}, {}
    for name, v in feed.items():
        v = np.ascontiguousarray(v)
        arrays["in_" + name] = v
        A[name] = nc.dram_tensor("in_" + name, v.shape, mybir.dt.from_np(v.dtype), kind="ExternalInput").ap()
    shapes = {"yT": (P, KC, NT), "kc": (NT, P), "vc": (NT, P), "ks": (NT, P), "vs": (NT, P), "kw": (SEQ, P), "vw": (SEQ, P),
              "wk": (NB, WINDOW, P), "wv": (NB, WINDOW, P), "cstate": (P, 4 * 18)}
    for name, shape in shapes.items():
        O[name] = nc.dram_tensor("out_" + name, shape, F32, kind="ExternalOutput").ap()
    program(nc, A, O)
    r = _run(nc, [arrays], core_ids=[0]).results[0]
    got = {name: a(r["out_" + name]) for name in shapes}
    y = got["yT"].transpose(1, 0, 2).reshape(D, NT).T
    cs = got["cstate"].reshape(P, 4, 18).transpose(2, 1, 0).reshape(18, 512)
    new = lambda n: got[n][SEQ:].reshape(1, NB, NQ, NG, HD)
    old = lambda n: got[n][:SEQ].reshape(1, 1, SEQ, NG, HD)
    win = lambda n: got[n].reshape(1, NB, WINDOW, NG, HD)
    return tuple(np.ascontiguousarray(v) for v in (
        y[:SEQ].reshape(1, SEQ, D), y[SEQ:].reshape(NB, NQ, D),
        old("kc"), old("vc"), old("ks"), old("vs"), old("kw"), old("vw"), cs[:2].reshape(1, 1, 2, 512),
        new("kc"), new("vc"), new("ks"), new("vs"), win("wk"), win("wv"), cs[2:].reshape(1, NB, 2, 512)))
```

```python
from contextlib import ExitStack

import numpy as np

import concourse.bass as bass
from concourse import mybir

D = 1024
SEQ = 256
NB = 8
NQ = 4
PAST = 1024
PAGE = 128
NPOOL = 80
NH, NG, R = 8, 2, 4
HD = 64
STRIDE = 16
WINDOW = 512
BLK = 64
NSEL = 17
PH, PK, PTOP = 8, 128, 16
EPS = 1e-6
NEG = -1e30
P = 128
NS = NB * NQ
NT = SEQ + NS
KC = D // P
TILES = [(0, P), (P, P), (2 * P, NS)]
QKV = 12 * HD + 4 * NG * HD + 3 * NH
PIECES = [(0, 512), (512, 512), (1024, QKV - 1024)]
PAGES = PAST // PAGE
SETB = 4
SCALE = HD ** -0.5
RING = 4
HALF = PK // 2
GT = 9
VBANK = (4, 5, 6, 7)

F32 = mybir.dt.float32
F32R = mybir.dt.float32r
BF16 = mybir.dt.bfloat16
I32 = mybir.dt.int32
U32 = mybir.dt.uint32
ALU = mybir.AluOpType
ACT = mybir.ActivationFunctionType
AX = mybir.AxisListType

C_KC, C_VC, C_VS, C_NG = 768, 896, 1024, 1280

W_TOK, W_CONV, W_MG, W_YC, W_YN, W_O, W_Q, W_U, W_V, W_END = 0, 12, 24, 40, 44, 48, 56, 72, 200, 328


def columns(parts):
    at, out = 0, {}
    for name, n in parts:
        out[name] = (at, at + n)
        at += n
    return out, at


CONST, NCONST = columns([("iota", P), ("ident", P), ("ones", P), ("cos", 3 * HD), ("sin", 3 * HD), ("causal", 2 * P),
                         ("cmpmask", 32), ("newmask", 2 * NS), ("winmask", NQ), ("ov", NSEL), ("forced", NSEL),
                         ("jp1", NSEL), ("rep", 2 * P), ("gsel", NH), ("iota16", PTOP)])
SMALL, NSMALL = columns([("norm_mix", KC), ("norm_ffn", KC), ("conv_w", 12), ("b1", 2), ("pos", 32),
                         ("state", 4 * NB * 2), ("gain", 12 * HD), ("kcgain", HD), ("w2", 2 * HD)])

ARENA = PK * NT
AR, USED = columns([("a", 10752), ("b", 6984), ("qnT", 1024), ("qrT", 1024), ("qbn", 256), ("qbr", 256), ("ksT", NT),
                    ("kwT", NT), ("z", 4 * NT), ("oT", 4 * NT), ("up", 4 * 258), ("us", 4 * NB * 6), ("vnew", 768),
                    ("kcT", 4 * P + 16), ("vc", 9 * P), ("sec", 256), ("hid", 256), ("kcn", 5 * P),
                    ("vset", 6144), ("kring", 1536), ("xcp", 512), ("rr", 2 * NT)])
assert USED <= ARENA, (USED, ARENA)
UP0 = HALF * NT
RT, USED = columns([("qq", 16 * NT), ("sub", 2048), ("sp", 3 * 2048), ("lv", 256), ("li", 256), ("lf", 256),
                    ("tv", 128), ("ti", 128), ("ab", 256), ("abf", 256), ("gi", 9 * P), ("z8", 16), ("rr", 2 * NT)])
RT["cand"], RT["eq"] = (0, 2048), (2048, 4096)
assert USED <= HALF * NT, USED
STATS = NCONST + NSMALL
LISTS, HOT = P, P + 3 * NT
AUX = max(STATS + 96 + 9 * NH + 8, HOT + GT * (P + HALF))


UNITS = [(t, v) for v in range(2) for t in range(5)]
PAGED = [u for u, (t, v) in enumerate(UNITS) if t < 4]


assert GT * P == KC // 2 * NT


def staged(i):
    return 2 * (i - W_Q)


def program(nc, A, O):
    with ExitStack() as ctx:
        def sb(name, shape, dt=F32):
            return ctx.enter_context(nc.sbuf_tensor(name, shape, dt))

        def sem(name):
            return ctx.enter_context(nc.semaphore(name))

        ps = ctx.enter_context(nc.psum_tensor("ps", [P, 8, 512], F32))
        aux = sb("aux", [P, AUX])
        cst, sml = aux[:, 0:NCONST], aux[:, NCONST:STATS]
        ring = sb("ring", [P, RING, 1024])
        xT = sb("xT", [P, KC, NT])
        mov_hi, mov_lo = sb("mov_hi", [P, KC, NT], F32R), sb("mov_lo", [P, KC, NT], F32R)
        w_hi, w_lo = sb("w_hi", [P, 2, 512], F32R), sb("w_lo", [P, 2, 512], F32R)
        ptab = sb("ptab", [1, 64], I32)
        oh = aux[:, HOT:HOT + GT * (P + HALF)].rearrange("p (x c) -> p x c", x=GT)
        zero16 = sb("zero16", [P, NT], BF16)
        arena = sb("arena", [P, ARENA])
        st = aux[:, STATS:STATS + 96]
        sg = aux[:, STATS + 96:STATS + 96 + 9 * NH].rearrange("p (t c) -> p t c", t=3)
        rg = aux[:, STATS + 96 + 9 * NH:STATS + 102 + 9 * NH]
        bias = aux[:, STATS + 102 + 9 * NH:STATS + 104 + 9 * NH]

        def C(name, n=P):
            a, b = CONST[name]
            return cst[0:n, a:b]

        def M(name):
            a, b = SMALL[name]
            return sml[:, a:b]

        def ar(name, lo=0, n=None):
            a, b = AR[name]
            return arena[:, a + lo:(b if n is None else a + lo + n)]

        def rt(name):
            a, b = RT[name]
            return arena[:, UP0 + a:UP0 + b]

        def over(x, axis, n):
            y = x.unsqueeze(axis)
            shape = list(y.shape)
            shape[axis] = n
            return y.broadcast_to(shape)

        ident = C("ident")
        rr = ar("rr").rearrange("p (i n) -> p i n", i=2)
        rr2 = rt("rr").rearrange("p (i n) -> p i n", i=2)
        h2 = arena[:, 0:KC * NT].rearrange("p (k n) -> p k n", k=KC)
        ptok = ar("b", 0, 3 * QKV).rearrange("p (t c) -> p t c", t=3)
        qn = ar("b", 3 * QKV, 768)
        qr = ar("b", 3 * QKV + 768, 768)
        tmpq = ar("b", 3 * QKV + 1536, 768)
        xsq = ar("b", 0, KC * NT).rearrange("p (k n) -> p k n", k=KC)
        xsq2 = ar("vset", 0, KC * NT).rearrange("p (k n) -> p k n", k=KC)
        mg = ar("b", 0, 16 * NT).rearrange("p (k n) -> p k n", k=16)
        mt = ar("b", 16 * NT, NT)
        w1 = ar("a", 0, 4096).rearrange("p (v k f) -> p v k f", v=2, k=16)
        xc = ar("a", 4096, 6144).rearrange("p (i j k g c) -> p i j k g c", i=3, j=16, k=8, g=NG)
        xcp = ar("xcp").rearrange("p (v k g c) -> p v k g c", v=2, k=8, g=NG)
        sc = ar("a", 0, 2048)
        pT = ar("a", 2048, 2560)
        vset = [ar("vset"), ar("a", 4608, 6144)]
        qnT = ar("qnT").rearrange("p (r n) -> p r n", r=R)
        qrT = ar("qrT").rearrange("p (r n) -> p r n", r=R)
        qbn = ar("qbn").rearrange("p (b m) -> p b m", b=NB)
        qbr = ar("qbr").rearrange("p (b m) -> p b m", b=NB)
        ksT, kwT = ar("ksT"), ar("kwT")
        zT = ar("z").rearrange("p (k n) -> p k n", k=4)
        oT = ar("oT").rearrange("p (r n) -> p r n", r=R)
        up = ar("up").rearrange("p (k n) -> p k n", k=4)
        us = ar("us").rearrange("p (k b n) -> p k b n", k=4, b=NB)
        vnew = ar("vnew").rearrange("p (t c) -> p t c", t=3)
        kcT = ar("kcT")
        vc = ar("vc").rearrange("p (b c) -> p b c", c=P)
        sec, hid = ar("sec"), ar("hid")
        kcn = ar("kcn").rearrange("p (t c) -> p t c", c=P)

        class Sems(dict):
            def __missing__(self, name):
                self[name] = sem(name)
                return self[name]

        S = Sems()
        ring_in = [sem(f"ring_in{i}") for i in range(RING)]

        def link_on(eng, s):
            count = [0]

            def link(ins):
                count[0] += 1
                ins.then_inc(s, 1)
                eng.wait_ge(s, count[0])
            return link

        kplaces = [[ar("kring", 512 * h, 512) for h in range(3)], [ar("qnT", 512 * h, 512) for h in range(3)],
                   [ar("up", 0, 512), ar("up", 512, 512), ar("kcn", 0, 512)], [ar("qnT", 1536, 512), ar("xcp"), ar("sec", 0, 512)]]

        def load_chunks(eng, i):
            t, v = UNITS[PAGED[i]]
            if i >= 3:
                eng.wait_ge(S["comp_mm"], PAGED[i - 3] + 1)
            for j in range(16):
                page = eng.value_load(ptab[0:1, 16 * t + j:16 * t + j + 1], min_val=0, max_val=NPOOL - 1)
                eng.dma_start(xc[:, i % 3, j, :, :, :].rearrange("p k g c -> p (k g c)"),
                              A["cache_cmp_" + "kv"[v]][bass.ds(page, 1)].rearrange("o p c -> (o p) c")).then_inc(S[f"xc_in{i % 6}"], 16)

        def load_keys(eng, b, h):
            if b >= 4:
                eng.wait_ge(S["k_scored"], 3 * (b - 4) + h + 1)
            elif b == 2:
                eng.wait_ge(S["kcn_turned"], 5)
                eng.wait_ge(S["comp_out"], 10)
            elif b:
                eng.wait_ge(S["p_scored"], 4)
            if h == 2:
                eng.dma_start(kplaces[b % 4][2], A["cache_win_kT"][b]).then_inc(S[f"k_in{b % 4}_2"], 16)
                return
            for p in range(4):
                at = b * PAGES + 4 * h + p
                page = eng.value_load(ptab[0:1, at:at + 1], min_val=0, max_val=NPOOL - 1)
                eng.dma_start(kplaces[b % 4][h][:, p * P:(p + 1) * P], A["cache_slc_k"][bass.ds(page, 1)].rearrange("o p c -> (o p) c"))\
                    .then_inc(S[f"k_in{b % 4}_{h}"], 16)

        hot_first = mov_hi[:, 4:8, :].rearrange("p k n -> p (k n)").rearrange("p (x c) -> p x c", x=GT)
        hot_second = mov_lo[:, 4:8, :].rearrange("p k n -> p (k n)").rearrange("p (x c) -> p x c", x=GT)
        hot_eq = aux[:, HOT:HOT + GT * HALF].rearrange("p (x c) -> p x c", x=GT)
        hot_sum = aux[:, HOT + GT * HALF:HOT + 2 * GT * HALF].rearrange("p (x c) -> p x c", x=GT)
        route_parts = ps[:, 1:4, :].rearrange("p b c -> p (b c)")[:, 0:GT * P].rearrange("p (n j) -> p n j", n=GT)
        gT_low = aux[:, HOT + 2 * GT * HALF:HOT + 2 * GT * HALF + NT]

        block = ctx.enter_context(nc.Block())

        def slot_ready(eng, i):
            eng.wait_ge(ring_in[i % RING], 16 * (i // RING + 1))

        @block.sync
        def _(sp):
            for i in range(4):
                sp.dma_start(xT[:, 2 * i:2 * i + 2, :], A["xT"][:, 2 * i:2 * i + 2, :]).then_inc(S[f"x_in{i}"], 16)

            def load(i):
                if i >= W_Q + RING:
                    sp.wait_ge(S["lo_ready"], 2 + staged(i - RING + 1))
                elif i >= RING:
                    sp.wait_ge(S["slots_used"], i - RING + 1)
                if i < W_CONV:
                    w = PIECES[i // 4][1]
                    sp.dma_start(ring[:, i % RING, 0:2 * w], A[f"wtok{i // 4}"][i % 4]).then_inc(ring_in[i % RING], 16)
                    return
                src = A["wT"][i - W_CONV] if i < W_YC else A["wout"][i - W_YC]
                sp.dma_start(ring[:, i % RING, :], src).then_inc(ring_in[i % RING], 16)

            for i in range(W_CONV):
                load(i)
                if i == RING - 1:
                    sp.dma_start(ar("a", 0, 4096), A["w1"]).then_inc(S["w1_in"], 16)
                    sp.wait_ge(S["ptab_in"], 16)
                    load_chunks(sp, 0)
                if i == 2 * RING - 1:
                    load_keys(sp, 0, 1)
                    load_keys(sp, 0, 2)
            for i in range(W_CONV, W_U):
                if i == W_MG:
                    load_chunks(sp, 4)
                if i == W_MG + RING:
                    load_chunks(sp, 6)
                load(i)
                if i == W_YC - RING:
                    load_keys(sp, 2, 1)
                    load_keys(sp, 2, 2)
                if i == W_YC:
                    for b in (1, 3):
                        load_keys(sp, b, 1)
                        load_keys(sp, b, 2)
                if i == W_YN - 1:
                    sp.dma_start(xT[:, :, :], A["xT"]).then_inc(S["x_again"], 16)
                    for b in range(4, NB):
                        load_keys(sp, b, 1)
                        load_keys(sp, b, 2)
                if i == W_Q - 1:
                    sp.dma_start(rt("sub"), A["sub"]).then_inc(S["sub_in"], 16)
            with sp.Fori(0, PK // RING) as it:
                for s in range(RING):
                    sp.wait_ge(S["lo_ready"], it * (2 * RING) + (2 + staged(W_U - RING + s + 1)))
                    sp.dma_start(ring[:, s, :], A["uT"][bass.ds(it * RING + s, 1)].rearrange("o p c -> (o p) c")).then_inc(ring_in[s], 16)
            with sp.Fori(0, PK // RING) as it:
                for s in range(RING):
                    sp.wait_ge(S["lo_ready"], it * (2 * RING) + (2 + staged(W_V - RING + s + 1)))
                    sp.dma_start(ring[:, s, :], A["v"][bass.ds(it * RING + s, 1)].rearrange("o p c -> (o p) c")).then_inc(ring_in[s], 16)
            for q in range(2):
                sp.wait_ge(S["y_ready"], 3 + q)
                sp.dma_start(O["yT"][:, 4 * q:4 * q + 4, :], xT[:, 4 * q:4 * q + 4, :]).then_inc(S["y_out"], 16)
            sp.wait_ge(S["y_out"], 32)

        @block.gpsimd
        def _(pool):
            pool.memset(ar("qbn"), 0.0).then_inc(S["u_free"], 2)
            pool.memset(ar("qbr"), 0.0).then_inc(S["hi_used"], 2)
            pool.memset(up[:, :, 0:2], 0.0).then_inc(S["w_free"], 1)
            pool.memset(hid[:, 0:128], 0.0).then_inc(S["lo_used"], 2)
            pool.memset(hid[:, 128:256], 0.0).then_inc(S["lo_ready"], 2)
            pool.memset(zero16[:, :], 0.0).then_inc(S["zeroed"], 1)
            pool.dma_start(ptab[:, :], A["pages"]).then_inc(S["ptab_in"], 16)
            pool.wait_ge(S["ptab_in"], 16)

            def load_values(s):
                for b4 in range(SETB):
                    b = SETB * s + b4
                    for p in range(PAGES):
                        page = pool.value_load(ptab[0:1, b * PAGES + p:b * PAGES + p + 1], min_val=0, max_val=NPOOL - 1)
                        pool.dma_start(vset[s][:, (b4 * 8 + p) * P:(b4 * 8 + p + 1) * P],
                                       A["cache_slc_v"][bass.ds(page, 1)].rearrange("o p c -> (o p) c")).then_inc(S[f"v_in{s}"], 16)
                    pool.dma_start(vset[s][:, 4096 + b4 * 512:4096 + (b4 + 1) * 512].rearrange("p (t c) -> p t c", t=4),
                                   A["cache_win_v"][b].rearrange("(t p) c -> p t c", p=P)).then_inc(S[f"v_in{s}"], 16)

            load_chunks(pool, 1)
            load_keys(pool, 0, 0)
            load_values(0)
            for i in (3, 5, 7):
                load_chunks(pool, i)
            for v in range(2):
                pool.dma_start(O[["wk", "wv"][v]][:, 0:WINDOW - NQ, :], A["cache_win_" + "kv"[v]][:, NQ:WINDOW, :])\
                    .then_inc(S["win_kept"], 16)
            pool.wait_ge(S["comp_mm"], 10)
            load_values(1)
            for b in (2, 1, 3, 4, 5, 6, 7):
                load_keys(pool, b, 0)
            pool.wait_ge(S["win_kept"], 32)

            def split_low(s, n, it=None, step=0):
                at = lambda c: c if it is None else it * step + c
                for h in range(2):
                    pool.wait_ge(S["hi_ready"], at(n + h + 1))
                    pool.wait_ge(S["lo_used"], at(n + h + 1))
                    pool.tensor_tensor(w_lo[:, h, :], ring[:, s, h * 512:(h + 1) * 512], w_hi[:, h, :].bitcast(F32), ALU.subtract)\
                        .then_inc(S["lo_ready"], 1)

            with pool.Fori(0, (W_END - W_Q) // RING) as it:
                for s in range(RING):
                    split_low(s, 2 * s, it, 2 * RING)

        @block.scalar
        def _(act):
            act.dma_start(cst[:, :], A["consts"]).then_inc(S["consts_in"], 16)
            act.dma_start(sml[:, :], A["smalls"]).then_inc(S["smalls_in"], 16)
            for i in range(4):
                act.wait_ge(S[f"x_in{i}"], 16)
                act.activation(xsq[:, 2 * i:2 * i + 2, :], xT[:, 2 * i:2 * i + 2, :], ACT.Square).then_inc(S["x_squared"], 1)
            act.wait_ge(S["x_var"], 1)
            act.activation(rr[:, 1, :], rr[:, 0, :], ACT.Sqrt).then_inc(S["x_std"], 1)
            act.wait_ge(S["ptab_in"], 16)
            load_chunks(act, 2)
            for p, (c0, w) in enumerate(PIECES):
                act.wait_ge(S["slots_used"], 4 * (p + 1))
                for t, (n0, n) in enumerate(TILES):
                    act.activation(ptok[0:n, t, c0:c0 + w], ps[0:n, 3 * (p % 2) + t, 0:w], ACT.Copy).then_inc(S["tok_copied"], 1)
            def copy_cc(c):
                act.wait_ge(S["slots_used"], W_CONV + 3 * c + 1)
                if c:
                    act.wait_ge(S["u_ready"], c)
                act.activation(rr[:, 1, :], ps[:, 5, 0:NT], ACT.Copy).then_inc(S["cc_copied"], 1)

            for t, (n0, n) in enumerate(TILES):
                act.wait_ge(S["qk_var"], t + 1)
                act.activation(st[0:n, 16:28], st[0:n, 0:12], ACT.Sqrt).then_inc(S["qk_std"], 1)
                act.wait_ge(S["tok_copied"], 9)
                for name, c in (("kc", C_KC), ("vc", C_VC)):
                    act.dma_start(O[name][n0:n0 + n, :], ptok[0:n, t, c:c + P]).then_inc(S["kv_rows_out"], 16)
                act.dma_start(O["vs"][n0:n0 + n, :], ptok[0:n, t, C_VS:C_VS + P]).then_inc(S["rows_out"], 16)
                copy_cc(t)
                act.wait_ge(S["qk_ready"], t + 1)
                act.dma_start(O["ks"][n0:n0 + n, :], qr[0:n, 512:640]).then_inc(S["k_rows_out"], 16)
                for v, src in enumerate([qr[0:n, 640:768], ptok[0:n, t, C_VS + P:C_VS + 2 * P]]):
                    done = S[["k_rows_out", "rows_out"][v]]
                    if t < 2:
                        act.dma_start(O[["kw", "vw"][v]][n0:n0 + n, :], src).then_inc(done, 16)
                    else:
                        act.dma_start(O[["wk", "wv"][v]][:, WINDOW - NQ:WINDOW, :], src).then_inc(done, 16)
                act.wait_ge(S["qk_turned"], t + 1)
                if t < 2:
                    act.activation(qnT[:, :, n0:n0 + n], ps[:, 0, :].rearrange("p (r n) -> p r n", r=R), ACT.Copy)
                    act.activation(qrT[:, :, n0:n0 + n], ps[:, 1, :].rearrange("p (r n) -> p r n", r=R), ACT.Copy)
                    for v in range(2):
                        for g in range(NG):
                            for s2 in range(2):
                                act.activation(xcp[64 * s2:64 * s2 + 64, v, :, g, 8 * t:8 * t + 8],
                                               ps[64 * g:64 * g + 64, 2, 256 + v * P:256 + (v + 1) * P]
                                               .rearrange("p (c k s) -> p s k c", k=8, s=2)[:, s2, :, :], ACT.Copy)
                else:
                    act.wait_ge(S["zeroed"], 1)
                    for i, q in enumerate((qbn, qbr)):
                        for g in range(NG):
                            for r in range(R):
                                act.activation(
                                    q[64 * g:64 * g + 64, :, 16 * g:16 * g + 16].rearrange("p b (q r) -> p b q r", r=R)[:, :, :, r],
                                    ps[64 * g:64 * g + 64, i, r * P:r * P + NS].rearrange("p (b q) -> p b q", b=NB), ACT.Copy)
                act.activation(ksT[:, n0:n0 + n], ps[:, 2, 0:n], ACT.Copy)
                act.activation(kwT[:, n0:n0 + n], ps[:, 2, P:P + n], ACT.Copy).then_inc(S["qT_copied"], 1)
            copy_cc(3)
            for t, (n0, n) in enumerate(TILES):
                act.activation(sg[0:n, t, :], ptok[0:n, t, C_NG:C_NG + 24], ACT.Exp, scale=-1.0).then_inc(S["gate_exp"], 1)
            act.wait_ge(S["u_ready"], 4)
            cstate = O["cstate"].rearrange("p (k n) -> p k n", k=4)
            act.dma_start(cstate[:, :, 0:2], up[:, :, 256:258]).then_inc(S["conv_out"], 16)
            for k in range(4):
                act.dma_start(cstate[:, k, 2:18].rearrange("p (b n) -> p b n", b=NB), us[:, k, :, 4:6]).then_inc(S["conv_out"], 16)
            for name, count in (("kv_rows_out", 6), ("rows_out", 6), ("k_rows_out", 6), ("conv_out", 5)):
                act.wait_ge(S[name], 16 * count)
            act.wait_ge(S["vnew_ready"], 3)

            for u, (t, v) in enumerate(UNITS):
                n = P if t < 4 else 16
                if u == 6:
                    act.wait_ge(S["kcn_var"], 1)
                    act.activation(st[:, 16:26], st[:, 0:10], ACT.Sqrt).then_inc(S["kcn_std"], 1)
                if u:
                    act.wait_ge(S["hid_ready"], u)
                act.wait_ge(S["comp_mm"], u + 1)
                act.activation(sec[:, 0:2 * n], ps[:, 3 + u % 2, 256:256 + 2 * n], ACT.Copy).then_inc(S["sec_copied"], 1)
                act.wait_ge(S["hid_sum"], u + 1)
                if u:
                    act.wait_ge(S["comp_out"], u)
                L = 64 if t < 4 else 16
                view = lambda x: x[:, 0:2 * n].rearrange("p (g c) -> p g c", c=L)[:, :, 0:L - 1]
                act.activation(view(hid), view(sec), ACT.Gelu, bias=bias[:, v:v + 1]).then_inc(S["hid_ready"], 1)
                act.wait_ge(S["comp_out"], u + 1)
                if v == 0:
                    act.activation(kcn[0:n, t, :], ps[0:n, 5, 0:P], ACT.Copy).then_inc(S["cmp_copied"], 1)
                elif t < 4:
                    act.activation(vc[0:64, 2 * t:2 * t + 2, :], ps[0:64, 5, 0:256].rearrange("p (b c) -> p b c", b=2), ACT.Copy)\
                        .then_inc(S["cmp_copied"], 1)
                else:
                    act.activation(vc[0:16, 8, :], ps[0:16, 5, 0:P], ACT.Copy).then_inc(S["cmp_copied"], 1)
                if u == 7:
                    for t in range(5):
                        n = P if t < 4 else 16
                        act.wait_ge(S["kcn_turned"], t + 1)
                        act.activation(kcT[:, t * P:t * P + n], ps[:, 6 + t % 2, 0:n], ACT.Copy).then_inc(S["kcT_copied"], 1)

            for u in range(4):
                qt, g = u // 2, u % 2
                nk = P * (qt + 1)
                for c in range(4):
                    i = 4 * u + c
                    act.wait_ge(S["slots_used"], W_MG + i + 1)
                    act.activation(mg[:, i, :], ps[:, 6 + i % 2, 0:NT], ACT.Exp, scale=-1.0).then_inc(S["mg_exp"], 1)
                    if c == 0:
                        act.wait_ge(S["pc_shift"], u + 1)
                        act.activation(st[:, 32:96], st[:, 32:96], ACT.Exp).then_inc(S["pc_exp"], 1)
                        act.wait_ge(S["ps_max"], u + 1)
                        for i8 in range(8):
                            last = act.activation(sc[:, i8 * nk:(i8 + 1) * nk], sc[:, i8 * nk:(i8 + 1) * nk], ACT.Exp,
                                                  bias=st[:, i8:i8 + 1], accum_out=st[:, 16 + i8:17 + i8])
                        last.then_inc(S["ps_exp"], 1)
                act.wait_ge(S["pp_turned"], u + 1)
                w = 1024 * (qt + 1)
                act.activation(pT[:, 0:w // 2], ps[:, 0:2, :].rearrange("p b c -> p (b c)")[:, 0:w // 2], ACT.Copy)
                act.activation(pT[0:16, 2048:2560], ps[0:16, 4, :], ACT.Copy).then_inc(S["pT_act"], 1)
                act.wait_ge(S["po_mm"], u + 1)
                act.activation(oT[64 * g:64 * g + 64, :, qt * P:(qt + 1) * P],
                               ps[64 * g:64 * g + 64, 5, :].rearrange("p (r n) -> p r n", r=R), ACT.Copy).then_inc(S["po_copied"], 1)

            def sample_exps(s):
                act.wait_ge(S["sc_max"], s + 1)
                act.activation(sc[:, 1600:1663], sc[:, 1600:1663], ACT.Exp, bias=st[:, 2:3], accum_out=st[:, 10:11]).then_inc(S["sc_exp"], 1)
                act.wait_ge(S["ss_max"], s + 1)
                act.activation(sc[:, 0:1056], sc[:, 0:1056], ACT.Exp, bias=st[:, 0:1], accum_out=st[:, 8:9])
                act.activation(sc[:, 1056:1600], sc[:, 1056:1600], ACT.Exp, bias=st[:, 1:2], accum_out=st[:, 9:10]).then_inc(S["ss_exp"], 1)

            def copy_weights(s):
                act.wait_ge(S["sp_turned"], s + 1)
                act.activation(pT[:, 0:1024], ps[:, 0:2, :].rearrange("p b c -> p (b c)"), ACT.Copy).then_inc(S["spT_act"], 1)

            def copy_heads(s):
                act.wait_ge(S["so_mm"], s + 1)
                for g in range(NG):
                    for r in range(R):
                        last = act.activation(
                            oT[64 * g:64 * g + 64, r, SEQ + 16 * s:SEQ + 16 * s + 16].rearrange("p (b q) -> p b q", b=SETB),
                            ps[64 * g:64 * g + 64, 7, 0:P].rearrange("p (b g q r) -> p b g q r", b=SETB, g=NG, q=NQ)[:, :, g, :, r], ACT.Copy)
                last.then_inc(S["so_copied"], 1)

            sample_exps(0)
            copy_weights(0)
            sample_exps(1)
            copy_heads(0)
            copy_weights(1)
            copy_heads(1)

            def high_tokens(k, again=0):
                act.wait_ge(S["h2_in"], 4 * again + k // 2 + 1)
                act.activation(mov_hi[:, k:k + 2, :], h2[:, k:k + 2, :], ACT.Copy).then_inc(S["h2_high"], 1)

            for k in range(KC):
                act.wait_ge(S["x1_ready"], k + 1)
                act.activation(xsq2[:, k, :], xT[:, k, :], ACT.Square).then_inc(S["x_squared"], 1)
                if k % 2:
                    high_tokens(k - 1)
            act.wait_ge(S["x_var"], 2)
            act.activation(rr2[:, 1, :], rr2[:, 0, :], ACT.Sqrt).then_inc(S["x_std"], 1)

            def split_high(i, it=None):
                n = staged(i)
                at = lambda c, step: c if it is None else it * step + c
                act.wait_ge(ring_in[i % RING], at(16 * (i // RING + 1), 16))
                for h in range(2):
                    act.wait_ge(S["hi_used"], at(n + h + 1, 2 * RING))
                    act.wait_ge(S["lo_ready"], at(n + h + 1, 2 * RING))
                    act.activation(w_hi[:, h, :], ring[:, i % RING, h * 512:(h + 1) * 512], ACT.Copy).then_inc(S["hi_ready"], 1)

            for i in range(W_Q, W_U):
                split_high(i)
            act.wait_ge(S["lo_used"], 2 + staged(W_U))
            for k in range(0, KC, 2):
                high_tokens(k, 1)
            split_high(W_U)
            for t, (n0, n) in enumerate(TILES):
                act.wait_ge(S["pk_mm"], t + 1)
                b0 = 4 * ((t + 1) % 2)
                act.activation(rt("sp")[0:n, t * 2048:(t + 1) * 2048], ps[0:n, b0:b0 + 4, :].rearrange("p b c -> p (b c)"), ACT.Copy)\
                    .then_inc(S["pk_copied"], 1)

            def gelus(it, j0, ahead=RING):
                for s in range(RING):
                    if s < ahead:
                        split_high(W_U + j0 + s + 1, it)
                    act.wait_ge(S["lo_used"], it * (2 * RING) + (2 + staged(W_U + j0 + s + 1)))
                    act.activation(arena[:, bass.ds((it * RING + (j0 + s)) * NT, NT)], ps[:, s % 2, 0:NT], ACT.Gelu).then_inc(S["u_free"], 1)

            for t, (n0, n) in enumerate(TILES):
                with act.Fori(0, 4) as it:
                    gelus(it, 16 * t)
                act.wait_ge(S["top_shift"], t + 1)
                act.activation(rt("tv")[0:n, :], rt("tv")[0:n, :], ACT.Exp).then_inc(S["top_exp"], 1)
            with act.Fori(0, 4) as it:
                gelus(it, 48)
            act.wait_ge(S["route_copied"], 1)
            with act.Fori(0, HALF // RING - 1) as it:
                gelus(it, HALF)
            with act.Fori(0, 1) as it:
                gelus(it, PK - RING, RING - 1)

            act.wait_ge(S["w_free"], 1 + 32)
            for q in range(4):
                if q == 2:
                    act.wait_ge(S["w_free"], 1 + 64)
                with act.Fori(0, 8) as it:
                    for s in range(RING):
                        act.wait_ge(S["lo_used"], it * (2 * RING) + (2 + staged(W_V + 32 * q + s - 1)))
                        act.activation(mov_hi[:, 2 * (s % 2):2 * (s % 2) + 2, :].rearrange("p j n -> p (j n)"),
                                       arena[:, bass.ds((it * 8 + (HALF * (q // 2) + 2 * s)) * NT, 2 * NT)], ACT.Copy)\
                            .then_inc(S["mov_high"], 1)
                        split_high(W_V + 32 * q + s, it)
                        if q < 2 and s % 2:
                            n = 32 + 16 * q + s // 2 + 1
                            act.wait_ge(S["route_mm"], it * 2 + n)
                            act.wait_ge(S["w_free"], it * 2 + n)
                            act.activation(hot_sum, route_parts[:, :, HALF:P], ACT.Copy).then_inc(S["low_copied"], 1)

        @block.vector
        def _(dve):
            link = link_on(dve, S["dve_order"])

            def mean_square(rr):
                dve.tensor_scalar(rr[:, 0, :], ps[:, 0, 0:NT], 1.0 / D, EPS, ALU.mult, ALU.add).then_inc(S["x_var"], 1)

            def scaled(out, k, gain, rr):
                return dve.scalar_tensor_tensor(out=out[:, k, :], in0=xT[:, k, :], scalar=gain[:, k:k + 1], in1=rr[:, 0, :],
                                                op0=ALU.mult, op1=ALU.mult)

            dve.wait_ge(S["smalls_in"], 16)
            dve.wait_ge(S["consts_in"], 16)
            dve.wait_ge(S["x_sumsq"], 1)
            mean_square(rr)
            dve.wait_ge(S["x_std"], 1)
            link(dve.reciprocal(rr[:, 0, :], rr[:, 1, :]))
            for k in range(KC):
                scaled(xT, k, M("norm_mix"), rr).then_inc(S["h_ready"], 1)
            dve.wait_ge(S["zeroed"], 1)
            dve.tensor_copy(us[:, :, :, 0:2], M("state").rearrange("p (k b n) -> p k b n", k=4, b=NB))

            heads = lambda x: x.rearrange("p (h d) -> p h d", d=HD)

            def head_rows(t, n):
                dve.wait_ge(S["tok_copied"], 3 + t + 1)
                if t:
                    dve.wait_ge(S["qk_turned"], t)
                    dve.wait_ge(S["k_rows_out"], 32 * t)
                qk = ptok[0:n, t, 0:768]
                link(dve.tensor_tensor(tmpq[0:n, :], qk, qk, ALU.mult))
                link(dve.tensor_reduce(st[0:n, 0:12], heads(tmpq[0:n, :]), AX.X, ALU.add))
                dve.tensor_scalar(st[0:n, 0:12], st[0:n, 0:12], 1.0 / HD, EPS, ALU.mult, ALU.add).then_inc(S["qk_var"], 1)
                dve.wait_ge(S["qk_std"], t + 1)
                link(dve.reciprocal(st[0:n, 0:12], st[0:n, 16:28]))
                link(dve.tensor_tensor(heads(qn[0:n, :]), heads(qk), over(st[0:n, 0:12], 2, HD), ALU.mult))
                link(dve.tensor_tensor(qn[0:n, :], qn[0:n, :], M("gain")[0:n, :], ALU.mult))
                cos, sin = C("cos", n)[:, t * HD:(t + 1) * HD], C("sin", n)[:, t * HD:(t + 1) * HD]
                q3, t3 = heads(qn[0:n, :]), heads(tmpq[0:n, :])
                dve.tensor_tensor(t3[:, :, 0:32], q3[:, :, 32:64], over(sin[:, 0:32], 1, 12), ALU.mult)
                dve.tensor_tensor(t3[:, :, 32:64], q3[:, :, 0:32], over(sin[:, 32:64], 1, 12), ALU.mult)
                link(dve.tensor_tensor(heads(qr[0:n, :]), q3, over(cos, 1, 12), ALU.mult))
                dve.tensor_tensor(qr[0:n, :], qr[0:n, :], tmpq[0:n, :], ALU.add).then_inc(S["qk_ready"], 1)

            cw = M("conv_w").rearrange("p (k c) -> p k c", k=3)

            def conv(c):
                dve.wait_ge(S["cc_copied"], c + 1)
                dve.wait_ge(S["slots_used"], W_CONV + 3 * c + 2)
                dve.tensor_tensor(up[:, c, 2:258], ps[:, 6, 0:SEQ], rr[:, 1, 0:SEQ], ALU.mult)
                dve.tensor_tensor(us[:, c, :, 2:6], ps[:, 6, SEQ:NT].rearrange("p (b n) -> p b n", b=NB),
                                  rr[:, 1, SEQ:NT].rearrange("p (b n) -> p b n", b=NB), ALU.mult).then_inc(S["u_ready"], 1)
                dve.wait_ge(S["u_ready"], c + 1)
                z_p, z_s = zT[:, c, 0:SEQ], zT[:, c, SEQ:NT].rearrange("p (b n) -> p b n", b=NB)
                dve.tensor_scalar(z_p, up[:, c, 0:SEQ], cw[:, 0, c:c + 1], None, ALU.mult)
                link(dve.tensor_scalar(z_s, us[:, c, :, 0:4], cw[:, 0, c:c + 1], None, ALU.mult))
                for k in (1, 2):
                    dve.scalar_tensor_tensor(out=z_p, in0=up[:, c, k:k + SEQ], scalar=cw[:, k, c:c + 1], in1=z_p, op0=ALU.mult, op1=ALU.add)
                    link(dve.scalar_tensor_tensor(out=z_s, in0=us[:, c, :, k:k + 4], scalar=cw[:, k, c:c + 1], in1=z_s, op0=ALU.mult, op1=ALU.add))
                dve.wait_ge(S["slots_used"], W_CONV + 3 * c + 3)
                dve.tensor_tensor(zT[:, c, :], ps[:, 7, 0:NT], zT[:, c, :], ALU.mult).then_inc(S["z_ready"], 1)

            for t, (n0, n) in enumerate(TILES):
                head_rows(t, n)
                conv(t)
            conv(3)
            dve.wait_ge(S["tok_copied"], 9)
            for t, (n0, n) in enumerate(TILES):
                dve.tensor_copy(vnew[0:n, t, :], ptok[0:n, t, C_VS:C_VS + 2 * P]).then_inc(S["vnew_ready"], 1)
            dve.wait_ge(S["gate_exp"], 3)
            for t, (n0, n) in enumerate(TILES):
                link(dve.tensor_scalar(sg[0:n, t, :], sg[0:n, t, :], 1.0, None, ALU.add))
                dve.reciprocal(sg[0:n, t, :], sg[0:n, t, :]).then_inc(S["gate_ready"], 1)

            dve.wait_ge(S["cbias_mm"], 1)
            dve.tensor_tensor(bias[:, :], ps[:, 7, 0:2], M("b1"), ALU.add)
            for u, (t, v) in enumerate(UNITS):
                n = P if t < 4 else 16
                dve.wait_ge(S["comp_mm"], u + 1)
                dve.wait_ge(S["sec_copied"], u + 1)
                L = 64 if t < 4 else 16
                f = ps[:, 3 + u % 2, 0:2 * n].rearrange("p (g c) -> p g c", c=L)
                s3 = sec[:, 0:2 * n].rearrange("p (g c) -> p g c", c=L)
                dve.tensor_tensor(s3[:, :, 0:L - 1], f[:, :, 0:L - 1], s3[:, :, 1:L], ALU.add).then_inc(S["hid_sum"], 1)
                if u != 5:
                    continue
                dve.wait_ge(S["cmp_copied"], 5)
                k2 = kcn.rearrange("p t (g d) -> p (t g) d", d=HD)
                sq = ar("b", 0, 5 * P).rearrange("p (g d) -> p g d", d=HD)
                for n, lo, hi in ((P, 0, 8), (16, 8, 10)):
                    link(dve.tensor_tensor(sq[0:n, lo:hi], k2[0:n, lo:hi], k2[0:n, lo:hi], ALU.mult))
                    if lo == 0:
                        link(dve.memset(st[:, 0:10], 1.0))
                    link(dve.tensor_reduce(st[0:n, lo:hi], sq[0:n, lo:hi], AX.X, ALU.add))
                dve.tensor_scalar(st[:, 0:10], st[:, 0:10], 1.0 / HD, EPS, ALU.mult, ALU.add).then_inc(S["kcn_var"], 1)
                dve.wait_ge(S["kcn_std"], 1)
                link(dve.reciprocal(st[:, 0:10], st[:, 16:26]))
                for n, lo, hi in ((P, 0, 8), (16, 8, 10)):
                    link(dve.tensor_tensor(k2[0:n, lo:hi], k2[0:n, lo:hi], over(st[0:n, lo:hi], 2, HD), ALU.mult))
                    dve.tensor_tensor(k2[0:n, lo:hi], k2[0:n, lo:hi], over(M("kcgain")[0:n, :], 1, hi - lo), ALU.mult).then_inc(S["kcn_ready"], 1)

            for u in range(4):
                qt, g = u // 2, u % 2
                nk = P * (qt + 1)
                dve.wait_ge(S["p_scored"], u + 1)
                if u:
                    dve.wait_ge(S["pp_turned"], u)
                cs = st[:, 32:96].rearrange("p (r c) -> p r c", r=R)
                link(dve.scalar_tensor_tensor(out=cs, in0=ps[:, 4, 0:64].rearrange("p (r c) -> p r c", r=R), scalar=SCALE,
                                              in1=over(C("cmpmask")[:, 16 * qt:16 * qt + 16], 1, R), op0=ALU.mult, op1=ALU.add))
                link(dve.tensor_reduce(st[:, 8:12], cs, AX.X, ALU.max))
                link(dve.tensor_scalar(st[:, 8:12], st[:, 8:12], NEG / 10, None, ALU.max))
                dve.tensor_tensor(cs, cs, over(st[:, 8:12], 2, 16), ALU.subtract).then_inc(S["pc_shift"], 1)
                s8 = sc[:, 0:8 * nk].rearrange("p (i c) -> p i c", c=nk)
                scores = ps[:, 0:2 * (qt + 1), :].rearrange("p b c -> p (b c)").rearrange("p (i c) -> p i c", c=nk)
                mask = C("causal")[:, P - P * qt:2 * P]
                link(dve.scalar_tensor_tensor(out=s8, in0=scores, scalar=SCALE, in1=over(mask, 1, 8), op0=ALU.mult, op1=ALU.add))
                dve.tensor_reduce(st[:, 0:8], s8, AX.X, ALU.max, negate=True).then_inc(S["ps_max"], 1)
                dve.wait_ge(S["pc_exp"], u + 1)
                link(dve.tensor_reduce(st[:, 24:28], cs, AX.X, ALU.add))
                link(dve.tensor_scalar(st[:, 24:28], st[:, 24:28], 1e-30, None, ALU.max))
                dve.wait_ge(S["ps_exp"], u + 1)
                link(dve.reciprocal(st[:, 16:28], st[:, 16:28]))
                gates = sg[:, qt, 12 * g:12 * g + 12].rearrange("p (r b) -> p b r", b=3)
                dve.tensor_tensor(st[:, 24:28], st[:, 24:28], gates[:, 0, :], ALU.mult)
                link(dve.tensor_tensor(st[:, 16:24].rearrange("p (b r) -> p b r", b=2), st[:, 16:24].rearrange("p (b r) -> p b r", b=2),
                                       gates[:, 1:3, :], ALU.mult))
                dve.tensor_tensor(cs, cs, over(st[:, 24:28], 2, 16), ALU.mult)
                dve.tensor_tensor(s8, s8, over(st[:, 16:24], 2, nk), ALU.mult).then_inc(S["p_weights"], 1)
                dve.wait_ge(S["pp_turned"], u + 1)
                w = 1024 * (qt + 1)
                if u:
                    dve.wait_ge(S["po_mm"], u)
                dve.tensor_copy(pT[:, w // 2:w], ps[:, 0:4, :].rearrange("p b c -> p (b c)")[:, w // 2:w]).then_inc(S["pT_dve"], 1)
                dve.wait_ge(S["mg_exp"], 4 * u + 4)
                four = mg[:, 4 * u:4 * u + 4, :]
                link(dve.tensor_scalar(four, four, 1.0, None, ALU.add))
                dve.reciprocal(four, four).then_inc(S["mg_ready"], 1)

            dve.wait_ge(S["rep_mm"], 1)
            for s in range(2):
                t24 = st[:, 32:56].rearrange("p (e b) -> p e b", b=3)
                link(dve.tensor_tensor(t24, ps[:, 5, 24 * s:24 * s + 24].rearrange("p (e b) -> p e b", b=3),
                                       over(C("gsel"), 2, 3), ALU.mult))
                dve.tensor_reduce(rg[:, 3 * s:3 * s + 3], t24.rearrange("p e b -> p b e"), AX.X, ALU.add).then_inc(S["rg_ready"], 1)
                dve.wait_ge(S["rg_ready"], s + 1)
            def y_product(slot, m):
                if m % 2:
                    dve.wait_ge(S["slots_used"], slot + m // 2 + 1)
                else:
                    dve.wait_ge(S["y_even"], (4 if slot == W_YN else 0) + m // 2 + 1)

            def gate_conv(chunks):
                for m in chunks:
                    y_product(W_YC, m)
                    dve.tensor_tensor(mg[:, m, :], ps[:, 4 + m % 2, 0:NT], mg[:, m, :], ALU.mult).then_inc(S["yc_used"], 1)

            for s in range(2):
                dve.wait_ge(S["k_scored"], 12 * (s + 1))
                if s:
                    dve.wait_ge(S["sp_turned"], s)
                cn, cg = sc[:, 1600:1663], sc[:, 1664:1727]
                link(dve.tensor_scalar(cn, ps[:, 3, 64:127], SCALE, None, ALU.mult))
                dve.tensor_reduce(st[:, 2:3], cn, AX.X, ALU.max, negate=True).then_inc(S["sc_max"], 1)
                nm = C("newmask")[:, NS * s:NS * s + NS]
                dve.scalar_tensor_tensor(out=sc[:, 1024:1056], in0=ps[:, 3, 0:32], scalar=SCALE, in1=nm, op0=ALU.mult, op1=ALU.add)
                dve.scalar_tensor_tensor(out=sc[:, 1568:1600], in0=ps[:, 3, 32:64], scalar=SCALE, in1=nm, op0=ALU.mult, op1=ALU.add)
                link(dve.tensor_scalar(sc[:, 1056:1568], ps[:, 2, :], SCALE, None, ALU.mult))
                link(dve.tensor_tensor(sc[:, 1056:1060], sc[:, 1056:1060], C("winmask"), ALU.add))
                link(dve.tensor_reduce(st[:, 1:2], sc[:, 1056:1600], AX.X, ALU.max, negate=True))
                dve.wait_ge(S["sc_exp"], s + 1)
                link(dve.reciprocal(st[:, 10:11], st[:, 10:11]))
                dve.tensor_scalar(cn, cn, st[:, 10:11], None, ALU.mult).then_inc(S["cn_ready"], 1)
                dve.wait_ge(S["cn_turned"], s + 1)
                g32, p4 = pT[0:63, 2048:2080], pT[0:63, 2080:2208]
                link(dve.tensor_reduce(g32, ps[0:63, 3, 128:256].rearrange("p (a r) -> p a r", r=R), AX.X, ALU.add))
                dve.tensor_copy(p4.rearrange("p (a r) -> p a r", r=R), over(g32, 2, R)).then_inc(S["p4_ready"], 1)
                if s == 0:
                    gate_conv((0, 1))
                dve.wait_ge(S["blk_mm"], s + 1)
                blk, eq = st[:, 32:49], st[:, 52:69]
                link(dve.tensor_tensor(blk, ps[:, 3, 256:273], C("forced"), ALU.add))
                link(dve.tensor_reduce(st[:, 12:13], blk, AX.X, ALU.min))
                link(dve.scalar_tensor_tensor(out=eq, in0=blk, scalar=st[:, 12:13], in1=C("jp1"), op0=ALU.is_equal, op1=ALU.mult))
                link(dve.tensor_reduce(st[:, 13:14], eq, AX.X, ALU.max))
                link(dve.tensor_scalar(eq, C("jp1"), st[:, 13:14], NEG, ALU.is_equal, ALU.mult))
                link(dve.scalar_tensor_tensor(out=sc[:, 0:1024].rearrange("p (j c) -> p j c", c=BLK),
                                              in0=ps[:, 0:2, :].rearrange("p b c -> p (b c)").rearrange("p (j c) -> p j c", c=BLK),
                                              scalar=SCALE, in1=over(eq[:, 0:16], 2, BLK), op0=ALU.mult, op1=ALU.add))
                dve.tensor_reduce(st[:, 0:1], sc[:, 0:1056], AX.X, ALU.max, negate=True).then_inc(S["ss_max"], 1)
                dve.wait_ge(S["ss_exp"], s + 1)
                link(dve.reciprocal(st[:, 8:10], st[:, 8:10]))
                link(dve.tensor_tensor(st[:, 8:10], st[:, 8:10], rg[:, 3 * s + 1:3 * s + 3], ALU.mult))
                dve.tensor_scalar(cg, cn, rg[:, 3 * s:3 * s + 1], None, ALU.mult)
                dve.tensor_scalar(sc[:, 0:1056], sc[:, 0:1056], st[:, 8:9], None, ALU.mult)
                dve.tensor_scalar(sc[:, 1056:1600], sc[:, 1056:1600], st[:, 9:10], None, ALU.mult).then_inc(S["s_weights"], 1)
                gate_conv((2, 3) if s == 0 else (4, 5))
                dve.wait_ge(S["sp_turned"], s + 1)
                if s:
                    dve.wait_ge(S["so_mm"], s)
                dve.tensor_copy(pT[:, 1024:1536], ps[:, 2, :])
                dve.tensor_copy(pT[0:32, 1536:1792], ps[0:32, 3, 0:256])
                dve.tensor_copy(pT[0:63, 1792:1920], ps[0:63, 3, 256:384]).then_inc(S["spT_dve"], 1)
            gate_conv((6, 7))
            for m in range(KC):
                y_product(W_YN, m)
                if m:
                    dve.wait_ge(S["merged"], m)
                link(dve.tensor_tensor(mt, ps[:, 4 + m % 2, 0:NT], mg[:, 8 + m, :], ALU.mult))
                dve.tensor_tensor(mg[:, m, :], mg[:, m, :], mt, ALU.add).then_inc(S["merged"], 1)
            dve.wait_ge(S["x_again"], 16)
            def low_tokens(k, again=0):
                dve.wait_ge(S["h2_high"], 4 * again + k // 2 + 1)
                dve.tensor_tensor(mov_lo[:, k:k + 2, :], h2[:, k:k + 2, :], mov_hi[:, k:k + 2, :].bitcast(F32), ALU.subtract)\
                    .then_inc(S["h2_split"], 1)

            for m in range(KC):
                dve.wait_ge(S["slots_used"], W_O + m + 1)
                dve.tensor_tensor(xT[:, m, :], xT[:, m, :], ps[:, 2 + m % 2, 0:NT], ALU.add).then_inc(S["x1_ready"], 1)
                dve.wait_ge(S["x1_ready"], m + 1)
                last = dve.tensor_scalar(h2[:, m, :], xT[:, m, :], M("norm_ffn")[:, m:m + 1], None, ALU.mult)
                if m % 2:
                    last.then_inc(S["h2_in"], 1)
                    low_tokens(m - 1)
            dve.wait_ge(S["x_sumsq"], 2)
            mean_square(rr2)
            dve.wait_ge(S["x_std"], 2)
            link(dve.reciprocal(rr2[:, 0, :], rr2[:, 1, :]))
            for i in range(16):
                dve.wait_ge(S["lo_used"], 2 + staged(W_Q + i + 1))
                dve.tensor_tensor(rt("qq")[:, i * NT:(i + 1) * NT], ps[:, i % 2, 0:NT], rr2[:, 0, :], ALU.mult).then_inc(S["qq_copied"], 1)
                if i in (3, 5, 7, 9):
                    two = h2[:, i - 3:i - 1, :]
                    dve.tensor_tensor(two, two, over(rr2[:, 0, :], 1, 2), ALU.mult).then_inc(S["h2_in"], 1)
            for k in range(0, KC, 2):
                low_tokens(k, 1)

            for t, (n0, n) in enumerate(TILES):
                sp, cand, eq = (rt(x)[0:n, :] for x in ("sp", "cand", "eq"))
                sp = sp[:, t * 2048:(t + 1) * 2048]
                lv, li, lf, tv, ti, ab, abf, z8 = (rt(x)[0:n, :] for x in ("lv", "li", "lf", "tv", "ti", "ab", "abf", "z8"))
                gi = rt("gi")[0:n, 3 * P * t:3 * P * (t + 1)]

                def top16(groups, width, src, val, idx):
                    for half in range(2):
                        for i in range(groups):
                            last = dve.max(out=val[:, 16 * i + 8 * half:16 * i + 8 * half + 8], in_=src[:, i * width:(i + 1) * width])
                        link(last)
                        for i in range(groups):
                            last = dve.max_index(out=idx[:, 16 * i + 8 * half:16 * i + 8 * half + 8],
                                                 in_max=val[:, 16 * i + 8 * half:16 * i + 8 * half + 8], in_values=src[:, i * width:(i + 1) * width])
                        if half == 0:
                            for i in range(groups):
                                last = dve.match_replace(out=src[:, i * width:(i + 1) * width], in_to_replace=val[:, 16 * i:16 * i + 8],
                                                         in_values=src[:, i * width:(i + 1) * width], imm_value=-3e38)
                        link(last)

                dve.wait_ge(S["pk_copied"], t + 1)
                top16(16, PK, sp, lv, li.bitcast(U32))
                link(dve.tensor_copy(lf, li.bitcast(U32)))
                l4 = lv.rearrange("p (h c k) -> p h c k", h=PH, c=2)
                c4 = cand.rearrange("p (h a b) -> p h a b", h=PH, a=PTOP)
                dve.wait_ge(S["pk_mm"], 3)
                link(dve.tensor_tensor(c4, over(l4[:, :, 0, :], 3, PTOP), over(l4[:, :, 1, :], 2, PTOP), ALU.add))
                top16(PH, 256, cand, tv, ti.bitcast(U32))
                t3 = tv.rearrange("p (h k) -> p h k", h=PH)
                link(dve.tensor_copy(z8[:, 0:8], t3[:, :, 0]))
                dve.tensor_tensor(t3, t3, over(z8[:, 0:8], 2, PTOP), ALU.subtract).then_inc(S["top_shift"], 1)
                u = ti.bitcast(U32)
                dve.tensor_scalar(ab[:, 0:P].bitcast(U32), u, 4, None, ALU.logical_shift_right)
                link(dve.tensor_scalar(ab[:, P:2 * P].bitcast(U32), u, 15, None, ALU.bitwise_and))
                link(dve.tensor_copy(abf, ab.bitcast(U32)))
                lf4 = lf.rearrange("p (h c k) -> p h c k", h=PH, c=2)
                e4 = eq.rearrange("p (h k a) -> p h k a", h=PH, k=PTOP)
                for c in range(2):
                    link(dve.tensor_tensor(eq.rearrange("p (k a) -> p k a", a=PTOP), over(abf[:, c * P:(c + 1) * P], 2, PTOP),
                                           over(C("iota16", n), 1, P), ALU.is_equal))
                    link(dve.tensor_tensor(e4, e4, over(lf4[:, :, c, :], 2, PTOP), ALU.mult))
                    link(dve.tensor_reduce(gi[:, (1 + c) * P:(2 + c) * P], eq.rearrange("p (k a) -> p k a", a=PTOP), AX.X, ALU.add))
                dve.wait_ge(S["top_exp"], t + 1)
                link(dve.tensor_reduce(z8[:, 0:8], t3, AX.X, ALU.add))
                link(dve.reciprocal(z8[:, 8:16], z8[:, 0:8]))
                dve.tensor_tensor(gi[:, 0:P].rearrange("p (h k) -> p h k", h=PH), t3, over(z8[:, 8:16], 2, PTOP), ALU.mult).then_inc(S["routed"], 1)
            dve.wait_ge(S["route_turned"], 1)
            last = dve.tensor_copy(aux[:, LISTS:HOT].rearrange("p (i n) -> p i n", i=3), ps[:, 5:8, 0:NT])
            last.then_inc(S["route_copied"], 1)
            dve.wait_ge(S["route_copied"], 1)
            gT, i1T, i2T = (aux[:, LISTS + i * NT:LISTS + (i + 1) * NT] for i in range(3))

            def one_hots(it, g):
                for x in range(GT):
                    n = it * (2 * GT) + (g * GT + x)
                    dve.tensor_scalar(oh[:, x, 0:P], C("iota"), i1T[:, bass.ds(n, 1)], None, ALU.is_equal)
                    last = dve.tensor_scalar(oh[:, x, P:P + HALF], C("iota")[:, 0:HALF],
                                             i2T[:, bass.ds(n, 1)], gT[:, bass.ds(n, 1)], ALU.is_equal, ALU.mult)
                last.then_inc(S["oh_ready"], 1)

            def weigh(it, g):
                dve.wait_ge(S["route_mm"], it * 2 + (g + 1))
                w = arena[:, 0:HALF * NT].rearrange("p (j n) -> p n j", n=NT)[:, bass.ds(it * (2 * GT) + g * GT, GT), :]
                dve.tensor_tensor(w, ps[:, 2:4, :].rearrange("p b c -> p (b c)")[:, 0:GT * HALF].rearrange("p (n j) -> p n j", n=GT),
                                  w, ALU.mult).then_inc(S["w_free"], 1)

            def first_rows(tok):
                dve.tensor_tensor(hot_first, over(C("iota"), 1, GT), over(i1T[:, bass.ds(tok, GT)], 2, P), ALU.is_equal)

            def second_places(tok):
                dve.tensor_tensor(hot_eq, over(C("iota")[:, HALF:P], 1, GT), over(i2T[:, bass.ds(tok, GT)], 2, HALF), ALU.is_equal)\
                    .then_inc(S["eq_ready"], 1)

            def second_rows(it, g0):
                tok = it * (2 * GT) + g0 * GT
                dve.wait_ge(S["eq_ready"], it * 2 + (g0 + 1))
                dve.tensor_tensor(hot_second[:, :, 0:HALF], hot_eq, over(gT[:, bass.ds(tok, GT)], 2, HALF), ALU.mult)
                dve.tensor_tensor(hot_second[:, :, HALF:P], hot_eq, over(gT_low[:, bass.ds(tok, GT)], 2, HALF), ALU.mult)\
                    .then_inc(S["oh_ready"], 1)

            def weigh_split(it, g0):
                dve.wait_ge(S["low_copied"], it * 2 + (g0 + 1))
                dve.tensor_tensor(hot_sum, route_parts[:, :, 0:HALF], hot_sum, ALU.add).then_inc(S["sum_ready"], 1)
                dve.wait_ge(S["sum_ready"], it * 2 + (g0 + 1))
                w = arena[:, HALF * NT:PK * NT].rearrange("p (j n) -> p n j", n=NT)[:, bass.ds(it * (2 * GT) + g0 * GT, GT), :]
                dve.tensor_tensor(w, hot_sum, w, ALU.mult).then_inc(S["w_free"], 1)

            def split_moving(it, q, s):
                dve.wait_ge(S["mov_high"], it * RING + (32 * q + s + 1))
                two = slice(2 * (s % 2), 2 * (s % 2) + 2)
                dve.tensor_tensor(mov_lo[:, two, :].rearrange("p j n -> p (j n)"),
                                  arena[:, bass.ds((it * 8 + (HALF * (q // 2) + 2 * s)) * NT, 2 * NT)],
                                  mov_hi[:, two, :].rearrange("p j n -> p (j n)").bitcast(F32), ALU.subtract)\
                    .then_inc(S["mov_ready"], 1)

            dve.wait_ge(S["u_free"], 2 + HALF)
            with dve.Fori(0, 16) as it:
                for g in range(2):
                    one_hots(it, g)
                    weigh(it, g)
            dve.wait_ge(S["u_free"], 2 + PK)
            link(dve.tensor_copy(hot_first.rearrange("p x c -> p (x c)")[:, 0:NT], gT))
            link(dve.tensor_tensor(gT_low, gT, hot_first.rearrange("p x c -> p (x c)")[:, 0:NT].bitcast(F32), ALU.subtract))
            first_rows(0)
            second_places(0)
            for q in range(4):
                if q == 0:
                    dve.wait_ge(S["w_free"], 1 + 32)
                if q == 2:
                    dve.wait_ge(S["w_free"], 1 + 64)
                if q >= 2:
                    with dve.Fori(0, 8) as it:
                        for s in range(RING):
                            split_moving(it, q, s)
                else:
                    split_moving(0, q, 0)
                    for times, at in ((7, 0), (1, 7)):
                        with dve.Fori(0, times) as it:
                            for s in range(0, RING, 2):
                                g0 = 16 * q + 2 * at + s // 2
                                tok = it * (2 * GT) + (g0 + 1) * GT
                                more = g0 < 31
                                second_rows(it, g0)
                                split_moving(it, q, RING * at + s + 1)
                                if more:
                                    dve.wait_ge(S["oh_ready"], it * 2 + (32 + g0 + 1))
                                    second_places(tok)
                                dve.wait_ge(S["route_mm"], it * 2 + (32 + g0 + 1))
                                if more:
                                    first_rows(tok)
                                if RING * at + s + 2 < 32:
                                    split_moving(it, q, RING * at + s + 2)
                                weigh_split(it, g0)
                dve.wait_ge(S["lo_used"], 2 + staged(W_V + 32 * (q + 1)))
                for m in range(4):
                    x = xT[:, 4 * (q % 2) + m, :]
                    last = dve.tensor_tensor(x, x, ps[:, VBANK[m], 0:NT], ALU.add)
                last.then_inc(S["y_ready"], 1)

        @block.tensor
        def _(pe):
            def project(i, bank, rhs, n=KC, at=0):
                slot_ready(pe, i)
                for k in range(n):
                    last = pe.matmul(ps[:, bank, 0:NT], ring[:, i % RING, at + k * P:at + (k + 1) * P], rhs[:, k, :],
                                     start=(k == 0), stop=(k == n - 1))
                return last

            def square_sum(x, k):
                return pe.matmul(ps[:, 0, 0:NT], C("ones"), x[:, k, :], start=(k == 0), stop=(k == KC - 1))

            pe.wait_ge(S["consts_in"], 16)
            for k in range(KC):
                pe.wait_ge(S["x_squared"], k // 2 + 1)
                last = square_sum(xsq, k)
            last.then_inc(S["x_sumsq"], 1)
            for p, (c0, w) in enumerate(PIECES):
                if p == 2:
                    pe.wait_ge(S["tok_copied"], 3)
                for i in range(4):
                    slot_ready(pe, 4 * p + i)
                    for kk in range(2):
                        k = 2 * i + kk
                        if p == 0:
                            pe.wait_ge(S["h_ready"], k + 1)
                        for t, (n0, n) in enumerate(TILES):
                            last = pe.matmul(ps[0:n, 3 * (p % 2) + t, 0:w], xT[:, k, n0:n0 + n],
                                             ring[:, (4 * p + i) % RING, kk * w:(kk + 1) * w], start=(k == 0), stop=(k == KC - 1))
                    last.then_inc(S["slots_used"], 1)

            def conv_chunks(c):
                if c == 0:
                    pe.wait_ge(S["tok_copied"], 6)
                else:
                    pe.wait_ge(S["cc_copied"], c)
                project(W_CONV + 3 * c, 5, xT).then_inc(S["slots_used"], 1)
                if c:
                    pe.wait_ge(S["u_ready"], c)
                project(W_CONV + 3 * c + 1, 6, xT).then_inc(S["slots_used"], 1)
                if c:
                    pe.wait_ge(S["z_ready"], c)
                project(W_CONV + 3 * c + 2, 7, xT).then_inc(S["slots_used"], 1)

            def comp_in(u):
                t, v = UNITS[u]
                if u == 0:
                    pe.wait_ge(S["w1_in"], 16)
                if t < 4:
                    i = PAGED.index(u)
                    pe.wait_ge(S[f"xc_in{i % 6}"], 256 * (i // 6 + 1))
                if u >= 2:
                    pe.wait_ge(S["hid_sum"], u - 1)
                for half in range(2):
                    for k in range(8):
                        if t < 4:
                            src = xc[:, i % 3, :, k, :, :].rearrange("p j g c -> p g j c")
                            dst = ps[:, 3 + u % 2, 256 * half:256 * half + 256].rearrange("p (g j c) -> p g j c", g=NG, j=16)
                        else:
                            src, dst = xcp[:, v, k, :, :], ps[:, 3 + u % 2, 256 * half:256 * half + 32].rearrange("p (g c) -> p g c", g=NG)
                        last = pe.matmul(dst, w1[:, v, 8 * half + k, :], src, start=(k == 0), stop=(k == 7))
                last.then_inc(S["comp_mm"], 1)

            for t, (n0, n) in enumerate(TILES):
                conv_chunks(t)
                if t < 2:
                    comp_in(t)
                pe.wait_ge(S["qk_ready"], t + 1)
                if t == 0:
                    pe.wait_ge(S["tok_copied"], 9)
                else:
                    pe.wait_ge(S["qT_copied"], t)
                for i, q in enumerate((qn, qr)):
                    for r in range(R):
                        pe.transpose(ps[:, i, r * P:r * P + n], q[0:n, r * P:(r + 1) * P], ident[0:n, 0:n])
                if t < 2:
                    for v, c in enumerate((C_KC, C_VC)):
                        pe.transpose(ps[:, 2, (2 + v) * P:(3 + v) * P], ptok[:, t, c:c + P], ident)
                pe.transpose(ps[:, 2, 0:n], qr[0:n, 512:640], ident[0:n, 0:n])
                pe.transpose(ps[:, 2, P:P + n], qr[0:n, 640:768], ident[0:n, 0:n]).then_inc(S["qk_turned"], 1)
            conv_chunks(3)

            pe.wait_ge(S["z_ready"], 4)
            for v in range(2):
                for k in range(16):
                    last = pe.matmul(ps[:, 7, v:v + 1], w1[:, v, k, :], M("pos")[:, 16 * v + k:16 * v + k + 1], start=(k == 0), stop=(k == 15))
            last.then_inc(S["cbias_mm"], 1)
            pe.wait_ge(S["qT_copied"], 3)

            def comp_out(u):
                t, v = UNITS[u]
                n = P if t < 4 else 16
                pe.wait_ge(S["hid_ready"], u + 1)
                if u:
                    pe.wait_ge(S["cmp_copied"], u)
                w2 = M("w2")[:, v * HD:(v + 1) * HD]
                if v == 0 or t == 4:
                    for g in range(NG):
                        last = pe.matmul(ps[0:n, 5, g * HD:(g + 1) * HD], hid[:, g * n:(g + 1) * n], w2, start=True, stop=True)
                else:
                    for b in range(2):
                        for g in range(NG):
                            last = pe.matmul(ps[0:64, 5, b * P + g * HD:b * P + (g + 1) * HD], hid[:, g * P + b * 64:g * P + b * 64 + 64], w2,
                                             start=True, stop=True)
                last.then_inc(S["comp_out"], 1)

            for u in range(2, 10):
                comp_in(u)
                if u == 2:
                    comp_out(0)
                comp_out(u - 1)
                if u == 9:
                    comp_out(9)
                if u == 8:
                    for t in range(5):
                        n = P if t < 4 else 16
                        pe.wait_ge(S["kcn_ready"], 1 if t < 4 else 2)
                        if t >= 2:
                            pe.wait_ge(S["kcT_copied"], t - 1)
                        pe.transpose(ps[:, 6 + t % 2, 0:n], kcn[0:n, t, :], ident[0:n, 0:n]).then_inc(S["kcn_turned"], 1)
            pe.wait_ge(S["kcT_copied"], 5)
            pe.wait_ge(S["cmp_copied"], 10)

            pe.wait_ge(S["vnew_ready"], 3)
            for u in range(4):
                qt, g = u // 2, u % 2
                nk = P * (qt + 1)
                lane, n0 = slice(64 * g, 64 * g + 64), qt * P
                if u:
                    pe.wait_ge(S["pT_act"], u)
                    pe.wait_ge(S["pT_dve"], u)
                flat = ps[:, 0:4, :].rearrange("p b c -> p (b c)")
                for r in range(R):
                    pe.matmul(ps[:, 4, 16 * r:16 * r + 16], qnT[lane, r, n0:n0 + P], kcT[lane, 4 * P:4 * P + 16], start=True, stop=True)
                    for br, keys in enumerate((ksT, kwT)):
                        i = 4 * br + r
                        last = pe.matmul(flat[:, i * nk:(i + 1) * nk], qrT[lane, r, n0:n0 + P], keys[lane, 0:nk], start=True, stop=True)
                last.then_inc(S["p_scored"], 1)
                for i in range(4 * u, 4 * u + 4):
                    if i >= 2:
                        pe.wait_ge(S["mg_exp"], i - 1)
                    project(W_MG + i, 6 + i % 2, xT).then_inc(S["slots_used"], 1)
                pe.wait_ge(S["p_weights"], u + 1)
                for i in range(8):
                    for kt in range(qt + 1):
                        x = i * (qt + 1) + kt
                        pe.transpose(flat[:, x * P:(x + 1) * P], sc[:, x * P:(x + 1) * P], ident)
                for r in range(R):
                    last = pe.transpose(ps[0:16, 4, r * P:(r + 1) * P], st[:, 32 + 16 * r:48 + 16 * r], ident)
                last.then_inc(S["pp_turned"], 1)
                pe.wait_ge(S["pT_act"], u + 1)
                pe.wait_ge(S["pT_dve"], u + 1)
                if u:
                    pe.wait_ge(S["po_copied"], u)
                for r in range(R):
                    o = ps[:, 5, r * P:(r + 1) * P]
                    pe.matmul(o, vc[0:16, 8, :], pT[0:16, 2048 + r * P:2048 + (r + 1) * P], start=True, stop=False)
                    for br in range(2):
                        for kt in range(qt + 1):
                            x = (4 * br + r) * (qt + 1) + kt
                            last = pe.matmul(o, vnew[:, kt, br * P:(br + 1) * P], pT[:, x * P:(x + 1) * P], start=False,
                                             stop=(br == 1 and kt == qt))
                last.then_inc(S["po_mm"], 1)

            pe.wait_ge(S["gate_ready"], 3)
            pe.wait_ge(S["po_copied"], 4)
            for s in range(2):
                last = pe.matmul(ps[:, 5, 24 * s:24 * s + 24], C("rep")[0:NS, s * P:(s + 1) * P], sg[0:NS, 2, :], start=True, stop=True)
            last.then_inc(S["rep_mm"], 1)
            def score(s):
                if s:
                    pe.wait_ge(S["spT_act"], s)
                    pe.wait_ge(S["spT_dve"], s)
                for b4 in range(SETB):
                    b = SETB * s + b4
                    rows = slice(32 * b4, 32 * b4 + 32)
                    pe.matmul(ps[rows, 3, 0:NS], qbr[:, b, :], ksT[:, SEQ:NT], start=True, stop=True)
                    pe.matmul(ps[rows, 3, NS:2 * NS], qbr[:, b, :], kwT[:, SEQ:NT], start=True, stop=True)
                    pe.matmul(ps[rows, 3, 64:128], qbn[:, b, :], kcT[:, 64 * b:64 * b + 64], start=True, stop=True)
                    for h in range(3):
                        pe.wait_ge(S[f"k_in{b % 4}_{h}"], (64 if h < 2 else 16) * (b // 4 + 1))
                        pe.matmul(ps[rows, h, :], qbr[:, b, :], kplaces[b % 4][h], start=True, stop=True).then_inc(S["k_scored"], 1)

            def turn_compressed(s):
                pe.wait_ge(S["cn_ready"], s + 1)
                pe.transpose(ps[0:63, 3, 128:256], sc[:, 1600:1663], ident).then_inc(S["cn_turned"], 1)

            def block_scores(s):
                pe.wait_ge(S["p4_ready"], s + 1)
                pe.matmul(ps[:, 3, 256:256 + NSEL], pT[0:63, 2080:2208], C("ov")[0:63, :], start=True, stop=True).then_inc(S["blk_mm"], 1)

            def conv_out(chunks):
                for m in chunks:
                    if m >= 2:
                        pe.wait_ge(S["yc_used"], m - 1)
                    last = project(W_YC + m // 2, 4 + m % 2, zT, 4, (m % 2) * 512)
                    last.then_inc(S["slots_used" if m % 2 else "y_even"], 1)

            def turn_weights(s):
                pe.wait_ge(S["s_weights"], s + 1)
                for i in range(12):
                    c0 = i * P if i < 8 else 1056 + (i - 8) * P
                    pe.transpose(ps[:, i // 4, (i % 4) * P:(i % 4 + 1) * P], sc[:, c0:c0 + P], ident)
                pe.transpose(ps[0:32, 3, 0:P], sc[:, 1024:1056], ident)
                pe.transpose(ps[0:32, 3, P:2 * P], sc[:, 1568:1600], ident)
                pe.transpose(ps[0:63, 3, 2 * P:3 * P], sc[:, 1664:1727], ident).then_inc(S["sp_turned"], 1)

            def weigh_values(s, b4):
                if b4 == 0:
                    if s:
                        pe.wait_ge(S["so_copied"], s)
                    pe.wait_ge(S["spT_act"], s + 1)
                    pe.wait_ge(S["spT_dve"], s + 1)
                    pe.wait_ge(S[f"v_in{s}"], 16 * 9 * SETB)
                    o = ps[:, 7, 0:P]
                    pe.matmul(o, vnew[0:NS, 2, 0:P], pT[0:NS, 1536:1664], start=True, stop=False, skip_group_check=True)
                    pe.matmul(o, vnew[0:NS, 2, P:2 * P], pT[0:NS, 1664:1792], start=False, stop=False, skip_group_check=True)
                b = SETB * s + b4
                o = ps[:, 7, 32 * b4:32 * b4 + 32]
                pe.matmul(o, vc[0:63, b, :], pT[0:63, 1792 + 32 * b4:1824 + 32 * b4], start=False, stop=False, skip_group_check=True)
                for i in range(12):
                    v0 = (8 * b4 + i) * P if i < 8 else 4096 + (4 * b4 + i - 8) * P
                    last = pe.matmul(o, vset[s][:, v0:v0 + P], pT[:, i * P + 32 * b4:i * P + 32 * b4 + 32], start=False,
                                     stop=(b4 == 3 and i == 11), skip_group_check=True)
                if b4 == 3:
                    last.then_inc(S["so_mm"], 1)

            score(0)
            pe.wait_ge(S["rg_ready"], 2)
            conv_out((0, 1))
            turn_compressed(0)
            block_scores(0)
            conv_out((2, 3))
            turn_weights(0)
            score(1)
            weigh_values(0, 0)
            turn_compressed(1)
            weigh_values(0, 1)
            block_scores(1)
            weigh_values(0, 2)
            weigh_values(0, 3)
            conv_out((4, 5))
            turn_weights(1)
            conv_out((6, 7))
            for b4 in range(SETB):
                weigh_values(1, b4)

            pe.wait_ge(S["so_copied"], 2)
            pe.wait_ge(S["yc_used"], KC)
            for m in range(KC):
                if m >= 2:
                    pe.wait_ge(S["merged"], m - 1)
                last = project(W_YN + m // 2, 4 + m % 2, oT, 4, (m % 2) * 512)
                last.then_inc(S["slots_used" if m % 2 else "y_even"], 1)
            pe.wait_ge(S["merged"], KC)
            for m in range(KC):
                if m >= 2:
                    pe.wait_ge(S["x1_ready"], m - 1)
                project(W_O + m, 2 + m % 2, mg).then_inc(S["slots_used"], 1)
                if m >= 2:
                    pe.wait_ge(S["x_squared"], 4 + m - 1)
                    square_sum(xsq2, m - 2)
            for k in range(KC - 2, KC):
                pe.wait_ge(S["x_squared"], 4 + k + 1)
                last = square_sum(xsq2, k)
            last.then_inc(S["x_sumsq"], 1)

            def split_project(n, bank, it=None):
                at = lambda c: c if it is None else it * (2 * RING) + c
                for h in range(2):
                    pe.wait_ge(S["hi_ready"], at(n + h + 1))
                    for mov in (mov_hi, mov_lo):
                        for k in range(4):
                            last = pe.matmul(ps[:, bank, 0:NT], w_hi[:, h, k * P:(k + 1) * P], mov[:, 4 * h + k, :],
                                             start=(h == 0 and k == 0 and mov is mov_hi), stop=False, skip_group_check=True)
                    last.then_inc(S["hi_used"], 1)
                    pe.wait_ge(S["lo_ready"], at(2 + n + h + 1))
                    for k in range(4):
                        last = pe.matmul(ps[:, bank, 0:NT], w_lo[:, h, k * P:(k + 1) * P], mov_hi[:, 4 * h + k, :],
                                         start=False, stop=(h == 1 and k == 3), skip_group_check=True)
                    last.then_inc(S["lo_used"], 1)

            pe.wait_ge(S["h2_split"], 4)
            for i in range(16):
                if i >= 2:
                    pe.wait_ge(S["qq_copied"], i - 1)
                split_project(staged(W_Q + i), i % 2)
            pe.wait_ge(S["qq_copied"], 16)
            pe.wait_ge(S["sub_in"], 16)
            for t, (n0, n) in enumerate(TILES):
                if t == 2:
                    pe.wait_ge(S["pk_copied"], 1)
                for i in range(16):
                    last = pe.matmul(ps[0:n, 4 * ((t + 1) % 2) + i // 4, (i % 4) * P:(i % 4 + 1) * P], rt("qq")[:, i * NT + n0:i * NT + n0 + n],
                                     rt("sub")[:, i * P:(i + 1) * P], start=True, stop=True)
                last.then_inc(S["pk_mm"], 1)

            def expert_tile(it, j0, s):
                pe.wait_ge(S["u_free"], it * RING + (j0 + s + 1))
                split_project(staged(W_U + j0 + s), s % 2, it)

            def routing_split(it, g):
                pe.wait_ge(S["oh_ready"], it * 2 + (32 + g + 1))
                pe.wait_ge(S["w_free"], it * 2 + (32 + g + 1))
                for x in range(GT):
                    last = pe.matmul(ps[:, 1 + x // 4, x % 4 * P:(x % 4 + 1) * P], hot_first[:, x, :], hot_second[:, x, :], start=True, stop=True)
                last.then_inc(S["route_mm"], 1)

            def routing(it, g):
                pe.wait_ge(S["oh_ready"], it * 2 + (g + 1))
                pe.wait_ge(S["w_free"], it * 2 + (g + 1))
                for x in range(GT):
                    at = x * HALF
                    last = pe.matmul(ps[:, 2 + at // 512, at % 512:at % 512 + HALF], oh[:, x, 0:P], oh[:, x, P:P + HALF], start=True, stop=True)
                last.then_inc(S["route_mm"], 1)

            pe.wait_ge(S["pk_copied"], 2)
            pe.wait_ge(S["h2_split"], 8)
            with pe.Fori(0, HALF // RING) as it:
                for s in range(RING):
                    expert_tile(it, 0, s)
            pe.wait_ge(S["routed"], 3)
            for t, (n0, n) in enumerate(TILES):
                for i in range(3):
                    last = pe.transpose(ps[:, 5 + i, n0:n0 + n], rt("gi")[0:n, (3 * t + i) * P:(3 * t + i + 1) * P], ident[0:n, 0:n])
            last.then_inc(S["route_turned"], 1)
            with pe.Fori(0, HALF // RING) as it:
                for s in range(RING):
                    expert_tile(it, HALF, s)
                    if s % 2 == 0:
                        routing(it, s // 2)
            pe.wait_ge(S["u_free"], 2 + PK)
            for q in range(4):
                if q:
                    pe.wait_ge(S["y_ready"], q)
                for m in range(4):
                    pe.matmul(ps[:, VBANK[m], 0:NT], zero16[:, 0:P], zero16[:, :], start=True, stop=False, skip_group_check=True)
                with pe.Fori(0, 8) as it:
                    for s in range(RING):
                        n = staged(W_V + 32 * q + s)
                        pe.wait_ge(S["mov_ready"], it * RING + (32 * q + s + 1))
                        for h in range(2):
                            pe.wait_ge(S["hi_ready"], it * (2 * RING) + (n + h + 1))
                            for m in range(4):
                                for mov in (mov_hi, mov_lo):
                                    last = pe.matmul(ps[:, VBANK[m], 0:NT], w_hi[:, h, m * P:(m + 1) * P], mov[:, 2 * (s % 2) + h, :],
                                                     start=False, stop=False, skip_group_check=True)
                            last.then_inc(S["hi_used"], 1)
                            pe.wait_ge(S["lo_ready"], it * (2 * RING) + (2 + n + h + 1))
                            for m in range(4):
                                last = pe.matmul(ps[:, VBANK[m], 0:NT], w_lo[:, h, m * P:(m + 1) * P], mov_hi[:, 2 * (s % 2) + h, :],
                                                 start=False, stop=False, skip_group_check=True)
                            last.then_inc(S["lo_used"], 1)
                        if q < 2 and s % 2 == 0:
                            routing_split(it, 16 * q + s // 2)


def constants():
    f = np.float32
    c = np.zeros((P, NCONST), f)

    def put(name, x):
        a, b = CONST[name]
        c[:x.shape[0], a:b] = x

    pos = np.concatenate([np.arange(SEQ), np.tile(PAST + np.arange(NQ), NB)]).astype(f)
    inv = np.power(f(10000.0), -np.arange(HD // 2, dtype=f) * f(2.0) / f(HD)).astype(f)
    ang = (pos[:, None] * inv[None, :]).astype(f)
    cos, sin = np.cos(ang).astype(f), np.sin(ang).astype(f)
    cc, ss = np.zeros((P, 3 * HD), f), np.zeros((P, 3 * HD), f)
    for t, (n0, n) in enumerate(TILES):
        cc[:n, t * HD:(t + 1) * HD] = np.concatenate([cos[n0:n0 + n]] * 2, 1)
        ss[:n, t * HD:(t + 1) * HD] = np.concatenate([-sin[n0:n0 + n], sin[n0:n0 + n]], 1)
    put("ident", np.eye(P, dtype=f))
    put("iota", np.tile(np.arange(P, dtype=f), (P, 1)))
    put("ones", np.ones((P, P), f))
    put("cos", cc)
    put("sin", ss)
    row = np.arange(P)
    tri = np.where(row[None, :] <= row[:, None], 0, NEG).astype(f)
    put("causal", np.concatenate([np.zeros((P, P), f), tri], 1))
    end = np.arange(16) * STRIDE + 2 * STRIDE - 1
    ok = (end[None, None, :] <= (row[:, None] + P * np.arange(2)[None, :])[:, :, None]) & (np.arange(16) < 15)
    put("cmpmask", np.where(ok, 0, NEG).astype(f).reshape(P, 32))
    rb, rq = row // 32, row % 16 // R
    nm = np.full((P, 2, NB, NQ), NEG, f)
    for s in range(2):
        for p in range(P):
            nm[p, s, SETB * s + rb[p], :rq[p] + 1] = 0
    put("newmask", nm.reshape(P, 2 * NS))
    put("winmask", np.where(np.arange(NQ)[None, :] > rq[:, None], 0, NEG).astype(f))
    c0, s0 = np.arange(63)[:, None] * STRIDE, np.arange(NSEL)[None, :] * BLK
    put("ov", (np.clip(np.minimum(c0 + 2 * STRIDE, s0 + BLK) - np.maximum(c0, s0), 0, None) / STRIDE).astype(f))
    forced = np.zeros(NSEL, f)
    forced[[0, NSEL - 2, NSEL - 1]] = 1e4
    put("forced", np.tile(forced, (P, 1)))
    put("jp1", np.tile(np.arange(1, NSEL + 1, dtype=f), (P, 1)))
    rep = np.zeros((NS, 2, P), f)
    for s in range(2):
        rep[(SETB * s + rb) * NQ + rq, s, row] = 1
    put("rep", rep.reshape(NS, 2 * P))
    put("gsel", (np.arange(NH)[None, :] == (row % 32 // 16 * R + row % R)[:, None]).astype(f))
    put("iota16", np.tile(np.arange(PTOP, dtype=f), (P, 1)))
    return c


def kernel(x_prompt, x_sample, cache_cmp_k, cache_cmp_v, cache_slc_k, cache_slc_v, cache_win_k, cache_win_v, state_conv,
           page_table, norm_mix, w_in, conv_w, cmp_pos_k, cmp_w1_k, cmp_b1_k, cmp_w2_k, cmp_pos_v, cmp_w1_v, cmp_b1_v,
           cmp_w2_v, q_norm, k_norm_cmp, k_norm_slc, k_norm_win, w_out_conv, w_out_nsa, w_o, norm_ffn, peer_wq,
           peer_sub_keys, peer_u, peer_v):
    import concourse.bacc as _bacc
    from concourse.bass_utils import run_bass_kernel_spmd as _run

    a = np.asarray
    x = np.concatenate([a(x_prompt)[0], a(x_sample).reshape(NS, D)], 0)
    w = a(w_in)[0]
    cut = np.cumsum([0, 512, 512, 512, 512, P, P, P, P, P, P, 24, 2048])
    cb, cc, ch, q, kc, vc, ks, vs, kw, vw, ng, mg = (w[:, cut[i]:cut[i + 1]] for i in range(12))
    q = q.reshape(D, NG, R, HD).transpose(0, 2, 1, 3).reshape(D, 512)
    tok = np.concatenate([q, ks, kw, kc, vc, vs, vw, ng], 1)

    def chunks(m):
        k, n = m.shape
        return m.reshape(k // P, P, n // P, P).transpose(2, 1, 0, 3).reshape(n // P, P, k // P * P)

    feed = {"xT": x.T.reshape(KC, P, NT).transpose(1, 0, 2), "consts": constants()}
    for p, (c0, n) in enumerate(PIECES):
        feed[f"wtok{p}"] = tok[:, c0:c0 + n].reshape(4, 2, P, n).transpose(0, 2, 1, 3).reshape(4, P, 2 * n)
    conv = np.stack([cc.reshape(D, 4, P), ch.reshape(D, 4, P), cb.reshape(D, 4, P)], 2).reshape(D, 12 * P)
    feed["wT"] = np.concatenate([chunks(conv), chunks(mg)], 0)
    pair = lambda m: chunks(m).reshape(4, 2, P, 512).transpose(0, 2, 1, 3).reshape(4, P, 1024)
    nsa = a(w_out_nsa)[0].reshape(NG, R, HD, D).transpose(1, 0, 2, 3).reshape(512, D)
    feed["wout"] = np.concatenate([pair(a(w_out_conv)[0]), pair(nsa), chunks(a(w_o)[0]), chunks(a(peer_wq)[0])], 0)
    w1 = np.stack([a(cmp_w1_k)[0], a(cmp_w1_v)[0]])
    feed["w1"] = w1.reshape(2, 16, 2 * HD, P).transpose(2, 0, 1, 3).reshape(P, 4096)
    pos = np.stack([a(cmp_pos_k)[0], a(cmp_pos_v)[0]])
    state = a(state_conv)[0].reshape(NB, 2, 4, P).transpose(3, 2, 0, 1).reshape(P, 4 * NB * 2)
    gain = np.concatenate([np.tile(a(q_norm)[0], 8), np.tile(a(k_norm_slc)[0], 2), np.tile(a(k_norm_win)[0], 2)])
    feed["smalls"] = np.concatenate([
        a(norm_mix)[0].reshape(KC, P).T, a(norm_ffn)[0].reshape(KC, P).T,
        a(conv_w)[0].reshape(3, 4, P).transpose(2, 0, 1).reshape(P, 12), np.stack([a(cmp_b1_k)[0], a(cmp_b1_v)[0]], 1),
        pos.reshape(2, 16, 2 * HD).transpose(2, 0, 1).reshape(P, 32), state, np.tile(gain, (P, 1)),
        np.tile(a(k_norm_cmp)[0], (P, 1)), a(cmp_w2_k)[0], a(cmp_w2_v)[0]], 1)
    assert feed["smalls"].shape == (P, NSMALL)
    pt = a(page_table)
    feed["pages"] = pt.reshape(1, 64)
    for n, c in (("cmp_k", cache_cmp_k), ("cmp_v", cache_cmp_v)):
        feed["cache_" + n] = a(c).reshape(NPOOL, 8, 8, 2, NG, HD).transpose(0, 3, 5, 2, 4, 1).reshape(NPOOL, P, P)
    feed["cache_slc_k"] = a(cache_slc_k).reshape(NPOOL, PAGE, P).transpose(0, 2, 1)
    feed["cache_slc_v"] = a(cache_slc_v).reshape(NPOOL, PAGE, P)
    feed["cache_win_kT"] = a(cache_win_k).reshape(NB, WINDOW, P).transpose(0, 2, 1)
    for n, c in (("win_k", cache_win_k), ("win_v", cache_win_v)):
        feed["cache_" + n] = a(c).reshape(NB, WINDOW, P)
    feed["sub"] = a(peer_sub_keys)[0].reshape(16, P, P).transpose(2, 0, 1).reshape(P, 2048)
    feed["uT"] = a(peer_u)[0].reshape(PK, PK, KC, P).transpose(1, 3, 2, 0).reshape(PK, P, D)
    feed["v"] = a(peer_v)[0].reshape(PK, 2, 32, 2, 2, 512).transpose(1, 4, 2, 0, 3, 5).reshape(PK, P, 1024)

    nc = _bacc.Bacc("TRN2", target_bir_lowering=False, num_devices=1)
    arrays, A, O = {}, {}, {}
    for name, v in feed.items():
        v = np.ascontiguousarray(v)
        arrays["in_" + name] = v
        A[name] = nc.dram_tensor("in_" + name, v.shape, mybir.dt.from_np(v.dtype), kind="ExternalInput").ap()
    shapes = {"yT": (P, KC, NT), "kc": (NT, P), "vc": (NT, P), "ks": (NT, P), "vs": (NT, P), "kw": (SEQ, P), "vw": (SEQ, P),
              "wk": (NB, WINDOW, P), "wv": (NB, WINDOW, P), "cstate": (P, 4 * 18)}
    for name, shape in shapes.items():
        O[name] = nc.dram_tensor("out_" + name, shape, F32, kind="ExternalOutput").ap()
    program(nc, A, O)
    r = _run(nc, [arrays], core_ids=[0]).results[0]
    got = {name: a(r["out_" + name]) for name in shapes}
    y = got["yT"].transpose(1, 0, 2).reshape(D, NT).T
    cs = got["cstate"].reshape(P, 4, 18).transpose(2, 1, 0).reshape(18, 512)
    new = lambda n: got[n][SEQ:].reshape(1, NB, NQ, NG, HD)
    old = lambda n: got[n][:SEQ].reshape(1, 1, SEQ, NG, HD)
    win = lambda n: got[n].reshape(1, NB, WINDOW, NG, HD)
    return tuple(np.ascontiguousarray(v) for v in (
        y[:SEQ].reshape(1, SEQ, D), y[SEQ:].reshape(NB, NQ, D),
        old("kc"), old("vc"), old("ks"), old("vs"), old("kw"), old("vw"), cs[:2].reshape(1, 1, 2, 512),
        new("kc"), new("vc"), new("ks"), new("vs"), win("wk"), win("wv"), cs[2:].reshape(1, NB, 2, 512)))
```
